# Optimizing a Trainium2 kernel written in Bass

```python
import numpy as np
import jax
import jax.numpy as jnp
from jax import lax

D_MODEL = 1024
BATCH = 1
SEQ = 512
DEPTH = 4

CHUNK = 64
N_MIXERS = 3
N_A = (DEPTH + 2) // 3
N_B = (DEPTH + 1) // 3
N_C = DEPTH // 3
EPS = 1e-6
ROPE_THETA = 500000.0
GM_BLOCK = 128
GM_HID = 2 * D_MODEL
GM_GROUPS = 8
SSD_D_INNER = 2 * D_MODEL
SSD_HEAD_DIM = 64
SSD_HEADS = SSD_D_INNER // SSD_HEAD_DIM
SSD_GROUPS = 8
SSD_STATE = 128
SSD_CONV = 4
SSD_CHUNK = 128
SSD_CONV_CH = SSD_D_INNER + 2 * SSD_GROUPS * SSD_STATE
SSD_IN = SSD_D_INNER + SSD_CONV_CH + SSD_HEADS
DSA_HEADS = 16
DSA_KV_HEADS = 4
DSA_HEAD_DIM = 64
DSA_IDX_HEADS = 8
DSA_IDX_DIM = 64
DSA_TOPK_MAX = 256
DSA_QBLOCK = 128
DSA_Q_W = DSA_HEADS * DSA_HEAD_DIM
DSA_KV_W = DSA_KV_HEADS * DSA_HEAD_DIM
DSA_QI_W = DSA_IDX_HEADS * DSA_IDX_DIM
DSA_IN = DSA_Q_W + 2 * DSA_KV_W + DSA_QI_W + DSA_IDX_DIM + DSA_IDX_HEADS
MEM_LEN = 256
XA_HEADS = 4
XA_HEAD_DIM = 128
XA_W = XA_HEADS * XA_HEAD_DIM
FFN_HID = 4 * D_MODEL

kernel_name = 'hybrid_chunk_causal_encoder'

def rms_norm(x, gain):
    x32 = x.astype(jnp.float32)
    y = x32 * lax.rsqrt(jnp.mean(x32 * x32, axis=-1, keepdims=True) + EPS)
    return y.astype(x.dtype) * gain

def rope_partial(x, positions):
    rot = x.shape[-1] // 4
    half = rot // 2
    inv_freq = ROPE_THETA ** (-jnp.arange(half, dtype=jnp.float32) / half)
    ang = positions.astype(jnp.float32)[..., None] * inv_freq
    cos = jnp.cos(ang)[:, :, None, :]
    sin = jnp.sin(ang)[:, :, None, :]
    xr = x[..., :rot].astype(jnp.float32)
    x1, x2 = xr[..., :half], xr[..., half:]
    r = jnp.concatenate([x1 * cos - x2 * sin, x2 * cos + x1 * sin], axis=-1).astype(x.dtype)
    return jnp.concatenate([r, x[..., rot:]], axis=-1)

def gmlp_mixer(h, w_in, v_norm, w_s, b_s, w_out):
    B_, S_, _ = h.shape
    uv = jax.nn.gelu(h @ w_in)
    u, v = uv[..., :GM_HID], uv[..., GM_HID:]
    v = rms_norm(v, v_norm)
    nb = S_ // GM_BLOCK
    v = v.reshape(B_, nb, GM_BLOCK, GM_GROUPS, GM_HID // GM_GROUPS)
    t = jnp.arange(GM_BLOCK)
    mask = (t[None, :] // CHUNK) <= (t[:, None] // CHUNK)
    ws = jnp.where(mask[None], w_s, 0)
    v = jnp.einsum('gts,bnsgc->bntgc', ws, v) + jnp.transpose(b_s)[None, None, :, :, None]
    v = v.reshape(B_, S_, GM_HID)
    return (u * v) @ w_out

def causal_dwconv(x, w, b):
    K = w.shape[0]
    y = lax.conv_general_dilated(x, w[:, None, :], window_strides=(1,), padding=[(K - 1, 0)],
                                 dimension_numbers=('NWC', 'WIO', 'NWC'),
                                 feature_group_count=x.shape[-1])
    return y + b

def ssd_mixer(h, w_in, conv_w, conv_b, dt_bias, a_log, d_skip, out_norm, w_out):
    B_, S_, _ = h.shape
    G, N, H, P, Q = SSD_GROUPS, SSD_STATE, SSD_HEADS, SSD_HEAD_DIM, SSD_CHUNK
    R = H // G
    nc = S_ // Q
    f32 = jnp.float32
    zxbcdt = h @ w_in
    z = zxbcdt[..., :SSD_D_INNER]
    xbc = zxbcdt[..., SSD_D_INNER:SSD_D_INNER + SSD_CONV_CH]
    dt = zxbcdt[..., SSD_D_INNER + SSD_CONV_CH:]
    xbc = jax.nn.silu(causal_dwconv(xbc, conv_w, conv_b))
    xs = xbc[..., :SSD_D_INNER]
    Bm = xbc[..., SSD_D_INNER:SSD_D_INNER + G * N]
    Cm = xbc[..., SSD_D_INNER + G * N:]
    dt = jax.nn.softplus((dt + dt_bias).astype(f32))
    A = -jnp.exp(a_log.astype(f32))
    xc = xs.reshape(B_, nc, Q, G, R, P).astype(f32)
    Bc = Bm.reshape(B_, nc, Q, G, N).astype(f32)
    Cc = Cm.reshape(B_, nc, Q, G, N).astype(f32)
    dtc = dt.reshape(B_, nc, Q, G, R)
    a_cum = jnp.cumsum(dtc * A.reshape(G, R), axis=2)
    xdt = xc * dtc[..., None]
    a_t = jnp.moveaxis(a_cum, 2, -1)
    tq = jnp.arange(Q)
    causal = tq[:, None] >= tq[None, :]
    seg = a_t[..., :, None] - a_t[..., None, :]
    L = jnp.exp(jnp.where(causal, seg, -jnp.inf))
    cb = jnp.einsum('bclgn,bcsgn->bcgls', Cc, Bc)
    y_diag = jnp.einsum('bcgrls,bcsgrp->bclgrp', L * cb[:, :, :, None], xdt)
    decay_states = jnp.exp(a_cum[:, :, -1:] - a_cum)
    states = jnp.einsum('bclgn,bclgrp->bcgrpn', Bc, xdt * decay_states[..., None])
    chunk_decay = jnp.exp(a_cum[:, :, -1])

    def step(carry, inp):
        st, dec = inp
        return carry * dec[..., None, None] + st, carry

    init = jnp.zeros((B_, G, R, P, N), f32)
    _, prev = lax.scan(step, init, (jnp.moveaxis(states, 1, 0), jnp.moveaxis(chunk_decay, 1, 0)))
    prev = jnp.moveaxis(prev, 0, 1)
    y_off = jnp.einsum('bclgn,bcgrpn->bclgrp', Cc, prev) * jnp.exp(a_cum)[..., None]
    y = y_diag + y_off + xc * d_skip.astype(f32).reshape(G, R)[..., None]
    y = y.reshape(B_, S_, SSD_D_INNER)
    g = (y * jax.nn.silu(z.astype(f32))).reshape(B_, S_, G, SSD_D_INNER // G)
    g = g * lax.rsqrt(jnp.mean(g * g, axis=-1, keepdims=True) + EPS)
    y = g.reshape(B_, S_, SSD_D_INNER).astype(h.dtype) * out_norm
    return y @ w_out

def dsa_mixer(h, positions, w_in, q_norm, k_norm, kidx_norm, w_out):
    B_, S_, _ = h.shape
    H, KVH, Dh, HI, DI = DSA_HEADS, DSA_KV_HEADS, DSA_HEAD_DIM, DSA_IDX_HEADS, DSA_IDX_DIM
    R = H // KVH
    f32 = jnp.float32
    o1 = DSA_Q_W
    o2 = o1 + DSA_KV_W
    o3 = o2 + DSA_KV_W
    o4 = o3 + DSA_QI_W
    o5 = o4 + DI
    proj = h @ w_in
    q = rope_partial(rms_norm(proj[..., :o1].reshape(B_, S_, H, Dh), q_norm), positions)
    k = rope_partial(rms_norm(proj[..., o1:o2].reshape(B_, S_, KVH, Dh), k_norm), positions)
    v = proj[..., o2:o3].reshape(B_, S_, KVH, Dh)
    qi = rope_partial(proj[..., o3:o4].reshape(B_, S_, HI, DI), positions)
    ki = rope_partial(rms_norm(proj[..., o4:o5], kidx_norm)[:, :, None, :], positions)[:, :, 0, :]
    wi = proj[..., o5:].astype(f32) * (HI ** -0.5 * DI ** -0.5)
    kv = jnp.concatenate([k, v], axis=-1)
    topk = min(DSA_TOPK_MAX, S_ // 4)
    nb = S_ // DSA_QBLOCK
    key_chunk = jnp.arange(S_) // CHUNK

    def to_blocks(a):
        return jnp.moveaxis(a.reshape(B_, nb, DSA_QBLOCK, *a.shape[2:]), 1, 0)

    def block_fn(args):
        qb, qib, wib, start = args
        q_chunk = (start + jnp.arange(DSA_QBLOCK)) // CHUNK
        admissible = key_chunk[None, :] <= q_chunk[:, None]
        logits = jnp.einsum('bqhd,bsd->bqhs', qib, ki)
        score = jnp.einsum('bqh,bqhs->bqs', wib, jax.nn.relu(logits).astype(f32))
        score = jnp.where(admissible[None], score, -jnp.inf)
        top_score, idx = lax.top_k(score, topk)
        valid = jnp.isfinite(top_score)
        kv_sel = jax.vmap(lambda kv_b, i_b: kv_b[i_b])(kv, idx)
        k_sel, v_sel = kv_sel[..., :Dh], kv_sel[..., Dh:]
        qg = qb.reshape(B_, DSA_QBLOCK, KVH, R, Dh)
        s = jnp.einsum('bqgrd,bqkgd->bqgrk', qg, k_sel).astype(f32) * (Dh ** -0.5)
        s = jnp.where(valid[:, :, None, None, :], s, -jnp.inf)
        p = jax.nn.softmax(s, axis=-1).astype(v_sel.dtype)
        o = jnp.einsum('bqgrk,bqkgd->bqgrd', p, v_sel)
        return o.reshape(B_, DSA_QBLOCK, H * Dh)

    starts = jnp.arange(nb, dtype=jnp.int32) * DSA_QBLOCK
    out = lax.map(block_fn, (to_blocks(q), to_blocks(qi), to_blocks(wi), starts))
    out = jnp.moveaxis(out, 0, 1).reshape(B_, S_, H * Dh)
    return out @ w_out

def memory_xattn(h, mem_n, w_q, w_kv, q_norm, k_norm, w_out):
    B_, S_, _ = h.shape
    M = mem_n.shape[1]
    q = rms_norm((h @ w_q).reshape(B_, S_, XA_HEADS, XA_HEAD_DIM), q_norm)
    kvm = mem_n @ w_kv
    k = rms_norm(kvm[..., :XA_W].reshape(B_, M, XA_HEADS, XA_HEAD_DIM), k_norm)
    v = kvm[..., XA_W:].reshape(B_, M, XA_HEADS, XA_HEAD_DIM)
    s = jnp.einsum('bshd,bmhd->bhsm', q, k).astype(jnp.float32) * (XA_HEAD_DIM ** -0.5)
    p = jax.nn.softmax(s, axis=-1).astype(v.dtype)
    o = jnp.einsum('bhsm,bmhd->bshd', p, v).reshape(B_, S_, XA_W)
    return o @ w_out

def sqrelu_ffn(h, w_up, w_down):
    return jnp.square(jax.nn.relu(h @ w_up)) @ w_down

def setup_inputs(seed: int = 0) -> dict:
    key = jax.random.key(seed)
    ks = jax.random.split(key, 32)
    f32 = jnp.float32

    def nrm(k, shape, scale):
        return jax.random.normal(k, shape, f32) * scale

    def gain(k, shape):
        return 1.0 + 0.02 * jax.random.normal(k, shape, f32)

    x = nrm(ks[0], (BATCH, SEQ, D_MODEL), 1.0)
    mem = nrm(ks[1], (BATCH, MEM_LEN, D_MODEL), 1.0)
    start = jax.random.randint(ks[2], (BATCH,), 0, 512, dtype=jnp.int32) * CHUNK
    positions = start[:, None] + jnp.arange(SEQ, dtype=jnp.int32)[None, :]
    dt0 = jnp.exp(jax.random.uniform(ks[12], (N_B, SSD_HEADS), f32, float(np.log(1e-3)), float(np.log(1e-1))))
    dt_bias = dt0 + jnp.log(-jnp.expm1(-dt0))
    a_log = jnp.log(jax.random.uniform(ks[13], (N_B, SSD_HEADS), f32, 1.0, 16.0))
    return {
        'x': x,
        'mem': mem,
        'positions': positions,
        'norm_mix': gain(ks[3], (DEPTH, D_MODEL)),
        'gm_w_in': nrm(ks[4], (N_A, D_MODEL, 2 * GM_HID), D_MODEL ** -0.5),
        'gm_v_norm': gain(ks[5], (N_A, GM_HID)),
        'gm_w_s': nrm(ks[6], (N_A, GM_GROUPS, GM_BLOCK, GM_BLOCK), GM_BLOCK ** -0.5),
        'gm_b_s': gain(ks[7], (N_A, GM_GROUPS, GM_BLOCK)),
        'gm_w_out': nrm(ks[8], (N_A, GM_HID, D_MODEL), GM_HID ** -0.5),
        'ssd_w_in': nrm(ks[9], (N_B, D_MODEL, SSD_IN), D_MODEL ** -0.5),
        'ssd_conv_w': nrm(ks[10], (N_B, SSD_CONV, SSD_CONV_CH), SSD_CONV ** -0.5),
        'ssd_conv_b': nrm(ks[11], (N_B, SSD_CONV_CH), 0.02),
        'ssd_dt_bias': dt_bias,
        'ssd_a_log': a_log,
        'ssd_d': gain(ks[14], (N_B, SSD_HEADS)),
        'ssd_out_norm': gain(ks[15], (N_B, SSD_D_INNER)),
        'ssd_w_out': nrm(ks[16], (N_B, SSD_D_INNER, D_MODEL), SSD_D_INNER ** -0.5),
        'dsa_w_in': nrm(ks[17], (N_C, D_MODEL, DSA_IN), D_MODEL ** -0.5),
        'dsa_q_norm': gain(ks[18], (N_C, DSA_HEAD_DIM)),
        'dsa_k_norm': gain(ks[19], (N_C, DSA_HEAD_DIM)),
        'dsa_kidx_norm': gain(ks[20], (N_C, DSA_IDX_DIM)),
        'dsa_w_out': nrm(ks[21], (N_C, DSA_Q_W, D_MODEL), DSA_Q_W ** -0.5),
        'norm_xa': gain(ks[22], (DEPTH, D_MODEL)),
        'norm_mem': gain(ks[23], (DEPTH, D_MODEL)),
        'xa_w_q': nrm(ks[24], (DEPTH, D_MODEL, XA_W), D_MODEL ** -0.5),
        'xa_w_kv': nrm(ks[25], (DEPTH, D_MODEL, 2 * XA_W), D_MODEL ** -0.5),
        'xa_q_norm': gain(ks[26], (DEPTH, XA_HEAD_DIM)),
        'xa_k_norm': gain(ks[27], (DEPTH, XA_HEAD_DIM)),
        'xa_w_out': nrm(ks[28], (DEPTH, XA_W, D_MODEL), XA_W ** -0.5),
        'norm_ffn': gain(ks[29], (DEPTH, D_MODEL)),
        'ffn_w_up': nrm(ks[30], (DEPTH, D_MODEL, FFN_HID), D_MODEL ** -0.5),
        'ffn_w_down': nrm(ks[31], (DEPTH, FFN_HID, D_MODEL), FFN_HID ** -0.5),
    }

def reference(x, mem, positions, norm_mix, gm_w_in, gm_v_norm, gm_w_s, gm_b_s, gm_w_out,
              ssd_w_in, ssd_conv_w, ssd_conv_b, ssd_dt_bias, ssd_a_log, ssd_d, ssd_out_norm, ssd_w_out,
              dsa_w_in, dsa_q_norm, dsa_k_norm, dsa_kidx_norm, dsa_w_out,
              norm_xa, norm_mem, xa_w_q, xa_w_kv, xa_q_norm, xa_k_norm, xa_w_out,
              norm_ffn, ffn_w_up, ffn_w_down):
    for i in range(DEPTH):
        kind = i % N_MIXERS
        j = i // N_MIXERS
        hn = rms_norm(x, norm_mix[i])
        if kind == 0:
            x = x + gmlp_mixer(hn, gm_w_in[j], gm_v_norm[j], gm_w_s[j], gm_b_s[j], gm_w_out[j])
        elif kind == 1:
            x = x + ssd_mixer(hn, ssd_w_in[j], ssd_conv_w[j], ssd_conv_b[j], ssd_dt_bias[j],
                              ssd_a_log[j], ssd_d[j], ssd_out_norm[j], ssd_w_out[j])
        else:
            x = x + dsa_mixer(hn, positions, dsa_w_in[j], dsa_q_norm[j], dsa_k_norm[j],
                              dsa_kidx_norm[j], dsa_w_out[j])
        x = x + memory_xattn(rms_norm(x, norm_xa[i]), rms_norm(mem, norm_mem[i]), xa_w_q[i],
                             xa_w_kv[i], xa_q_norm[i], xa_k_norm[i], xa_w_out[i])
        x = x + sqrelu_ffn(rms_norm(x, norm_ffn[i]), ffn_w_up[i], ffn_w_down[i])
    return x


_drawn_inputs = setup_inputs


def setup_inputs(seed=0):
    import zlib

    import numpy as np

    out = dict(_drawn_inputs(seed))
    spreads = {}
    factors = {'gm_v_norm': 4.073,
     'gm_b_s': 3.662,
     'ssd_conv_b': 3.529,
     'ssd_d': 7.764,
     'ssd_out_norm': 4.424,
     'dsa_q_norm': 8.0,
     'dsa_k_norm': 8.0,
     'dsa_kidx_norm': 8.0,
     'norm_xa': 8.0,
     'norm_mem': 8.0,
     'xa_q_norm': 8.0,
     'xa_k_norm': 8.0}
    for name, (base, spread) in spreads.items():
        noise = np.random.default_rng([zlib.crc32(name.encode()), seed]).standard_normal(out[name].shape)
        drawn = base * np.exp(spread * noise) if base else spread * noise
        out[name] = jnp.asarray(drawn.astype(out[name].dtype))
    for name, factor in factors.items():
        out[name] = (out[name] * factor).astype(out[name].dtype)
    return out
```

```python
from contextlib import ExitStack

import concourse.bass as bass
import numpy as np
from concourse import mybir

F32 = mybir.dt.float32
F32R = mybir.dt.float32r
I32 = mybir.dt.int32
ALU = mybir.AluOpType
ACT = mybir.ActivationFunctionType
AX = mybir.AxisListType.X
ds = bass.ds

P = 128
D = 1024
KT = D // P
S = 512
TT = S // P
MEM = 256
MT = MEM // P
EPS = 1e-6
DEPTH = 4
GM_HID = 2048
GM_G = 8
XH = 4
XSCALE = 128 ** -0.5
FFN = 4096
HALF = FFN // 2
HT = HALF // P
SSD_IN = 6176
SSD_XBC = 2048
SSD_DT = 6144
NHEAD = 32
UNIT = 2048
CW = 256

TAB_MIX, TAB_XA, TAB_MEM, TAB_FFN = 0, 32, 64, 96
TAB_VN, TAB_ON, TAB_CB, TAB_XQ, TAB_XK = 0, 32, 48, 80, 84
TAB_DQ, TAB_DK, TAB_DI = 88, 89, 90
TAB1_ROWS = 91

LAYERS = ("gmlp", "ssd", "dsa", "gmlp")

UNITS = {"load": 0, "gmlp": 24, "ssd": 33, "dsa": 14, "xattn": 8, "ffn": 32, "store": 0}
GROUPS = {"load": 8, "gmlp": 29, "ssd": 45, "dsa": 79, "xattn": 18, "ffn": 24, "store": 4}
OWN = {"load": 8, "gmlp": 9, "ssd": 16, "dsa": 65, "xattn": 8, "ffn": 0, "store": 4}
DH = 16
DI_H = 8
DSCALE = 64 ** -0.5
DSA_IN = 2120
DSA_K, DSA_V, DSA_QI, DSA_KI = 1024, 1280, 1536, 2048
HIDE = 1e30
OUT_OF_REACH = 3.3e38
TAKEN = 3.4e38
PI = 3.1415925
ROUND = 12582912.0
TURN1 = 6.28125
TURN2 = 0.0019350051879882812
TURN3 = 2 * np.pi - TURN1 - TURN2
SSD_G = 8
SSD_ACT = 17
SSD_DVE = 22
SSD_AUX = 8
SSD_AUX0 = 3
PAR_CW, PAR_CB, PAR_A, PAR_D, PAR_G = 0, 16, 20, 36, 38
OUT_GROUPS = 4


def constants():
    c = np.zeros((P, 5 * P + 8), np.float32)
    c[:, 0:P] = np.eye(P)
    c[P - 1, P:2 * P] = 1.0
    t = np.arange(P)
    c[:, 2 * P:3 * P] = t[None, :] >= t[:, None]
    rot = np.zeros((P, P), np.float32)
    for h in (0, 64):
        for i in range(8):
            rot[h + 8 + i, h + i] = -1.0
            rot[h + i, h + 8 + i] = 1.0
    c[:, 3 * P:4 * P] = rot
    c[0, 4 * P:4 * P + 64] = 1.0
    c[1, 4 * P + 64:5 * P] = 1.0
    inv = (np.float32(500000.0) ** (-np.arange(8, dtype=np.float32) / np.float32(8))).astype(np.float32)
    for h in (0, 64):
        c[h:h + 8, 5 * P] = inv
        c[h + 8:h + 16, 5 * P] = inv
    c[0:64, 5 * P + 1] = 1.0
    c[64:128, 5 * P + 2] = 1.0
    c[:, 5 * P + 3] = 1.0
    c[:, 5 * P + 4:5 * P + 8] = -0.5
    return c


def build(nc, t, out, phases):
    unit0, group0, own0 = [], [], []
    u = g = o = 0
    for kind, _ in phases:
        unit0.append(u), group0.append(g), own0.append(o)
        u, g, o = u + UNITS[kind], g + GROUPS[kind], o + OWN[kind]
    n_units = u
    dma_count = [1] * (n_units + 2)
    for ph, (kind, _) in enumerate(phases):
        if kind == "ssd":
            for j in range(SSD_G):
                dma_count[unit0[ph] + 2 + 3 * j] = 2
        if kind == "dsa":
            for j, n in DSA_DMAS.items():
                dma_count[unit0[ph] + j] = n
    landed = []
    for n, c in enumerate(dma_count):
        landed.append(16 * c + (landed[n - 2] if n >= 2 else 0))

    with ExitStack() as ctx:
        top = [16512]

        def sb(name, shape, dt=F32, at=None):
            size = 4 * int(np.prod(shape[1:]))
            offset = top[0] if at is None else at
            if at is None:
                top[0] += (size + 31) // 32 * 32
            h = nc.alloc_sbuf_tensor_at(name, shape, dt, offset=offset)
            where[name] = offset
            return h

        where = {}

        def sem(name):
            return ctx.enter_context(nc.semaphore(name))

        x = sb("x_res", [P, KT, S])
        hn_hi = sb("hn_hi", [P, KT, S], F32R)
        hn_lo = sb("hn_lo", [P, KT, S], F32R)
        stage = [sb(f"stage{i}", [P, UNIT]) for i in range(2)]
        w_hi = [sb(f"w_hi{i}", [P, UNIT], F32R) for i in range(2)]
        w_lo = [sb(f"w_lo{i}", [P, UNIT], F32R) for i in range(2)]
        mem_hi = sb("mem_hi", [P, KT, MEM], F32R)
        mem_lo = sb("mem_lo", [P, KT, MEM], F32R)
        mem_raw = sb("mem_raw", [P, KT, MEM], at=where["mem_lo"])
        kv_at = top[0]
        k_t = sb("k_t", [P, XH, MEM])
        v_m = sb("v_m", [P, MT, 512])
        ws_t = sb("ws_t", [P, GM_G, P], at=where["k_t"])
        bs_b = sb("bs_b", [P, GM_G, P], at=where["v_m"])
        tmp = sb("tmp", [P, 2, S])
        sq = [sb(f"sq{i}", [P, 2, S]) for i in range(2)]
        cst = sb("cst", [P, 5 * P + 8])
        tab = [sb("tab0", [P, P]), sb("tab1", [P, TAB1_ROWS]), sb("tab2", [P, P])]
        var = sb("var", [P, 16])
        rs = sb("rs", [P, 16])
        soft = sb("soft", [P, 2, 3, 4])
        rinv = sb("rinv", [P, 2, 4])
        nh16 = sb("nh16", [P, 16])
        big = top[0]
        top[0] += 65536
        a_log = sb("a_log", [P, 1])
        dt_bias = sb("dt_bias", [P, 1])
        neg_a = sb("neg_a", [P, 1])
        d_pair = sb("d_pair", [2, 16])
        d_col = sb("d_col", [P, 16])
        dta_tok = sb("dta_tok", [P, 2, TT, NHEAD])
        dec_tok = sb("dec_tok", [P, TT, NHEAD])
        cd_b = sb("cd_b", [P, TT, NHEAD])
        par = [sb(f"par{i}", [P, 40]) for i in range(2)]
        wi_tok = sb("wi_tok", [P, TT, DI_H])
        top8 = sb("top8", [P, 8])
        soft_d = sb("soft_d", [P, 2, 4])
        scrap, scrap_d = sb("scrap", [P, 1]), sb("scrap_d", [P, 1])
        ident = cst[:, 0:P]
        ones = cst[:, 5 * P + 3:5 * P + 4]

        hid_hi = sb("hid_hi", [P, HT, S], F32R, at=big)
        hid_lo = sb("hid_lo", [P, HT, S], F32R, at=big + 32768)
        v_tok = sb("v_tok", [P, TT, GM_HID], at=big)
        uv_hi = sb("uv_hi", [P, TT, GM_HID], F32R, at=big)
        u_t = sb("u_t", [P, 16, S], at=big + 32768)
        uv_lo = sb("uv_lo", [P, 16, S], F32R, at=big + 32768)
        ws_raw = sb("ws_raw", [P, GM_G, P], at=big + 32768)
        square_a = sb("square_a", [P, GM_HID], at=big + 32768 + 8192)
        square_d = sb("square_d", [P, GM_HID], at=big + 32768 + 16384)
        q_raw = sb("q_raw", [P, XH, S], at=big)
        k_raw = sb("k_raw", [P, XH, MEM], at=big + 8192)
        prob = [sb(f"prob{i}", [P, TT, MEM], at=big + 12288 + 4096 * i) for i in range(2)]
        prob_t = [sb(f"prob_t{i}", [P, MT, S], at=big + 20480 + 4096 * i) for i in range(2)]
        o_hi = sb("o_hi", [P, XH, S], F32R, at=big + 28672)
        o_lo = sb("o_lo", [P, XH, S], F32R, at=big + 36864)
        y_f = sb("y_f", [P, 16, S], at=big)
        y_lo = sb("y_lo", [P, 16, S], F32R, at=big)
        y_hi = sb("y_hi", [P, 16, S], F32R, at=big + 32768)
        work = big + 32768
        xg = sb("xg", [P, 2, S], at=work)
        bc = sb("bc", [P, 2, S], at=work + 4096)
        zg = sb("zg", [P, 2, S], at=work + 8192)
        xdt = sb("xdt", [P, TT, CW], at=work + 12288)
        xdd = sb("xdd", [P, TT, CW], at=work + 16384)
        cs = sb("cs", [P, 4, S], at=work + 20480)
        dtw = sb("dtw", [P, 4, S], at=work)
        dta = sb("dta", [P, 2, S], at=work + 8192)
        b_tok = sb("b_tok", [P, S], at=kv_at)
        cbm = sb("cbm", [P, S], at=kv_at + 2048)
        state = sb("state", [P, 3, CW], at=kv_at + 4096)
        q_d = sb("q_d", [P, 8, S], at=big)
        k_d = sb("k_d", [P, 4, S], at=big + 16384)
        v_d = sb("v_d", [P, TT, CW], at=big + 24576)
        qi = sb("qi", [P, 4, S], at=big + 28672)
        ki_w = sb("ki_w", [P, 2, S], at=big + 36864)
        msk = sb("msk", [P, TT, S], at=big + 40960)
        pr_d = [sb(f"pr_d{i}", [P, S], at=big + 49152 + 2048 * i) for i in range(2)]
        pt_d = [sb(f"pt_d{i}", [P, S], at=big + 53248 + 2048 * i) for i in range(2)]
        ang = sb("ang", [P, 2, S], at=big + 57344)
        pos_i = sb("pos_i", [P, S], I32, at=big + 61440)
        cos_t = sb("cos_t", [P, S], at=kv_at)
        sin_t = sb("sin_t", [P, S], at=kv_at + 2048)
        x_tok = sb("x_tok", [P, TT, D], at=big)
        mem_tok = sb("mem_tok", [P, MT, D], at=big + 16384)
        tab_raw = [sb(f"tab_raw{i}", [P, P], at=big + 24576 + 512 * i) for i in range(3)]
        mem_row = sb("mem_row", [P, KT, MEM], at=big + 28672)

        pair = [ctx.enter_context(nc.psum_tensor(f"pair{i}", [P, 2, S], F32)) for i in range(2)]
        aux = ctx.enter_context(nc.psum_tensor("aux", [P, 4, S], F32))

        mem_scratch = nc.dram_tensor("mem_scratch", [P, KT * MEM], F32, kind="Internal").ap()

        w_landed = [sem("w_landed0"), sem("w_landed1")]
        w_high = sem("w_high")
        w_low = sem("w_low")
        w_used = sem("w_used")
        own_done = sem("own_done")
        evac = [sem("evac0"), sem("evac1")]
        loaded = sem("loaded")
        stored = sem("stored")
        sq_done = sem("sq_done")
        sq_used = sem("sq_used")
        var_done = sem("var_done")
        rs_done = sem("rs_done")
        rb_done = sem("rb_done")
        hn_t = sem("hn_t")
        hn_high = sem("hn_high")
        hn_low = sem("hn_low")
        mn_t, mn_high, mn_low = sem("mn_t"), sem("mn_high"), sem("mn_low")
        mem_in = sem("mem_in")
        mem_made = sem("mem_made")
        mem_kept = sem("mem_kept")
        a_sq = sem("a_sq")
        a_high = sem("a_high")
        a_low = sem("a_low")
        dve = sem("dve_chain")
        kn_done = sem("kn_done")
        qn_done = sem("qn_done")
        score_done = sem("score_done")
        nb_done = sem("nb_done")
        exp_done = sem("exp_done")
        prob_done = sem("prob_done")
        o_high, o_low = sem("o_high"), sem("o_low")
        half_out = sem("half_out")
        ws_in = sem("ws_in")
        ws_ready = sem("ws_ready")
        vss_a, vss_d = sem("vss_a"), sem("vss_d")
        consts_set = sem("consts_set")
        ssd_aux = sem("ssd_aux")
        ssd_d, ssd_dt, ssd_e = sem("ssd_d"), sem("ssd_dt"), sem("ssd_e")
        ssd_scan, ssd_tok, ssd_dec = sem("ssd_scan"), sem("ssd_tok"), sem("ssd_dec")
        s_par = sem("s_par")
        s_act = sem("s_act")
        s_xdd, s_cb, s_seg, s_m, s_c = sem("s_xdd"), sem("s_cb"), sem("s_seg"), sem("s_m"), sem("s_c")
        s_state, s_yz, ssd_y = sem("s_state"), sem("s_yz"), sem("ssd_y")
        s_yhigh, s_ylow = sem("s_yhigh"), sem("s_ylow")

        pos_in = sem("pos_in")
        (d_sq, d_sum, d_norm,
         d_rot, d_cos, d_rope,
         d_ang, d_sin,
         d_logit, d_relu, d_acc,
         d_score, d_nb, d_exp, d_inv, d_prob,
         d_out, d_ohigh, d_olow) = [sem(x_) for x_ in (
             "d_sq", "d_sum", "d_norm", "d_rot", "d_cos", "d_rope", "d_ang", "d_sin", "d_logit", "d_relu", "d_acc",
             "d_score", "d_nb", "d_exp", "d_inv", "d_prob", "d_out", "d_ohigh", "d_olow")]

        def over_tiles(a, m):
            return a[:].rearrange("p (o s) -> p o s", o=1).broadcast_to((P, m, S))

        def seg(r):
            return sq[r // 2][:, r % 2, :]

        def spread64(a):
            shape = tuple(a.shape)
            names = " ".join("abcd"[:len(shape) - 1])
            return a.rearrange(f"{names} (e o) -> {names} e o", o=1).broadcast_to(shape + (64,))

        CH = {k: [] for k in ("sq", "var", "dvec")}

        def repeat(eng, count, body, peel=False):
            if peel:
                body(0)
            with eng.Fori(1 if peel else 0, count) as i:
                body(i)

        def split_high(act, n, adv=0, dmas=None):
            act.wait_ge(w_landed[n % 2], landed[n] + (8 * adv if dmas is None else dmas))
            if n >= 2 or not isinstance(adv, int):
                act.wait_ge(w_used, n - 1 + adv)
            nc.scalar.copy(w_hi[n % 2][:], stage[n % 2][:]).then_inc(w_high, 1)

        def split_low(vec, n, adv=0):
            vec.wait_ge(w_high, n + 1 + adv)
            nc.vector.tensor_tensor(w_lo[n % 2][:], stage[n % 2][:], w_hi[n % 2][:].bitcast(F32),
                                    ALU.subtract).then_inc(w_low, 1)

        def load_unit(sp, n, dst_src, adv=0):
            if n >= 2 or not isinstance(adv, int):
                sp.wait_ge(w_low, n - 1 + adv)
            for dst, src in dst_src:
                sp.dma_start(dst, src).then_inc(w_landed[n % 2], 16)

        def cols(w, c0, width=CW, k0=0, kt=KT):
            return w[k0:k0 + kt * P, :].rearrange("(k p) m -> p k m", p=P)[:, :, ds(c0, width)]

        def slot(n, kt=KT, width=CW):
            return stage[n % 2][:, 0:kt * width].rearrange("p (k m) -> p k m", k=kt)

        def free_pair(pe, g, adv=0):
            if g >= 2:
                pe.wait_ge(evac[g % 2], g // 2 + adv)

        def read_out(eng, g, adv=0):
            eng.wait_ge(evac[g % 2], g // 2 + 1 + adv)

        def three(psum, hi_w, lo_w, hi_x, lo_x, first, last):
            nc.tensor.matmul(psum, hi_w, hi_x, start=first, stop=False, skip_group_check=True)
            nc.tensor.matmul(psum, hi_w, lo_x, start=False, stop=False, skip_group_check=True)
            return nc.tensor.matmul(psum, lo_w, hi_x, start=False, stop=last, skip_group_check=True)

        def unit_w(n, kt=KT, width=CW):
            f = "p (k m) -> p k m"
            return (w_hi[n % 2][:, 0:kt * width].rearrange(f, k=kt),
                    w_lo[n % 2][:, 0:kt * width].rearrange(f, k=kt))

        def product(pe, n, g, rhs_hi, rhs_lo, adv=0, first=True, last=True, ready=None, width=CW,
                    tokens=S, done=True):
            pe.wait_ge(w_low, n + 1 + adv)
            hi, lo = unit_w(n)
            for kt in range(KT):
                if ready:
                    ready(kt)
                for m in range(width // P):
                    c = slice(m * P, (m + 1) * P)
                    mm = three(pair[g % 2][:, m, 0:tokens], hi[:, kt, c], lo[:, kt, c], rhs_hi(kt), rhs_lo(kt),
                               first and kt == 0, last and kt == KT - 1)
            if done:
                mm.then_inc(w_used, 1)

        def product_tok(pe, n, g, x_hi, x_lo, tiles, adv=0, ready=None):
            pe.wait_ge(w_low, n + 1 + adv)
            if ready:
                for kt in range(KT):
                    ready(kt)
            hi, lo = unit_w(n)
            per = tiles // 2
            for tt in range(tiles):
                po = pair[g % 2][:, tt // per, (tt % per) * CW:(tt % per + 1) * CW]
                c = slice(tt * P, (tt + 1) * P)
                for kt in range(KT):
                    mm = three(po, x_hi[:, kt, c], x_lo[:, kt, c], hi[:, kt, :], lo[:, kt, :], kt == 0, kt == KT - 1)
            mm.then_inc(w_used, 1)

        sqn, varn, dven = Tally(), Tally(), Tally()

        def norm_act_squares(act, c, x_group):
            for k in range(KT // 2):
                read_out(act, x_group + k)
                if c.sq + k >= 2:
                    act.wait_ge(sq_used, c.sq + k - 1)
                nc.scalar.activation(sq[(c.sq + k) % 2][:], x[:, 2 * k:2 * k + 2, :], ACT.Square).then_inc(sq_done, 1)
            c.sq += KT // 2

        def norm_pe_sums(pe, c):
            for k in range(KT // 2):
                pe.wait_ge(sq_done, c.sq + k + 1)
                for i in range(2):
                    for tt in range(TT):
                        mm = nc.tensor.matmul(aux[:, 3, tt:tt + 1], sq[(c.sq + k) % 2][:, i, tt * P:(tt + 1) * P], ones,
                                              start=(k == 0 and i == 0 and tt == 0), stop=(k == KT // 2 - 1 and i == 1),
                                              skip_group_check=True)
                mm.then_inc(sq_used, 1)
            c.sq += KT // 2

        def make_var(vec, c, sums, width, scale):
            vec.wait_ge(rs_done, c.var)
            nc.vector.tensor_scalar(var[:, 0:width], sums, scale, EPS, ALU.mult, ALU.add).then_inc(var_done, 1)
            c.var += 1

        def pool_root(pool, c, width):
            pool.wait_ge(var_done, c.var + 1)
            pool.wait_ge(rb_done, c.var)
            nc.gpsimd.tensor_tensor(rs[:, 0:width], var[:, 0:width], nh16[:, 0:width], ALU.pow).then_inc(rs_done, 1)
            c.var += 1

        def spread(pe, c, bank, col=0, step=1, tiles=TT, last=True, wait=True):
            if wait:
                pe.wait_ge(rs_done, c.var + 1)
            for tt in range(tiles):
                mm = nc.tensor.matmul(aux[:, bank, tt * P:(tt + 1) * P],
                                      rs[:, col + step * tt:col + step * tt + 1].broadcast_to((P, P)), ident,
                                      start=True, stop=True)
            if last:
                mm.then_inc(rb_done, 1)
                c.var += 1

        def norm_tiles(vec, c, gain, tiles):
            for kt in tiles:
                if c.hn >= 2:
                    vec.wait_ge(hn_low, c.hn - 1)
                nc.vector.scalar_tensor_tensor(tmp[:, kt % 2, :], x[:, kt, :], tab[0][:, gain + kt:gain + kt + 1],
                                               aux[:, 2, :], ALU.mult, ALU.mult).then_inc(hn_t, 1)
                c.hn += 1
                if kt > 0:
                    norm_low(vec, c, kt - 1)
                if kt == KT - 1:
                    norm_low(vec, c, kt)

        def norm_low(vec, c, kt):
            vec.wait_ge(hn_high, c.lo + 1)
            nc.vector.tensor_tensor(hn_lo[:, kt, :], tmp[:, kt % 2, :], hn_hi[:, kt, :].bitcast(F32),
                                    ALU.subtract).then_inc(hn_low, 1)
            c.lo += 1

        def norm_act_high(act, c, tiles=range(KT)):
            for kt in tiles:
                c.hn += 1
                act.wait_ge(hn_t, c.hn)
                nc.scalar.copy(hn_hi[:, kt, :], tmp[:, kt % 2, :]).then_inc(hn_high, 1)

        def hn_ready(pe, n):
            return lambda kt: pe.wait_ge(hn_low, KT * n + kt + 1)

        def hn(a):
            return lambda kt: a[:, kt, :]

        def add_residual(vec, g, k, adv=0):
            nc.vector.tensor_tensor(x[:, ds(2 * k, 2), :], pair[g % 2][:], x[:, ds(2 * k, 2), :],
                                    ALU.add).then_inc(evac[g % 2], 1)

        def mem_norm_vec(vec, c, l):
            vec.wait_ge(mem_in, 16 * (l + 1))
            for k in range(KT):
                if c.mn >= 2:
                    vec.wait_ge(mn_low, c.mn - 1)
                nc.vector.tensor_scalar(tmp_m(k), mem_raw[:, k, :], tab[0][:, TAB_MEM + 8 * l + k:TAB_MEM + 8 * l + k + 1],
                                        None, ALU.mult).then_inc(mn_t, 1)
                c.mn += 1
                if k > 0:
                    mem_low(vec, c, k - 1)
            mem_low(vec, c, KT - 1)

        def tmp_m(k):
            return mem_tmp[:, k % 2, :]

        mem_tmp = sb("mem_tmp", [P, 2, MEM])

        def mem_low(vec, c, k):
            vec.wait_ge(mn_high, c.ml + 1)
            nc.vector.tensor_tensor(mem_lo[:, k, :], tmp_m(k), mem_hi[:, k, :].bitcast(F32), ALU.subtract).then_inc(mn_low, 1)
            c.ml += 1

        def mem_norm_act(act, c):
            for k in range(KT):
                act.wait_ge(mn_t, c.mn + k + 1)
                nc.scalar.copy(mem_hi[:, k, :], tmp_m(k)).then_inc(mn_high, 1)
            c.mn += KT

        def mem_norm_pool(pool, l, u_free):
            if u_free is not None:
                pool.wait_ge(w_used, u_free)
            pool.dma_start(mem_raw[:], mem_scratch.rearrange("p (k m) -> p k m", k=KT)).then_inc(mem_in, 16)


        def load_sync(sp, ph):
            names = [("norm_mix", TAB_MIX), ("norm_xa", TAB_XA), ("norm_mem", TAB_MEM), ("norm_ffn", TAB_FFN)]
            n = 0

            def put(dst, src, **kw):
                nonlocal n
                sp.dma_start(dst, src, **kw).then_inc(loaded, 16)
                n += 1
            xv = t["x"].rearrange("a (t p) d -> (a p) t d", p=P)
            for tt in range(TT):
                put(x_tok[:, tt, :], xv[:, tt, :])
            put(cst[:], t["constants"])
            mv = t["mem"].rearrange("a (t p) d -> (a p) t d", p=P)
            put(mem_tok[:], mv)
            for name, row in names:
                put(tab_raw[0][row:row + 32, :], t[name].rearrange("l (k p) -> (l k) p", p=P))
            put(tab_raw[1][TAB_VN:TAB_VN + 32, :], t["gm_v_norm"].rearrange("l (k p) -> (l k) p", p=P))
            put(tab_raw[1][TAB_ON:TAB_ON + 16, :], t["ssd_out_norm"].rearrange("l (k p) -> (l k) p", p=P))
            put(tab_raw[1][TAB_CB:TAB_CB + 32, :], t["ssd_conv_b"].rearrange("l (k p) -> (l k) p", p=P))
            put(tab_raw[1][TAB_XQ:TAB_XQ + 4, :], t["xa_q_norm"])
            put(tab_raw[1][TAB_XK:TAB_XK + 4, :], t["xa_k_norm"])
            for row, name in ((TAB_DQ, "dsa_q_norm"), (TAB_DK, "dsa_k_norm"), (TAB_DI, "dsa_kidx_norm")):
                for h in (0, 64):
                    put(tab_raw[1][row:row + 1, h:h + 64], t[name])
            put(a_log[96:P, :], t["ssd_a_log"].rearrange("a h -> h a"))
            put(dt_bias[96:P, :], t["ssd_dt_bias"].rearrange("a h -> h a"))
            put(d_pair[:], t["ssd_d"].rearrange("a (j h) -> (a h) j", h=2), allow_slow_non_contiguous=True)
            put(tab_raw[2][:], t["ssd_conv_w"].rearrange("l c (k p) -> (l c k) p", p=P))
            assert n == N_LOADS

        def load_pe(pe, ph, c):
            g = group0[ph]
            pe.wait_ge(loaded, 16 * N_LOADS)
            for k in range(0, KT, 2):
                free_pair(pe, g)
                for i in range(2):
                    for tt in range(TT):
                        mm = nc.tensor.transpose(pair[g % 2][:, i, tt * P:(tt + 1) * P],
                                                 x_tok[:, tt, (k + i) * P:(k + i + 1) * P], ident)
                mm.then_inc(own_done, 1)
                g += 1
            for k in range(0, KT, 4):
                free_pair(pe, g)
                for i in range(4):
                    for tt in range(MT):
                        mm = nc.tensor.transpose(pair[g % 2][:, i // 2, (i % 2) * MEM + tt * P:(i % 2) * MEM + (tt + 1) * P],
                                                 mem_tok[:, tt, (k + i) * P:(k + i + 1) * P], ident)
                mm.then_inc(own_done, 1)
                g += 1
            free_pair(pe, g)
            nc.tensor.transpose(pair[g % 2][:, 0, 0:P], tab_raw[0][:], ident)
            nc.tensor.transpose(pair[g % 2][:, 1, 0:TAB1_ROWS], tab_raw[1][0:TAB1_ROWS, :],
                                cst[0:TAB1_ROWS, 0:TAB1_ROWS]).then_inc(own_done, 1)
            g += 1
            free_pair(pe, g)
            nc.tensor.transpose(pair[g % 2][:, 0, 0:P], tab_raw[2][:], ident).then_inc(own_done, 1)
            for k in range(KT // 2):
                pe.wait_ge(sq_done, c.sq + k + 1)
                for i in range(2):
                    for tt in range(MT):
                        mm = nc.tensor.matmul(aux[:, 3, tt:tt + 1], sq[(c.sq + k) % 2][:, i, tt * P:(tt + 1) * P], ones,
                                              start=(k == 0 and i == 0 and tt == 0), stop=(k == KT // 2 - 1 and i == 1),
                                              skip_group_check=True)
                mm.then_inc(sq_used, 1)
            c.sq += KT // 2
            spread(pe, c, 2, tiles=MT)

        def load_act(act, ph, c):
            g = group0[ph]
            for k in range(KT // 2):
                read_out(act, g + 4 + k // 2)
                if k >= 2:
                    act.wait_ge(sq_used, k - 1)
                nc.scalar.activation(sq[k % 2][:, :, 0:MEM], mem_row[:, 2 * k:2 * k + 2, :], ACT.Square).then_inc(sq_done, 1)
            c.sq += KT // 2
            mem_norm_act(act, c)

        def load_vec(vec, ph, c):
            g, o = group0[ph], own0[ph]
            for k in range(0, KT, 2):
                vec.wait_ge(own_done, o + k // 2 + 1)
                nc.vector.tensor_copy(x[:, k:k + 2, :], pair[g % 2][:]).then_inc(evac[g % 2], 1)
                g += 1
            for k in range(0, KT, 4):
                vec.wait_ge(own_done, o + 4 + k // 4 + 1)
                nc.vector.tensor_copy(mem_row[:, k:k + 4, :].rearrange("p (a b) m -> p a (b m)", a=2),
                                      pair[g % 2][:]).then_inc(evac[g % 2], 1)
                g += 1
            vec.wait_ge(own_done, o + 7)
            nc.vector.tensor_copy(tab[0][:], pair[g % 2][:, 0, 0:P])
            nc.vector.tensor_copy(tab[1][:], pair[g % 2][:, 1, 0:TAB1_ROWS]).then_inc(evac[g % 2], 1)
            g += 1
            vec.wait_ge(own_done, o + 8)
            nc.vector.tensor_copy(tab[2][:], pair[g % 2][:, 0, 0:P]).then_inc(evac[g % 2], 1)
            read_out(vec, g)
            vec.wait_ge(sq_used, c.sq + KT // 2)
            c.sq += KT // 2
            vec.wait_ge(consts_set, 2)
            make_var(vec, c, aux[:, 3, 0:MT], MT, 1.0 / D)
            vec.wait_ge(rb_done, c.var)
            for k in range(KT):
                ins = nc.vector.tensor_tensor(mem_row[:, k, :], mem_row[:, k, :], aux[:, 2, 0:MEM], ALU.mult)
            ins.then_inc(mem_made, 1)
            mem_norm_vec(vec, c, 0)

        def load_pool(pool, ph, c):
            nc.gpsimd.memset(var[:], 1.0).then_inc(consts_set, 1)
            nc.gpsimd.memset(nh16[:], -0.5).then_inc(consts_set, 1)
            pool.wait_ge(consts_set, 2)
            pool_root(pool, c, MT)
            pool.wait_ge(mem_made, 1)
            pool.dma_start(mem_scratch.rearrange("p (k m) -> p k m", k=KT), mem_row[:]).then_inc(mem_kept, 16)
            pool.wait_ge(mem_kept, 16)
            mem_norm_pool(pool, 0, None)

        def ffn_units(sp, ph, l):
            up, down = t["ffn_w_up"][l], t["ffn_w_down"][l]
            n0 = unit0[ph]
            for half in range(2):
                def up_units(i):
                    for j in range(2):
                        load_unit(sp, n0 + j, [(slot(j + n0), cols(up, half * HALF + (2 * i + j) * CW))], 2 * i)

                repeat(sp, 4, up_units, n0 == 0)
                n0 += 8
                with sp.Fori(0, 2) as i:
                    for j in range(4):
                        load_unit(sp, n0 + j, [(slot(j + n0), cols(down, (2 * i + j // 2) * CW, k0=half * HALF + (j % 2) * D))],
                                  4 * i)
                n0 += 8

        def ffn_pe(pe, ph, l, c, x_group):
            n, g = unit0[ph], group0[ph]
            norm_pe_sums(pe, c)
            spread(pe, c, 2)
            for half in range(2):
                with pe.Fori(0, 4) as i:
                    for j in range(2):
                        free_pair(pe, g + j, i)
                        product(pe, n + j, g + j, hn(hn_hi), hn(hn_lo), 2 * i, ready=hn_ready(pe, ph - 1) if j == 0 else None)
                n, g = n + 8, g + 8
                a0 = a_base(ph) + 8 * half
                with pe.Fori(0, 2) as i:
                    for j in range(4):
                        if j % 2 == 0:
                            free_pair(pe, g + j // 2, i)
                        first = j == 0
                        product(pe, n + j, g + j // 2, lambda kt, j=j: hid_hi[:, 8 * (j % 2) + kt, :],
                                lambda kt, j=j: hid_lo[:, 8 * (j % 2) + kt, :], 4 * i, first=j % 2 == 0, last=j % 2 == 1,
                                ready=(lambda kt, j=j, a0=a0: pe.wait_ge(a_low, a0 + (8 * j + kt) // 2 + 1)) if j < 2 else None)
                n, g = n + 8, g + 4

        def ffn_act(act, ph, l, c, x_group):
            norm_act_squares(act, c, x_group)
            norm_act_high(act, c)
            n, g = unit0[ph], group0[ph]
            for half in range(2):
                a0 = a_base(ph) + 8 * half
                def up(i):
                    for j in range(2):
                        split_high(act, n + j + 1, 2 * i)
                        act.wait_ge(w_used, n + j + 1 + 2 * i)
                        if a0 + j > 0 or not isinstance(i, int):
                            act.wait_ge(a_low, a0 + j + 2 * i)
                        nc.scalar.activation(tmp[:], pair[(g + j) % 2][:], ACT.Relu).then_inc(evac[(g + j) % 2], 1)
                        act.wait_ge(a_sq, a0 + j + 1 + 2 * i)
                        nc.scalar.copy(hid_hi[:, ds(4 * i + 2 * j, 2), :], tmp[:]).then_inc(a_high, 1)

                repeat(act, 4, up, n == 0)
                n, g = n + 8, g + 8
                if half == 0 and l + 1 < DEPTH:
                    mem_norm_act(act, c)
                with act.Fori(0, 2) as i:
                    for j in range(4):
                        split_high(act, n + j + 1, 4 * i)
                n, g = n + 8, g + 4

        def ffn_vec(vec, ph, l, c, x_group):
            vec.wait_ge(sq_used, c.sq + KT // 2)
            c.sq += KT // 2
            make_var(vec, c, aux[:, 3, 0:TT], TT, 1.0 / D)
            vec.wait_ge(rb_done, c.var)
            norm_tiles(vec, c, TAB_FFN + 8 * l, range(KT))
            n, g = unit0[ph], group0[ph]
            for half in range(2):
                a0 = a_base(ph) + 8 * half
                with vec.Fori(0, 4) as i:
                    for j in range(2):
                        split_low(vec, n + j + 1, 2 * i)
                        read_out(vec, g + j, i)
                        nc.vector.tensor_tensor(tmp[:], tmp[:], tmp[:], ALU.mult).then_inc(a_sq, 1)
                        vec.wait_ge(a_high, a0 + j + 1 + 2 * i)
                        nc.vector.tensor_tensor(hid_lo[:, ds(4 * i + 2 * j, 2), :], tmp[:],
                                                hid_hi[:, ds(4 * i + 2 * j, 2), :].bitcast(F32),
                                                ALU.subtract).then_inc(a_low, 1)
                n, g = n + 8, g + 8
                if half == 0 and l + 1 < DEPTH:
                    mem_norm_vec(vec, c, l + 1)
                with vec.Fori(0, 2) as i:
                    for j in range(4):
                        split_low(vec, n + j + 1, 4 * i)
                        if j % 2 == 1:
                            vec.wait_ge(w_used, n + j + 1 + 4 * i)
                            if half == 1:
                                read_out(vec, g - 12 + j // 2, i)
                            add_residual(vec, g + j // 2, 2 * i + j // 2)
                n, g = n + 8, g + 4

        def ffn_pool(pool, ph, l, c):
            pool_root(pool, c, TT)
            if l + 1 < DEPTH:
                mem_norm_pool(pool, l + 1, unit0[ph])

        def xattn_units(sp, ph, l):
            n = unit0[ph]
            for j in range(2):
                load_unit(sp, n + j, [(slot(n + j), cols(t["xa_w_kv"][l], j * CW))])
            for j in range(2):
                load_unit(sp, n + 2 + j, [(slot(n + j), cols(t["xa_w_kv"][l], 512 + j * CW))])
            for j in range(2):
                load_unit(sp, n + 4 + j, [(slot(n + j), cols(t["xa_w_q"][l], j * CW))])
            for j in range(2):
                load_unit(sp, n + 6 + j, [(slot(n + j, 4, 512), cols(t["xa_w_out"][l], j * 512, 512, kt=4))])

        def xattn_pe(pe, ph, l, c, x_group):
            n, g = unit0[ph], group0[ph]
            mem_ready = lambda kt: pe.wait_ge(mn_low, KT * l + kt + 1)
            mem_h, mem_l = (lambda kt: mem_hi[:, kt, :]), (lambda kt: mem_lo[:, kt, :])
            free_pair(pe, g)
            product(pe, n, g, mem_h, mem_l, ready=mem_ready, tokens=MEM)
            norm_pe_sums(pe, c)
            free_pair(pe, g + 1)
            product(pe, n + 1, g + 1, mem_h, mem_l, tokens=MEM)
            spread(pe, c, 2)
            for j in range(2):
                free_pair(pe, g + 2 + j)
                product_tok(pe, n + 2 + j, g + 2 + j, mem_hi, mem_lo, MT)
            for h in range(0, XH, 2):
                pe.wait_ge(sq_done, c.sq + 1)
                for i in range(2):
                    for tt in range(MT):
                        mm = nc.tensor.matmul(aux[:, 0, XH * tt + h + i:XH * tt + h + i + 1],
                                              sq[c.sq % 2][:, i, tt * P:(tt + 1) * P], ones, start=True, stop=True)
                mm.then_inc(sq_used, 1)
                c.sq += 1
            for j in range(2):
                free_pair(pe, g + 4 + j)
                product(pe, n + 4 + j, g + 4 + j, hn(hn_hi), hn(hn_lo), ready=hn_ready(pe, ph - 1) if j == 0 else None)
            pe.wait_ge(rs_done, c.var + 1)
            for h in range(XH):
                for tt in range(MT):
                    col = XH * tt + h
                    mm = nc.tensor.matmul(aux[:, h // 2, (h % 2) * MEM + tt * P:(h % 2) * MEM + (tt + 1) * P],
                                          rs[:, col:col + 1].broadcast_to((P, P)), ident, start=True, stop=True)
            mm.then_inc(rb_done, 1)
            c.var += 1
            for h in range(0, XH, 2):
                pe.wait_ge(sq_done, c.sq + 1)
                for i in range(2):
                    for tt in range(TT):
                        mm = nc.tensor.matmul(aux[:, 3, XH * tt + h + i:XH * tt + h + i + 1],
                                              sq[c.sq % 2][:, i, tt * P:(tt + 1) * P], ones, start=True, stop=True)
                mm.then_inc(sq_used, 1)
                c.sq += 1
            pe.wait_ge(rs_done, c.var + 1)
            pe.wait_ge(kn_done, XH * (l + 1))
            for h in range(XH):
                if h == 2:
                    pe.wait_ge(hn_low, KT * ph)
                spread(pe, c, h, col=h, step=XH, last=h == XH - 1, wait=False)
            pg = g + 6

            def scores(h):
                pe.wait_ge(qn_done, XH * l + (h + 1 if h < 2 else XH))
                if h == 0:
                    pe.wait_ge(qn_done, XH * l + 2)
                if h == 1:
                    pe.wait_ge(qn_done, XH * l + 4)
                if h >= 2:
                    pe.wait_ge(exp_done, TT * (XH * l + h - 1))
                for tt in range(TT):
                    mm = nc.tensor.matmul(aux[:, 2 * (h % 2) + tt // 2, (tt % 2) * MEM:(tt % 2 + 1) * MEM],
                                          q_raw[:, h, tt * P:(tt + 1) * P], k_t[:, h, :], start=True, stop=True)
                mm.then_inc(score_done, 1)

            def turn(h):
                gg = pg + 2 * h
                pe.wait_ge(prob_done, XH * l + h + 1)
                free_pair(pe, gg)
                for m in range(MT):
                    for tt in range(TT):
                        mm = nc.tensor.transpose(pair[gg % 2][:, m, tt * P:(tt + 1) * P],
                                                 prob[h % 2][:, tt, m * P:(m + 1) * P], ident)
                mm.then_inc(own_done, 1)

            def values(h):
                gg = pg + 2 * h + 1
                read_out(pe, gg - 1)
                free_pair(pe, gg)
                for m in range(MT):
                    mm = nc.tensor.matmul(pair[gg % 2][:, 0, :], v_m[:, m, h * P:(h + 1) * P], prob_t[h % 2][:, m, :],
                                          start=m == 0, stop=m == MT - 1)
                mm.then_inc(own_done, 1)

            scores(0)
            scores(1)
            for h in range(XH):
                turn(h)
                if h + 2 < XH:
                    scores(h + 2)
                values(h)
            for j in range(2):
                pe.wait_ge(w_low, n + 6 + j + 1)
                hi, lo = unit_w(n + j, 4, 512)
                for half in range(2):
                    gg = g + 14 + 2 * j + half
                    free_pair(pe, gg)
                    for kt in range(XH):
                        pe.wait_ge(o_low, XH * l + kt + 1)
                        for m in range(2):
                            cc = slice((2 * half + m) * P, (2 * half + m + 1) * P)
                            mm = three(pair[gg % 2][:, m, :], hi[:, kt, cc], lo[:, kt, cc], o_hi[:, kt, :], o_lo[:, kt, :],
                                       kt == 0, kt == XH - 1)
                    mm.then_inc(w_used if half else half_out, 1)

        def xattn_act(act, ph, l, c, x_group):
            n, g = unit0[ph], group0[ph]
            split_high(act, n + 1)
            norm_act_squares(act, c, x_group)
            split_high(act, n + 2)
            norm_act_high(act, c, range(4))
            split_high(act, n + 3)
            norm_act_high(act, c, range(4, KT))
            for j in range(2):
                read_out(act, g + j)
                act.wait_ge(sq_used, c.sq - 1)
                nc.scalar.activation(sq[c.sq % 2][:, :, 0:MEM], k_raw[:, 2 * j:2 * j + 2, :], ACT.Square).then_inc(sq_done, 1)
                c.sq += 1
            for j in range(2):
                act.wait_ge(w_used, n + 3 + j)
                nc.scalar.copy(v_m[:, :, j * CW:(j + 1) * CW], pair[(g + 2 + j) % 2][:, :, 0:CW]).then_inc(evac[(g + 2 + j) % 2], 1)
                split_high(act, n + 4 + j)
            split_high(act, n + 6)
            for j in range(2):
                read_out(act, g + 4 + j)
                act.wait_ge(sq_used, c.sq - 1)
                nc.scalar.activation(sq[c.sq % 2][:], q_raw[:, 2 * j:2 * j + 2, :], ACT.Square).then_inc(sq_done, 1)
                c.sq += 1
            split_high(act, n + 7)

            def exps(h):
                act.wait_ge(nb_done, XH * l + h + 1)
                if h >= 2:
                    act.wait_ge(own_done, own0[ph] + 2 * (h - 2) + 1)
                for tt in range(TT):
                    nc.scalar.activation(prob[h % 2][:, tt, :], aux[:, 2 * (h % 2) + tt // 2, (tt % 2) * MEM:(tt % 2 + 1) * MEM],
                                         ACT.Exp, bias=soft[:, h % 2, 1, tt:tt + 1], scale=XSCALE,
                                         accum_out=soft[:, h % 2, 2, tt:tt + 1]).then_inc(exp_done, 1)

            def high(h):
                act.wait_ge(own_done, own0[ph] + 2 * h + 2)
                nc.scalar.copy(o_hi[:, h, :], pair[(g + 7 + 2 * h) % 2][:, 0, :]).then_inc(o_high, 1)

            exps(0)
            exps(1)
            for h in range(XH):
                if h + 2 < XH:
                    exps(h + 2)
                high(h)
            split_high(act, n + 8)

        def xattn_vec(vec, ph, l, c, x_group):
            n, g = unit0[ph], group0[ph]
            split_low(vec, n + 1)
            vec.wait_ge(w_used, n + 1)
            nc.vector.tensor_copy(k_raw[:, 0:2, :], pair[g % 2][:, :, 0:MEM]).then_inc(evac[g % 2], 1)
            split_low(vec, n + 2)
            vec.wait_ge(sq_used, c.sq + KT // 2)
            c.sq += KT // 2
            make_var(vec, c, aux[:, 3, 0:TT], TT, 1.0 / D)
            vec.wait_ge(w_used, n + 2)
            nc.vector.tensor_copy(k_raw[:, 2:4, :], pair[(g + 1) % 2][:, :, 0:MEM]).then_inc(evac[(g + 1) % 2], 1)
            vec.wait_ge(rb_done, c.var)
            norm_tiles(vec, c, TAB_XA + 8 * l, range(4))
            split_low(vec, n + 3)
            norm_tiles(vec, c, TAB_XA + 8 * l, range(4, KT))
            vec.wait_ge(sq_used, c.sq + 2)
            c.sq += 2
            make_var(vec, c, aux[:, 0, 0:XH * MT], XH * MT, 1.0 / P)
            split_low(vec, n + 4)
            split_low(vec, n + 5)
            for j in range(2):
                vec.wait_ge(w_used, n + 5 + j)
                nc.vector.tensor_copy(q_raw[:, 2 * j:2 * j + 2, :], pair[(g + j) % 2][:]).then_inc(evac[(g + j) % 2], 1)
                split_low(vec, n + 6 + j)
            vec.wait_ge(rb_done, c.var)
            for h in range(XH):
                nc.vector.scalar_tensor_tensor(k_t[:, h, :], k_raw[:, h, :], tab[1][:, TAB_XK + l:TAB_XK + l + 1],
                                               aux[:, h // 2, (h % 2) * MEM:(h % 2 + 1) * MEM], ALU.mult,
                                               ALU.mult).then_inc(kn_done, 1)
            vec.wait_ge(sq_used, c.sq + 2)
            c.sq += 2
            make_var(vec, c, aux[:, 3, 0:XH * TT], XH * TT, 1.0 / P)
            vec.wait_ge(rb_done, c.var)
            for h in range(XH):
                nc.vector.scalar_tensor_tensor(q_raw[:, h, :], q_raw[:, h, :], tab[1][:, TAB_XQ + l:TAB_XQ + l + 1],
                                               aux[:, h, :], ALU.mult, ALU.mult).then_inc(qn_done, 1)

            def maxima(h):
                vec.wait_ge(score_done, XH * l + h + 1)
                a = 2 * (h % 2)
                nc.vector.reduce_max(soft[:, h % 2, 0, :].rearrange("p (a b) -> p a b", a=2),
                                     aux[:, a:a + 2, :].rearrange("p a (b m) -> p a b m", b=2), AX).then_inc(dve, 1)
                c.dv += 1
                vec.wait_ge(dve, c.dv)
                nc.vector.tensor_scalar(soft[:, h % 2, 1, :], soft[:, h % 2, 0, :], -XSCALE, None, ALU.mult).then_inc(nb_done, 1)

            def norm(h):
                vec.wait_ge(exp_done, TT * (XH * l + h + 1))
                nc.vector.reciprocal(rinv[:, h % 2, :], soft[:, h % 2, 2, :]).then_inc(dve, 1)
                c.dv += 1
                vec.wait_ge(dve, c.dv)
                for tt in range(TT):
                    ins = nc.vector.tensor_scalar(prob[h % 2][:, tt, :], prob[h % 2][:, tt, :], rinv[:, h % 2, tt:tt + 1],
                                                  None, ALU.mult)
                ins.then_inc(prob_done, 1)

            def copy_turned(h):
                vec.wait_ge(own_done, own0[ph] + 2 * h + 1)
                gg = g + 6 + 2 * h
                nc.vector.tensor_copy(prob_t[h % 2][:], pair[gg % 2][:]).then_inc(evac[gg % 2], 1)

            def low(h):
                vec.wait_ge(o_high, XH * l + h + 1)
                gg = g + 7 + 2 * h
                nc.vector.tensor_tensor(o_lo[:, h, :], pair[gg % 2][:, 0, :], o_hi[:, h, :].bitcast(F32),
                                        ALU.subtract).then_inc(o_low, 1)
                nc.vector.tensor_copy(junk[:, 0:1], cst[:, 0:1]).then_inc(evac[gg % 2], 1)

            maxima(0)
            maxima(1)
            for h in range(XH):
                norm(h)
                copy_turned(h)
                if h + 2 < XH:
                    maxima(h + 2)
                low(h)
            split_low(vec, n + 8)
            for k in range(4):
                gg = g + 14 + k
                if k % 2:
                    vec.wait_ge(w_used, n + 7 + k // 2)
                else:
                    vec.wait_ge(half_out, 2 * l + k // 2 + 1)
                add_residual(vec, gg, k)

        junk = sb("junk", [P, 4])

        def xattn_pool(pool, ph, l, c):
            pool_root(pool, c, TT)
            pool_root(pool, c, XH * MT)
            pool_root(pool, c, XH * TT)

        UM = [("u", 0), ("u", 1)]
        for k in range(6):
            UM += [("m", k), ("u", k + 2)]
        UM += [("m", 6), ("m", 7)]

        def gmlp_units(sp, ph, l, j):
            w, n = t["gm_w_in"][j], unit0[ph]

            def v_units(i):
                for k in range(2):
                    load_unit(sp, n + k, [(slot(n + k), cols(w, GM_HID + (2 * i + k) * CW))], 2 * i)

            repeat(sp, 4, v_units, n == 0)
            n += 8
            with sp.Fori(0, 4) as i:
                for k in range(2):
                    load_unit(sp, n + k, [(slot(n + k), cols(w, (2 * i + k) * CW))], 2 * i)
            n += 8
            with sp.Fori(0, 2) as i:
                for k in range(4):
                    load_unit(sp, n + k, [(slot(n + k), cols(t["gm_w_out"][j], (2 * i + k // 2) * CW, k0=(k % 2) * D))], 4 * i)

        def gmlp_pe(pe, ph, l, j, c, x_group):
            n, g, o = unit0[ph], group0[ph], own0[ph]
            norm_pe_sums(pe, c)
            spread(pe, c, 2)
            with pe.Fori(0, 4) as i:
                for k in range(2):
                    free_pair(pe, g + k, i)
                    product_tok(pe, n + k, g + k, hn_hi, hn_lo, TT, 2 * i, ready=hn_ready(pe, ph - 1) if k == 0 else None)
            n, g = n + 8, g + 8
            pe.wait_ge(ws_in, 32 * (j + 1))
            free_pair(pe, g)
            for k in range(GM_G):
                mm = nc.tensor.transpose(pair[g % 2][:, k // 4, (k % 4) * P:(k % 4 + 1) * P], ws_raw[:, k, :], ident)
            mm.then_inc(own_done, 1)
            g += 1
            for kind, k in UM:
                free_pair(pe, g)
                if kind == "u":
                    product(pe, n, g, hn(hn_hi), hn(hn_lo))
                    n += 1
                else:
                    if k == 0:
                        c.var += 1
                        pe.wait_ge(rb_done, c.var)
                        pe.wait_ge(ws_ready, j + 1)
                    for i in range(2):
                        ct = 2 * k + i
                        for b in range(TT):
                            mm = nc.tensor.matmul(pair[g % 2][:, i, b * P:(b + 1) * P], v_tok[:, b, ct * P:(ct + 1) * P],
                                                  ws_t[:, k, :], start=True, stop=True)
                    mm.then_inc(own_done, 1)
                g += 1
            a0 = a_base(ph)
            with pe.Fori(0, 2) as i:
                for k in range(4):
                    if k % 2 == 0:
                        free_pair(pe, g + k // 2, i)
                    product(pe, n + k, g + k // 2,
                            lambda kt, k=k: uv_hi[:, :, (8 * (k % 2) + kt) * P:(8 * (k % 2) + kt + 1) * P],
                            lambda kt, k=k: uv_lo[:, 8 * (k % 2) + kt, :].rearrange("p (a b) -> p a b", a=TT),
                            4 * i, first=k % 2 == 0, last=k % 2 == 1,
                            ready=(lambda kt, k=k: pe.wait_ge(a_low, a0 + (8 * k + kt) // 2 + 1)) if k < 2 else None)

        def gmlp_act(act, ph, l, j, c, x_group):
            n, g, o = unit0[ph], group0[ph], own0[ph]
            norm_act_squares(act, c, x_group)
            norm_act_high(act, c)

            def v_step(i):
                for k in range(2):
                    split_high(act, n + k + 1, 2 * i)
                    act.wait_ge(w_used, n + k + 1 + 2 * i)
                    nc.scalar.activation(v_tok[:, :, ds((2 * i + k) * CW, CW)],
                                         pair[(g + k) % 2][:].rearrange("p a (b m) -> p (a b) m", b=2),
                                         ACT.Gelu_apprx_tanh).then_inc(evac[(g + k) % 2], 1)

            repeat(act, 4, v_step, n == 0)
            n, g = n + 8, g + 8
            read_out(act, g - 2)
            read_out(act, g - 1)
            for b in range(2):
                if b:
                    act.wait_ge(vss_a, 2 * j + b)
                nc.scalar.activation(square_a[:], v_tok[:, b, :], ACT.Square, accum_out=vss[:, b:b + 1]).then_inc(vss_a, 1)
            g += 1
            m = 0
            for q, (kind, k) in enumerate(UM):
                if kind == "u":
                    split_high(act, n + 1)
                    act.wait_ge(w_used, n + 1)
                    if k == 0:
                        act.wait_ge(own_done, o + 1)
                    if k == 2:
                        act.wait_ge(vss_a, 2 * (j + 1))
                    if k == 4:
                        act.wait_ge(vss_d, 2 * (j + 1))
                    nc.scalar.activation(u_t[:, 2 * k:2 * k + 2, :], pair[g % 2][:], ACT.Gelu_apprx_tanh).then_inc(evac[g % 2], 1)
                    n += 1
                else:
                    act.wait_ge(a_sq, a_base(ph) + k + 1)
                    nc.scalar.copy(uv_hi[:, :, 2 * k * P:(2 * k + 2) * P].rearrange("p b (c q) -> p c b q", c=2),
                                   tmp[:].rearrange("p c (b q) -> p c b q", b=TT)).then_inc(a_high, 1)
                g += 1
            with act.Fori(0, 2) as i:
                for k in range(4):
                    split_high(act, n + k + 1, 4 * i)

        vss = sb("vss", [P, TT])

        def gmlp_vec(vec, ph, l, j, c, x_group):
            n, g, o = unit0[ph], group0[ph], own0[ph]
            vec.wait_ge(sq_used, c.sq + KT // 2)
            c.sq += KT // 2
            make_var(vec, c, aux[:, 3, 0:TT], TT, 1.0 / D)
            vec.wait_ge(rb_done, c.var)
            norm_tiles(vec, c, TAB_MIX + 8 * l, range(KT))
            with vec.Fori(0, 4) as i:
                for k in range(2):
                    split_low(vec, n + k + 1, 2 * i)
            n, g = n + 8, g + 8
            vec.wait_ge(own_done, o + 1)
            nc.vector.tensor_copy(ws_t[:], pair[g % 2][:].rearrange("p a (b t) -> p (a b) t", b=4)).then_inc(evac[g % 2], 1)
            read_out(vec, g)
            nc.vector.memset(ws_t[64:128, :, 0:64], 0.0).then_inc(ws_ready, 1)
            read_out(vec, g - 2)
            read_out(vec, g - 1)
            for b in range(2, TT):
                if b == 3:
                    vec.wait_ge(vss_d, 2 * j + 1)
                nc.vector.tensor_tensor_reduce(square_d[:], v_tok[:, b, :], v_tok[:, b, :], 1.0, 0.0, ALU.mult, ALU.add,
                                               vss[:, b:b + 1]).then_inc(vss_d, 1)
            vec.wait_ge(vss_d, 2 * (j + 1))
            vec.wait_ge(vss_a, 2 * (j + 1))
            make_var(vec, c, vss[:], TT, 1.0 / GM_HID)
            split_low(vec, n + 1)
            vec.wait_ge(rs_done, c.var)
            for b in range(TT):
                ins = nc.vector.tensor_scalar(v_tok[:, b, :], v_tok[:, b, :], rs[:, b:b + 1], None, ALU.mult)
            ins.then_inc(rb_done, 1)
            n += 1
            g += 1
            um_group = {}
            for q, (kind, k) in enumerate(UM):
                um_group[kind, k] = g + q
                if kind == "u":
                    if k < 7 or True:
                        if k > 0:
                            split_low(vec, n + 1)
                            n += 1
                else:
                    own = [x_ for x_ in UM[:q] if x_[0] == "m"]
                    gg = g + q
                    vec.wait_ge(own_done, o + 2 + len(own))
                    for i in range(2):
                        ct = 2 * k + i
                        if a_base(ph) + k > 0:
                            vec.wait_ge(a_low, a_base(ph) + k)
                        gain = TAB_VN + 16 * j + ct
                        ins = nc.vector.scalar_tensor_tensor(
                            tmp[:, i, :].rearrange("p (b t) -> p b t", b=TT), pair[gg % 2][:, i, :].rearrange("p (b t) -> p b t", b=TT),
                            tab[1][:, gain:gain + 1], bs_b[:, k:k + 1, :].broadcast_to((P, TT, P)), ALU.mult, ALU.add)
                    ins.then_inc(evac[gg % 2], 1)
                    read_out(vec, gg)
                    read_out(vec, um_group["u", k])
                    nc.vector.tensor_tensor(tmp[:], tmp[:], u_t[:, 2 * k:2 * k + 2, :], ALU.mult).then_inc(a_sq, 1)
                    vec.wait_ge(a_high, a_base(ph) + k + 1)
                    nc.vector.tensor_tensor(uv_lo[:, 2 * k:2 * k + 2, :].rearrange("p c (b q) -> p c b q", b=TT),
                                            tmp[:].rearrange("p c (b q) -> p c b q", b=TT),
                                            uv_hi[:, :, 2 * k * P:(2 * k + 2) * P].rearrange("p b (c q) -> p c b q", c=2).bitcast(F32),
                                            ALU.subtract).then_inc(a_low, 1)
            g += len(UM)
            with vec.Fori(0, 2) as i:
                for k in range(4):
                    split_low(vec, n + k + 1, 4 * i)
                    if k % 2 == 1:
                        vec.wait_ge(w_used, n + k + 1 + 4 * i)
                        add_residual(vec, g + k // 2, 2 * i + k // 2)

        def gmlp_pool(pool, ph, l, j, c):
            pool_root(pool, c, TT)
            pool.wait_ge(w_used, unit0[ph])
            if unit0[ph] == 0:
                pool.wait_ge(own_done, 8)
            pool.dma_start(ws_raw[:], t["gm_w_s"][j].rearrange("g t s -> t g s")).then_inc(ws_in, 16)
            pool.dma_start(bs_b[:], t["gm_b_s"][j:j + 1].broadcast_to((P, GM_G, P))).then_inc(ws_in, 16)
            pool_root(pool, c, TT)

        def ssd_units(sp, ph):
            w, n = t["ssd_w_in"][0], unit0[ph]
            load_unit(sp, n, [(slot(n, width=P), cols(w, SSD_IN - P, P))])
            wbc = w[:, 2 * SSD_XBC:SSD_DT].rearrange("(k p) (q m) -> p k q m", p=P, q=2)
            with sp.Fori(0, SSD_G // 2) as i:
                for p in range(2):
                    gv, u = 2 * i + p, n + 1 + 3 * p
                    load_unit(sp, u, [(slot(u), cols(w, SSD_XBC + gv * CW))], 6 * i)
                    bc_col = sp.snap(gv * P)
                    load_unit(sp, u + 1, [(slot(u + 1)[:, :, q * P:(q + 1) * P], wbc[:, :, q, ds(bc_col, P)])
                                          for q in range(2)], 6 * i)
                    load_unit(sp, u + 2, [(slot(u + 2), cols(w, 2 * CW * i + p * CW))], 6 * i)
            n += 1 + 3 * SSD_G
            with sp.Fori(0, 2) as i:
                for k in range(4):
                    load_unit(sp, n + k, [(slot(n + k), cols(t["ssd_w_out"][0], (2 * i + k // 2) * CW, k0=(k % 2) * D))], 4 * i)

        def ssd_pe(pe, ph, c, x_group):
            n, g, o = unit0[ph], group0[ph], own0[ph]
            norm_pe_sums(pe, c)
            spread(pe, c, 2)
            nc.tensor.matmul(aux[:, 0, 0:16], cst[0:2, 4 * P:5 * P], d_pair[:], start=True, stop=True).then_inc(ssd_aux, 1)
            free_pair(pe, g)
            pe.wait_ge(w_low, n + 1)
            hi, lo = unit_w(n, width=P)
            for kt in range(KT):
                hn_ready(pe, ph - 1)(kt)
                mm = three(pair[g % 2][:, 0, :], hi[:, kt, :], lo[:, kt, :], hn_hi[:, kt, :], hn_lo[:, kt, :], kt == 0, kt == KT - 1)
            mm.then_inc(w_used, 1)
            pe.wait_ge(ssd_scan, TT)
            pe.wait_ge(ssd_d, 1)
            for q in range(2):
                for b in range(TT):
                    mm = nc.tensor.transpose(aux[:, 0, (q * TT + b) * 32:(q * TT + b + 1) * 32], dta[96:P, q, b * P:(b + 1) * P],
                                             cst[96:P, 96:P])
            mm.then_inc(ssd_aux, 1)
            pe.wait_ge(ssd_tok, 1)
            nc.tensor.matmul(aux[:, 1, 0:P], cst[:, P:2 * P], dta_tok[:, 1, :, :].rearrange("p b h -> p (b h)"),
                             start=True, stop=True).then_inc(ssd_aux, 1)
            with pe.Fori(0, SSD_G // 2) as i:
                for p in range(2):
                    gv, u, gg, adv, ga = 2 * i + p, n + 1 + 3 * p, g + 1 + 5 * p, 6 * i, 5 * i
                    for k in range(3):
                        free_pair(pe, gg + k, ga)
                        product(pe, u + k, gg + k, hn(hn_hi), hn(hn_lo), adv)
                    pe.wait_ge(s_act, SSD_ACT * gv + 3)
                    free_pair(pe, gg + 3, ga)
                    for ct in range(2):
                        for b in range(TT):
                            mm = nc.tensor.transpose(pair[(gg + 3) % 2][:, b // 2, (b % 2) * CW + ct * P:(b % 2) * CW + (ct + 1) * P],
                                                     xg[:, ct, b * P:(b + 1) * P], ident)
                    mm.then_inc(own_done, 1)
                    pe.wait_ge(s_act, SSD_ACT * gv + 6)
                    pe.wait_ge(ssd_dec, 1)
                    for b in range(TT):
                        mm = nc.tensor.transpose(aux[:, 0, b * P:(b + 1) * P], bc[:, 0, b * P:(b + 1) * P], ident)
                    mm.then_inc(ssd_aux, 1)
                    for b in range(TT):
                        mm = nc.tensor.matmul(aux[:, 1, b * P:(b + 1) * P], bc[:, 0, b * P:(b + 1) * P], bc[:, 1, b * P:(b + 1) * P],
                                              start=True, stop=True)
                    mm.then_inc(ssd_aux, 1)
                    for r in range(4):
                        if r < 2:
                            pe.wait_ge(ssd_y, 2 * gv)
                        else:
                            pe.wait_ge(s_seg, 4 * gv + r - 1)
                        for b in range(TT):
                            mm = nc.tensor.matmul(aux[:, 2 + r % 2, b * P:(b + 1) * P],
                                                  par[p][:, PAR_A + 4 * b + r:PAR_A + 4 * b + r + 1].broadcast_to((P, P)), ident,
                                                  start=True, stop=True)
                        mm.then_inc(ssd_aux, 1)
                    pe.wait_ge(s_act, SSD_ACT * gv + 8)
                    pe.wait_ge(s_cb, gv + 1)
                    pe.wait_ge(s_xdd, gv + 1)
                    for b in range(TT - 1):
                        mm = nc.tensor.matmul(aux[:, b // 2, (b % 2) * CW:(b % 2 + 1) * CW], b_tok[:, b * P:(b + 1) * P], xdd[:, b, :],
                                              start=True, stop=True)
                    mm.then_inc(ssd_aux, 1)
                    free_pair(pe, gg + 4, ga)
                    pe.wait_ge(s_state, gv + 1)
                    for r in range(4):
                        pe.wait_ge(s_m, 4 * gv + r + 1)
                        pe.wait_ge(s_c, 4 * gv + r + 1)
                        rows = slice(64 * (r % 2), 64 * (r % 2) + 64)
                        for b in range(TT):
                            po = pair[(gg + 4) % 2][rows, r // 2, b * P:(b + 1) * P]
                            mm = nc.tensor.matmul(po, xdt[:, b, 64 * r:64 * r + 64], seg(r)[:, b * P:(b + 1) * P],
                                                  start=True, stop=b == 0)
                            if b > 0:
                                mm = nc.tensor.matmul(po, state[:, b - 1, 64 * r:64 * r + 64], cs[:, r, b * P:(b + 1) * P],
                                                      start=False, stop=True)
                    mm.then_inc(own_done, 1)
                    pe.wait_ge(s_act, SSD_ACT * gv + 17)
                    pe.wait_ge(s_seg, 4 * gv + 4)
                    for ct in range(2):
                        for b in range(TT):
                            mm = nc.tensor.matmul(aux[:, 3, b:b + 1], tmp[:, ct, b * P:(b + 1) * P], ones,
                                                  start=(ct == 0 and b == 0), stop=ct == 1, skip_group_check=True)
                    mm.then_inc(ssd_aux, 1)
                    pe.wait_ge(rs_done, c.var + 1 + gv)
                    for b in range(TT):
                        mm = nc.tensor.matmul(aux[:, 2, b * P:(b + 1) * P], rs[:, b:b + 1].broadcast_to((P, P)), ident,
                                              start=True, stop=True)
                    mm.then_inc(rb_done, 1)
            c.var += SSD_G
            n, g = n + 1 + 3 * SSD_G, g + 1 + 5 * SSD_G
            with pe.Fori(0, 2) as i:
                for k in range(4):
                    if k % 2 == 0:
                        free_pair(pe, g + k // 2, i)
                    product(pe, n + k, g + k // 2, lambda kt, k=k: y_hi[:, 8 * (k % 2) + kt, :],
                            lambda kt, k=k: y_lo[:, 8 * (k % 2) + kt, :], 4 * i, first=k % 2 == 0, last=k % 2 == 1,
                            ready=(lambda kt, k=k: pe.wait_ge(s_ylow, (8 * k + kt) // 2 + 1)) if k < 2 else None)

        def ssd_act(act, ph, c, x_group):
            n, g, o = unit0[ph], group0[ph], own0[ph]
            norm_act_squares(act, c, x_group)
            norm_act_high(act, c)
            split_high(act, n + 1)
            act.wait_ge(ssd_dt, 1)
            nc.scalar.activation(dtw[96:P, 2, :], dtw[96:P, 1, :], ACT.Exp, scale=-1.0).then_inc(ssd_e, 1)
            nc.scalar.activation(neg_a[96:P, :], a_log[96:P, :], ACT.Exp).then_inc(ssd_e, 1)
            act.wait_ge(ssd_tok, 2)
            nc.scalar.activation(dec_tok[:], dec_tok[:], ACT.Exp).then_inc(ssd_e, 1)
            nc.scalar.activation(cd_b[:], aux[:, 1, 0:P].rearrange("p (b h) -> p b h", b=TT), ACT.Exp).then_inc(ssd_e, 1)

            with act.Fori(0, SSD_G // 2) as i:
                for p in range(2):
                    gv, u, gg, adv, ga = 2 * i + p, n + 1 + 3 * p, g + 1 + 5 * p, 6 * i, 5 * i
                    k = 0

                    def did(ins):
                        nonlocal k
                        k += 1
                        ins.then_inc(s_act, 1)

                    split_high(act, u + 1, adv, 64 * i)
                    act.wait_ge(w_used, u + 1 + adv)
                    act.wait_ge(s_par, gv + 1)
                    act.wait_ge(ssd_y, 2 * gv)
                    for ct in range(2):
                        did(nc.scalar.activation(xg[:, ct, :], pair[gg % 2][:, ct, :], ACT.Identity,
                                                 bias=par[p][:, PAR_CB + ct:PAR_CB + ct + 1],
                                                 scale=par[p][:, PAR_CW + 12 + ct:PAR_CW + 12 + ct + 1]))
                    split_high(act, u + 2, adv, 64 * i)
                    read_out(act, gg, ga)
                    did(nc.scalar.activation(xg[:], xg[:], ACT.Silu))
                    act.wait_ge(w_used, u + 2 + adv)
                    act.wait_ge(own_done, o + 2 * gv)
                    for ct in range(2):
                        did(nc.scalar.activation(bc[:, ct, :], pair[(gg + 1) % 2][:, ct, :], ACT.Identity,
                                                 bias=par[p][:, PAR_CB + 2 + ct:PAR_CB + 3 + ct],
                                                 scale=par[p][:, PAR_CW + 14 + ct:PAR_CW + 15 + ct]))
                    split_high(act, u + 3, adv, 64 * i)
                    read_out(act, gg + 1, ga)
                    did(nc.scalar.activation(bc[:], bc[:], ACT.Silu))
                    act.wait_ge(w_used, u + 3 + adv)
                    nc.scalar.activation(zg[:], pair[(gg + 2) % 2][:], ACT.Silu).then_inc(evac[(gg + 2) % 2], 1)
                    k += 1
                    nc.scalar.copy(scrap[:], cst[:, 0:1]).then_inc(s_act, 1)
                    a = SSD_AUX * gv + SSD_AUX0
                    act.wait_ge(ssd_aux, a + 1)
                    did(nc.scalar.copy(b_tok[:], aux[:, 0, :]))
                    for r in range(4):
                        act.wait_ge(ssd_aux, a + 3 + r)
                        did(nc.scalar.activation(cs[:, r, :], aux[:, 2 + r % 2, :], ACT.Exp))
                        act.wait_ge(s_seg, 4 * gv + r + 1)
                        did(nc.scalar.activation(seg(r), seg(r), ACT.Exp))
                    act.wait_ge(s_yz, gv + 1)
                    did(nc.scalar.activation(tmp[:], xg[:], ACT.Square))
                    assert k == SSD_ACT
            n, g = n + 1 + 3 * SSD_G, g + 1 + 5 * SSD_G
            act.wait_ge(own_done, o + 2 * SSD_G)
            act.wait_ge(ssd_y, 2 * SSD_G)
            for k in range(8):
                nc.scalar.copy(y_hi[:, 2 * k:2 * k + 2, :], y_f[:, 2 * k:2 * k + 2, :]).then_inc(s_yhigh, 1)
            with act.Fori(0, 2) as i:
                for k in range(4):
                    split_high(act, n + k + 1, 4 * i)

        def ssd_vec(vec, ph, c, x_group):
            n, g, o = unit0[ph], group0[ph], own0[ph]
            vec.wait_ge(sq_used, c.sq + KT // 2)
            c.sq += KT // 2
            make_var(vec, c, aux[:, 3, 0:TT], TT, 1.0 / D)
            vec.wait_ge(rb_done, c.var)
            norm_tiles(vec, c, TAB_MIX + 8, range(KT))
            split_low(vec, n + 1)
            vec.wait_ge(ssd_aux, 1)
            nc.vector.tensor_copy(d_col[:], aux[:, 0, 0:16]).then_inc(ssd_d, 1)

            def own(ins):
                c.dv += 1
                ins.then_inc(dve, 1)
                vec.wait_ge(dve, c.dv)

            q = slice(96, P)
            vec.wait_ge(w_used, n + 1)
            own(nc.vector.tensor_scalar(dtw[q, 0, :], pair[g % 2][q, 0, :], dt_bias[q, :], None, ALU.add))
            nc.vector.scalar_tensor_tensor(dtw[q, 1, :], dtw[q, 0, :], -1.0, dtw[q, 0, :], ALU.mult, ALU.max).then_inc(ssd_dt, 1)
            own(nc.vector.tensor_scalar(dtw[q, 0, :], dtw[q, 0, :], 0.0, None, ALU.max))
            vec.wait_ge(ssd_e, 2)
            own(nc.vector.tensor_scalar(dtw[q, 1, :], dtw[q, 2, :], 2.0, None, ALU.add))
            own(nc.vector.reciprocal(dtw[q, 3, :], dtw[q, 1, :]))
            own(nc.vector.tensor_tensor(dtw[q, 1, :], dtw[q, 2, :], dtw[q, 3, :], ALU.mult))
            own(nc.vector.tensor_tensor(dtw[q, 2, :], dtw[q, 1, :], dtw[q, 1, :], ALU.mult))
            own(nc.vector.tensor_scalar(dtw[q, 3, :], dtw[q, 2, :], 1.0 / 17, None, ALU.mult))
            for odd in (15, 13, 11, 9, 7, 5, 3):
                own(nc.vector.scalar_tensor_tensor(dtw[q, 3, :], dtw[q, 3, :], 1.0 / odd, dtw[q, 2, :], ALU.add, ALU.mult))
            own(nc.vector.scalar_tensor_tensor(dtw[q, 3, :], dtw[q, 3, :], 1.0, dtw[q, 1, :], ALU.add, ALU.mult))
            own(nc.vector.scalar_tensor_tensor(dta[q, 0, :], dtw[q, 3, :], 2.0, dtw[q, 0, :], ALU.mult, ALU.add))
            own(nc.vector.tensor_scalar(neg_a[q, :], neg_a[q, :], -1.0, None, ALU.mult))
            own(nc.vector.tensor_scalar(dtw[q, 3, :], dta[q, 0, :], neg_a[q, :], None, ALU.mult))
            own(nc.vector.memset(dtw[q, 2, 0:P], 1.0))
            for b in range(TT):
                nc.vector.tensor_tensor_scan(dta[q, 1, b * P:(b + 1) * P], dtw[q, 2, 0:P], dtw[q, 3, b * P:(b + 1) * P],
                                             0.0, ALU.mult, ALU.add).then_inc(ssd_scan, 1)
            vec.wait_ge(ssd_scan, TT)
            nc.vector.tensor_copy(scrap_d[:], cst[:, 0:1]).then_inc(evac[g % 2], 1)
            vec.wait_ge(ssd_aux, 2)
            nc.vector.tensor_copy(dta_tok[:].rearrange("p q b h -> p (q b h)"), aux[:, 0, 0:2 * P]).then_inc(ssd_tok, 1)
            vec.wait_ge(ssd_aux, 3)
            vec.wait_ge(ssd_tok, 1)
            nc.vector.tensor_tensor(dec_tok[:], aux[:, 1, 0:P].rearrange("p (b h) -> p b h", b=TT), dta_tok[:, 1, :, :],
                                    ALU.subtract).then_inc(ssd_tok, 1)
            vec.wait_ge(ssd_e, 4)
            nc.vector.tensor_copy(scrap_d[:], cst[:, 0:1]).then_inc(ssd_dec, 1)

            v0 = c.dv
            with vec.Fori(0, SSD_G // 2) as i:
                for p in range(2):
                    gv, u, gg, adv, ga = 2 * i + p, n + 1 + 3 * p, g + 1 + 5 * p, 6 * i, 5 * i
                    k = 0

                    def step(ins, wait=True):
                        nonlocal k
                        k += 1
                        ins.then_inc(dve, 1)
                        if wait:
                            vec.wait_ge(dve, v0 + SSD_DVE * gv + k)

                    pr = par[p]
                    step(nc.vector.tensor_copy(pr[:, PAR_CW:PAR_CW + 16].rearrange("p (t c) -> p t c", t=4)[:, :, 0:2],
                                               tab[2][:].rearrange("p (t c) -> p t c", t=4)[:, :, ds(2 * gv, 2)]), False)
                    step(nc.vector.tensor_copy(pr[:, PAR_CW:PAR_CW + 16].rearrange("p (t c) -> p t c", t=4)[:, :, 2:4],
                                               tab[2][:].rearrange("p (t c q) -> p t c q", t=4, c=4)[:, :, 2:4, ds(gv, 1)].rearrange("p t c q -> p t (c q)")), False)
                    step(nc.vector.tensor_copy(pr[:, PAR_CB:PAR_CB + 2], tab[1][:, ds(TAB_CB + 2 * gv, 2)]), False)
                    step(nc.vector.tensor_copy(pr[:, PAR_CB + 2:PAR_CB + 3], tab[1][:, ds(TAB_CB + 16 + gv, 1)]), False)
                    step(nc.vector.tensor_copy(pr[:, PAR_CB + 3:PAR_CB + 4], tab[1][:, ds(TAB_CB + 24 + gv, 1)]), False)
                    step(nc.vector.tensor_copy(pr[:, PAR_D:PAR_D + 2], d_col[:, ds(2 * gv, 2)]), False)
                    step(nc.vector.tensor_copy(pr[:, PAR_G:PAR_G + 2], tab[1][:, ds(TAB_ON + 2 * gv, 2)]))
                    nc.vector.tensor_copy(pr[:, PAR_A:PAR_A + 16].rearrange("p (b r) -> p b r", b=TT),
                                          dta_tok[:, 1, :, ds(4 * gv, 4)]).then_inc(s_par, 1)
                    vec.wait_ge(s_par, gv + 1)
                    split_low(vec, u + 1, adv)

                    def conv(dst, src, tap_act, pc, last):
                        vec.wait_ge(s_act, SSD_ACT * gv + tap_act)
                        for back in range(1, 4):
                            for ct in range(2):
                                w = PAR_CW + 4 * (3 - back) + pc + ct
                                ins = nc.vector.scalar_tensor_tensor(dst[:, ct, back:S], src[:, ct, 0:S - back], pr[:, w:w + 1],
                                                                     dst[:, ct, back:S], ALU.mult, ALU.add)
                                if back == 3 and ct == 1:
                                    ins.then_inc(last, 1)
                                else:
                                    step(ins, ct == 1)

                    conv(xg, pair[gg % 2], 2, 0, evac[gg % 2])
                    split_low(vec, u + 2, adv)
                    conv(bc, pair[(gg + 1) % 2], 5, 2, evac[(gg + 1) % 2])
                    split_low(vec, u + 3, adv)
                    f = "p b (r c) -> p b r c"
                    vec.wait_ge(own_done, o + 2 * gv + 1)
                    px = pair[(gg + 3) % 2][:].rearrange("p a (b r c) -> p (a b) r c", b=2, r=4)
                    nc.vector.tensor_tensor(xdt[:].rearrange(f, r=4), px, spread64(dta_tok[:, 0, :, ds(4 * gv, 4)]),
                                            ALU.mult).then_inc(evac[(gg + 3) % 2], 1)
                    read_out(vec, gg + 3, ga)
                    nc.vector.tensor_tensor(xdd[:].rearrange(f, r=4), xdt[:].rearrange(f, r=4),
                                            spread64(dec_tok[:, :, ds(4 * gv, 4)]), ALU.mult).then_inc(s_xdd, 1)
                    a = SSD_AUX * gv + SSD_AUX0
                    vec.wait_ge(ssd_aux, a + 2)
                    nc.vector.tensor_tensor(cbm[:].rearrange("p (b l) -> p b l", b=TT), aux[:, 1, :].rearrange("p (b l) -> p b l", b=TT),
                                            cst[:, 2 * P:3 * P].rearrange("p (a l) -> p a l", a=1).broadcast_to((P, TT, P)),
                                            ALU.mult).then_inc(s_cb, 1)

                    def decays(r):
                        vec.wait_ge(s_act, SSD_ACT * gv + 9 + 2 * r)
                        for b in range(TT):
                            ins = nc.vector.tensor_scalar(seg(r)[:, b * P:(b + 1) * P], aux[:, 2 + r % 2, b * P:(b + 1) * P],
                                                          pr[:, PAR_A + 4 * b + r:PAR_A + 4 * b + r + 1], 0.0, ALU.subtract, ALU.min)
                        ins.then_inc(s_seg, 1)

                    def weights(r):
                        if r == 0:
                            vec.wait_ge(s_cb, gv + 1)
                        vec.wait_ge(s_act, SSD_ACT * gv + 10 + 2 * r)
                        nc.vector.tensor_tensor(seg(r), seg(r), cbm[:], ALU.mult).then_inc(s_m, 1)

                    decays(0)
                    decays(1)
                    weights(0)
                    decays(2)
                    weights(1)
                    decays(3)
                    weights(2)
                    weights(3)
                    vec.wait_ge(ssd_aux, a + 7)
                    step(nc.vector.tensor_copy(state[:, 0, :], aux[:, 0, 0:CW]))
                    for b in range(1, TT - 1):
                        sv = lambda m: state[:, m, :].rearrange("p (r c) -> p r c", r=4)
                        step(nc.vector.tensor_tensor(sv(b), sv(b - 1),
                                                     spread64(cd_b[:, b:b + 1, ds(4 * gv, 4)].rearrange("p b r -> p (b r)")), ALU.mult))
                        ins = nc.vector.tensor_tensor(state[:, b, :], aux[:, b // 2, (b % 2) * CW:(b % 2 + 1) * CW], state[:, b, :], ALU.add)
                        if b == TT - 2:
                            ins.then_inc(s_state, 1)
                        else:
                            step(ins)
                    vec.wait_ge(own_done, o + 2 * gv + 2)
                    for ct in range(2):
                        ins = nc.vector.scalar_tensor_tensor(xg[:, ct, :], xg[:, ct, :], pr[:, PAR_D + ct:PAR_D + ct + 1],
                                                             pair[(gg + 4) % 2][:, ct, :], ALU.mult, ALU.add)
                        if ct == 0:
                            step(ins, False)
                        else:
                            ins.then_inc(evac[(gg + 4) % 2], 1)
                    read_out(vec, gg + 4, ga)
                    read_out(vec, gg + 2, ga)
                    nc.vector.tensor_tensor(xg[:], xg[:], zg[:], ALU.mult).then_inc(s_yz, 1)
                    vec.wait_ge(ssd_aux, a + 8)
                    vec.wait_ge(rs_done, c.var + gv)
                    nc.vector.tensor_scalar(var[:, 0:TT], aux[:, 3, 0:TT], 1.0 / CW, EPS, ALU.mult, ALU.add).then_inc(var_done, 1)
                    vec.wait_ge(rb_done, c.var + 1 + gv)
                    for ct in range(2):
                        nc.vector.scalar_tensor_tensor(y_f[:, ds(2 * gv + ct, 1), :].rearrange("p a s -> p (a s)"), xg[:, ct, :],
                                                       pr[:, PAR_G + ct:PAR_G + ct + 1], aux[:, 2, :], ALU.mult, ALU.mult).then_inc(ssd_y, 1)
                    assert k == SSD_DVE, k
            c.var += SSD_G
            c.dv = v0 + SSD_DVE * SSD_G
            n, g = n + 1 + 3 * SSD_G, g + 1 + 5 * SSD_G
            for k in range(8):
                vec.wait_ge(s_yhigh, k + 1)
                if k == 0:
                    vec.wait_ge(ssd_y, 2 * SSD_G)
                nc.vector.tensor_tensor(y_lo[:, 2 * k:2 * k + 2, :], y_f[:, 2 * k:2 * k + 2, :],
                                        y_hi[:, 2 * k:2 * k + 2, :].bitcast(F32), ALU.subtract).then_inc(s_ylow, 1)
            with vec.Fori(0, 2) as i:
                for k in range(4):
                    split_low(vec, n + k + 1, 4 * i)
                    if k % 2 == 1:
                        vec.wait_ge(w_used, n + k + 1 + 4 * i)
                        add_residual(vec, g + k // 2, 2 * i + k // 2)

        def ssd_pool(pool, ph, c):
            pool_root(pool, c, TT)
            with pool.Fori(0, SSD_G // 2) as i:
                for p in range(2):
                    gv = 2 * i + p
                    for r in range(4):
                        pool.wait_ge(s_act, SSD_ACT * gv + 9 + 2 * r)
                        nc.gpsimd.tensor_tensor(cs[:, r, :], cs[:, r, :], bc[:, 1, :], ALU.mult).then_inc(s_c, 1)
                    pool.wait_ge(var_done, c.var + 1 + gv)
                    pool.wait_ge(rb_done, c.var + gv)
                    nc.gpsimd.tensor_tensor(rs[:, 0:TT], var[:, 0:TT], nh16[:, 0:TT], ALU.pow).then_inc(rs_done, 1)
            c.var += SSD_G

        STEPS = ([("qi", k, 2, None, True) for k in range(2)] + [("ki", 0, 1, TAB_DI, True)]
                 + [("q", k, 2, TAB_DQ, True) for k in range(4)] + [("k", k, 2, TAB_DK, True) for k in range(2)]
                 + [("v", 0, 0, None, False)])
        N_STEPS = len(STEPS)
        NORMED = [s_ for s_, st in enumerate(STEPS) if st[3] is not None]
        ROTATED = [s_ for s_, st in enumerate(STEPS) if st[4]]
        HEADS = [(b, h) for b in range(TT) for h in range(DH)]

        def made(s_):
            kind, k = STEPS[s_][0:2]
            return {"qi": qi, "ki": ki_w, "q": q_d, "k": k_d}[kind][:, 2 * k:2 * k + 2, :]

        def head_q(h):
            return slice(64 * (h % 2), 64 * (h % 2) + 64), h // 2

        def dsa_units(sp, ph):
            w, n = t["dsa_w_in"][0], unit0[ph]
            for s_, (kind, k, *_) in enumerate(STEPS):
                s = slot(n + s_)
                if kind == "ki":
                    parts = [(s[:, :, 0:64], cols(w, DSA_KI, 64)), (s[:, :, 64:P], cols(w, DSA_KI, 64)),
                             (s[:, :, P:CW], cols(w, DSA_IN - P, P))]
                elif kind == "k":
                    parts = [(s[:, :, 64 * q:64 * q + 64], cols(w, DSA_K + 64 * (2 * k + q // 2), 64)) for q in range(4)]
                else:
                    parts = [(s, cols(w, {"qi": DSA_QI, "q": 0, "v": DSA_V}[kind] + k * CW))]
                load_unit(sp, n + s_, parts)
            for k in range(4):
                load_unit(sp, n + N_STEPS + k, [(slot(n + N_STEPS + k), cols(t["dsa_w_out"][0], k * CW))])

        def dsa_pe(pe, ph, c, x_group):
            n, g, o = unit0[ph], group0[ph], own0[ph]
            norm_pe_sums(pe, c)
            spread(pe, c, 2)
            v0 = c.var
            for s_ in range(N_STEPS + 2):
                if s_ < N_STEPS:
                    ready = hn_ready(pe, ph - 1) if s_ == 0 else None
                    free_pair(pe, g + s_)
                    if STEPS[s_][0] == "v":
                        product_tok(pe, n + s_, g + s_, hn_hi, hn_lo, TT)
                    else:
                        product(pe, n + s_, g + s_, hn(hn_hi), hn(hn_lo), ready=ready)
                if s_ in NORMED:
                    k = NORMED.index(s_)
                    pe.wait_ge(d_sq, k + 1)
                    done = sum(r <= s_ - 3 for r in ROTATED)
                    if done:
                        pe.wait_ge(d_rope, done)
                    for i in range(STEPS[s_][2]):
                        for b in range(TT):
                            mm = nc.tensor.matmul(aux[:, 0, 4 * b + 2 * i:4 * b + 2 * i + 2], sq[k % 2][:, i, b * P:(b + 1) * P],
                                                  cst[:, 5 * P + 1:5 * P + 3], start=True, stop=True)
                    mm.then_inc(d_sum, 1)
                if STEPS[s_ - 2][4] if 2 <= s_ else False:
                    k = ROTATED.index(s_ - 2)
                    if s_ - 2 in NORMED:
                        pe.wait_ge(d_norm, NORMED.index(s_ - 2) + 1)
                    else:
                        read_out(pe, g + s_ - 2)
                    if k:
                        pe.wait_ge(d_rope, k)
                    pe.wait_ge(var_done, v0 + sum(r <= s_ for r in NORMED))
                    for i in range(STEPS[s_ - 2][2]):
                        mm = nc.tensor.matmul(aux[:, i, :], cst[:, 3 * P:4 * P], made(s_ - 2)[:, i, :], start=True, stop=True)
                    mm.then_inc(d_rot, 1)
                if s_ - 1 in NORMED:
                    k = NORMED.index(s_ - 1)
                    pe.wait_ge(rs_done, v0 + k + 1)
                    if k:
                        pe.wait_ge(d_norm, k)
                    else:
                        pe.wait_ge(hn_low, KT * ph)
                    for i in range(STEPS[s_ - 1][2]):
                        for b in range(TT):
                            for half in range(2):
                                col = rs[:, 4 * b + 2 * i + half:4 * b + 2 * i + half + 1].broadcast_to((P, 64))
                                mm = nc.tensor.matmul(aux[64 * half:64 * half + 64, 2 + i, b * P:(b + 1) * P], col, ident,
                                                      start=True, stop=True)
                    mm.then_inc(rb_done, 1)
            c.var += len(NORMED)
            gg = g + N_STEPS
            free_pair(pe, gg)
            for b in range(TT):
                mm = nc.tensor.transpose(pair[gg % 2][:, 0, b * P:(b + 1) * P], ki_w[:, 1, b * P:(b + 1) * P], ident)
            mm.then_inc(own_done, 1)
            pe.wait_ge(d_rope, len(ROTATED))
            k = 0
            for b in range(1, TT):
                for h in range(DI_H):
                    rows, ht = head_q(h)
                    if k >= 2:
                        pe.wait_ge(d_relu, k - 1)
                    nc.tensor.matmul(aux[:, k % 2, 0:(b + 1) * P], qi[rows, ht, b * P:(b + 1) * P], ki_w[rows, 0, 0:(b + 1) * P],
                                     start=True, stop=True).then_inc(d_logit, 1)
                    k += 1

            def scores(i):
                b, h = HEADS[i]
                rows, ht = head_q(h)
                if i >= 2:
                    pe.wait_ge(d_nb, i - 1)
                nc.tensor.matmul(aux[:, 2 + i % 2, 0:(b + 1) * P], q_d[rows, ht, b * P:(b + 1) * P], k_d[rows, h // 4, 0:(b + 1) * P],
                                 start=True, stop=True).then_inc(d_score, 1)

            def turn(i):
                b, h = HEADS[i]
                q = gg + 1 + i
                pe.wait_ge(d_prob, i + 1)
                free_pair(pe, q)
                for m in range(b + 1):
                    mm = nc.tensor.transpose(pair[q % 2][:, 0, m * P:(m + 1) * P], pr_d[i % 2][:, m * P:(m + 1) * P], ident)
                mm.then_inc(own_done, 1)

            def values(i):
                b, h = HEADS[i]
                rows, ht = head_q(h)
                read_out(pe, gg + 1 + i)
                if i == 0:
                    pe.wait_ge(d_relu, DI_H * (TT - 1))
                if i >= 4 and i % 2 == 0:
                    pe.wait_ge(d_olow, i // 2 - 1)
                for m in range(b + 1):
                    mm = nc.tensor.matmul(aux[rows, (i // 2) % 2, 0:P], v_d[:, m, 64 * (h // 4):64 * (h // 4) + 64],
                                          pt_d[i % 2][:, m * P:(m + 1) * P], start=m == 0, stop=m == b)
                mm.then_inc(d_out, 1)

            for i in range(len(HEADS) + 2):
                if i < len(HEADS):
                    scores(i)
                if 1 <= i <= len(HEADS):
                    turn(i - 1)
                if i >= 2:
                    values(i - 2)
            g2 = gg + 1 + len(HEADS)
            pe.wait_ge(d_olow, len(HEADS) // 2)
            for k in range(4):
                free_pair(pe, g2 + k)
                product(pe, n + N_STEPS + k, g2 + k, hn(hn_hi), hn(hn_lo))

        def dsa_act(act, ph, c, x_group):
            n, g, o = unit0[ph], group0[ph], own0[ph]
            norm_act_squares(act, c, x_group)
            norm_act_high(act, c)
            act.wait_ge(d_ang, 1)
            nc.scalar.activation(sin_t[:], ang[:, 0, :], ACT.Sin).then_inc(d_sin, 1)
            nc.scalar.activation(cos_t[:], ang[:, 1, :], ACT.Sin).then_inc(d_sin, 1)
            for s_ in range(N_STEPS):
                split_high(act, n + s_ + 1)
                if s_ in NORMED:
                    k = NORMED.index(s_)
                    read_out(act, g + s_)
                    if k >= 2:
                        act.wait_ge(d_sum, k - 1)
                    m = STEPS[s_][2]
                    nc.scalar.activation(sq[k % 2][:, 0:m, :], made(s_)[:, 0:m, :], ACT.Square).then_inc(d_sq, 1)
                if STEPS[s_][0] == "v":
                    act.wait_ge(w_used, n + s_ + 1)
                    nc.scalar.copy(v_d[:], pair[(g + s_) % 2][:].rearrange("p a (b m) -> p (a b) m", b=2)).then_inc(evac[(g + s_) % 2], 1)
            k = 0
            act.wait_ge(d_rope, len(ROTATED))
            for b in range(1, TT):
                for h in range(DI_H):
                    act.wait_ge(d_logit, k + 1)
                    if k >= 2:
                        act.wait_ge(d_acc, k - 1)
                    nc.scalar.activation(tmp[:, k % 2, 0:(b + 1) * P], aux[:, k % 2, 0:(b + 1) * P], ACT.Relu).then_inc(d_relu, 1)
                    k += 1
            gg = g + N_STEPS

            def exps(i):
                b, h = HEADS[i]
                act.wait_ge(d_nb, i + 1)
                nc.scalar.activation(pr_d[i % 2][:, 0:(b + 1) * P], pr_d[i % 2][:, 0:(b + 1) * P], ACT.Exp,
                                     bias=soft_d[:, i % 2, 1:2], scale=DSCALE, accum_out=soft_d[:, i % 2, 2:3]).then_inc(d_exp, 1)

            def copy_turned(i):
                b, h = HEADS[i]
                q = gg + 1 + i
                act.wait_ge(own_done, o + 2 + i)
                if i >= 2:
                    act.wait_ge(d_out, i - 1)
                nc.scalar.copy(pt_d[i % 2][:, 0:(b + 1) * P], pair[q % 2][:, 0, 0:(b + 1) * P]).then_inc(evac[q % 2], 1)

            def high(i):
                b, h = HEADS[i]
                act.wait_ge(d_out, i + 1)
                nc.scalar.copy(hn_hi[:, h // 2, b * P:(b + 1) * P], aux[:, (i // 2) % 2, 0:P]).then_inc(d_ohigh, 1)

            for i in range(len(HEADS) + 2):
                if i < len(HEADS):
                    exps(i)
                if 1 <= i <= len(HEADS):
                    copy_turned(i - 1)
                if i >= 2 and i % 2 == 1:
                    high(i - 2)
            for k in range(4):
                split_high(act, n + N_STEPS + k + 1)

        def dsa_vec(vec, ph, c, x_group):
            n, g, o = unit0[ph], group0[ph], own0[ph]
            vec.wait_ge(sq_used, c.sq + KT // 2)
            c.sq += KT // 2
            make_var(vec, c, aux[:, 3, 0:TT], TT, 1.0 / D)
            vec.wait_ge(rb_done, c.var)
            norm_tiles(vec, c, TAB_MIX + 16, range(KT))

            def own(ins):
                c.dv += 1
                ins.then_inc(dve, 1)
                vec.wait_ge(dve, c.dv)

            vec.wait_ge(pos_in, 16)
            own(nc.vector.tensor_copy(ang[:, 0, :], pos_i[:]))
            own(nc.vector.tensor_scalar(ang[:, 0, :], ang[:, 0, :], cst[:, 5 * P:5 * P + 1], None, ALU.mult))
            own(nc.vector.tensor_scalar(ang[:, 1, :], ang[:, 0, :], 1 / (2 * np.pi), ROUND, ALU.mult, ALU.add))
            own(nc.vector.tensor_scalar(ang[:, 1, :], ang[:, 1, :], ROUND, None, ALU.subtract))
            for part in (TURN1, TURN2, TURN3):
                own(nc.vector.scalar_tensor_tensor(ang[:, 0, :], ang[:, 1, :], -part, ang[:, 0, :], ALU.mult, ALU.add))
            own(nc.vector.tensor_scalar(ang[:, 0, :], ang[:, 0, :], -PI, PI, ALU.max, ALU.min))
            own(nc.vector.scalar_tensor_tensor(ang[:, 1, :], ang[:, 0, :], -1.0, ang[:, 0, :], ALU.mult, ALU.max))
            nc.vector.tensor_scalar(ang[:, 1, :], ang[:, 1, :], -1.0, np.pi / 2, ALU.mult, ALU.add).then_inc(d_ang, 1)

            v0 = c.var
            for s_ in range(N_STEPS + 2):
                if s_ < N_STEPS:
                    split_low(vec, n + s_ + 1)
                if s_ < N_STEPS and STEPS[s_][0] != "v":
                    vec.wait_ge(w_used, n + s_ + 1)
                    nc.vector.tensor_copy(made(s_), pair[(g + s_) % 2][:]).then_inc(evac[(g + s_) % 2], 1)
                if s_ in NORMED:
                    k = NORMED.index(s_)
                    width = 16
                    vec.wait_ge(d_sum, k + 1)
                    if STEPS[s_][2] == 1:
                        vec.wait_ge(rs_done, c.var)
                        nc.vector.tensor_scalar(var[:, 0:16].rearrange("p (b i) -> p b i", b=TT)[:, :, 0:2],
                                                aux[:, 0, 0:16].rearrange("p (b i) -> p b i", b=TT)[:, :, 0:2],
                                                1.0 / 64, EPS, ALU.mult, ALU.add).then_inc(var_done, 1)
                        c.var += 1
                    else:
                        make_var(vec, c, aux[:, 0, 0:width], width, 1.0 / 64)
                if 2 <= s_ and STEPS[s_ - 2][4]:
                    k, m = ROTATED.index(s_ - 2), STEPS[s_ - 2][2]
                    vec.wait_ge(d_rot, k + 1)
                    if k == 0:
                        vec.wait_ge(d_sin, 2)
                    own(nc.vector.tensor_tensor(tmp[:, 0:m, :], aux[:, 0:m, :], over_tiles(sin_t, m), ALU.mult))
                    vec.wait_ge(d_cos, k + 1)
                    nc.vector.tensor_tensor(made(s_ - 2)[:, 0:m, :], made(s_ - 2)[:, 0:m, :], tmp[:, 0:m, :], ALU.add).then_inc(d_rope, 1)
                    vec.wait_ge(d_rope, k + 1)
                if s_ - 1 in NORMED:
                    k, m, gain = NORMED.index(s_ - 1), STEPS[s_ - 1][2], STEPS[s_ - 1][3]
                    vec.wait_ge(rb_done, v0 + k + 1)
                    nc.vector.scalar_tensor_tensor(made(s_ - 1)[:, 0:m, :], made(s_ - 1)[:, 0:m, :], tab[1][:, gain:gain + 1],
                                                   aux[:, 2:2 + m, :], ALU.mult, ALU.mult).then_inc(d_norm, 1)
            gg = g + N_STEPS
            vec.wait_ge(own_done, o + 1)
            nc.vector.tensor_scalar(wi_tok[:], pair[gg % 2][:, 0, :].rearrange("p (b m) -> p b m", b=TT)[:, :, P - DI_H:P],
                                    DI_H ** -0.5 * 64 ** -0.5, None, ALU.mult).then_inc(evac[gg % 2], 1)
            read_out(vec, gg)
            own(nc.vector.memset(msk[:, 0, 0:P], 0.0))
            own(nc.vector.memset(msk[0:64, 0, 64:P], -HIDE))
            k = 0
            for b in range(1, TT):
                for h in range(DI_H):
                    vec.wait_ge(d_relu, k + 1)
                    a = msk[:, b, 0:(b + 1) * P]
                    if h == 0:
                        ins = nc.vector.tensor_scalar(a, tmp[:, k % 2, 0:(b + 1) * P], wi_tok[:, b, h:h + 1], None, ALU.mult)
                    else:
                        ins = nc.vector.scalar_tensor_tensor(a, tmp[:, k % 2, 0:(b + 1) * P], wi_tok[:, b, h:h + 1], a, ALU.mult, ALU.add)
                    ins.then_inc(d_acc, 1)
                    k += 1
                    vec.wait_ge(d_acc, k)
                own(nc.vector.memset(msk[0:64, b, (b + 1) * P - 64:(b + 1) * P], -OUT_OF_REACH))

            def top_round(b):
                a = msk[:, b, 0:(b + 1) * P]
                own(nc.vector.max(top8[:], a))
                own(nc.vector.match_replace(a, top8[:], a, -TAKEN))

            def scores(i):
                b, h = HEADS[i]
                w = (b + 1) * P
                vec.wait_ge(d_score, i + 1)
                if i >= 2:
                    vec.wait_ge(own_done, o + i)
                own(nc.vector.tensor_tensor_reduce(pr_d[i % 2][:, 0:w], aux[:, 2 + i % 2, 0:w], msk[:, b, 0:w], 1.0, -3e38,
                                                   ALU.add, ALU.max, soft_d[:, i % 2, 0:1]))
                nc.vector.tensor_scalar(soft_d[:, i % 2, 1:2], soft_d[:, i % 2, 0:1], -DSCALE, None, ALU.mult).then_inc(d_nb, 1)

            def inverse(i):
                vec.wait_ge(d_exp, i + 1)
                nc.vector.reciprocal(soft_d[:, i % 2, 3:4], soft_d[:, i % 2, 2:3]).then_inc(d_inv, 1)

            def low(i):
                b, h = HEADS[i]
                vec.wait_ge(d_ohigh, i // 2 + 1)
                nc.vector.tensor_tensor(hn_lo[:, h // 2, b * P:(b + 1) * P], aux[:, (i // 2) % 2, 0:P],
                                        hn_hi[:, h // 2, b * P:(b + 1) * P].bitcast(F32), ALU.subtract).then_inc(d_olow, 1)

            for i in range(len(HEADS) + 3):
                if i < len(HEADS):
                    scores(i)
                    b, h = HEADS[i]
                    if b + 1 < TT:
                        top_round(b + 1)
                        if h == DH - 1:
                            a = msk[:, b + 1, 0:(b + 2) * P]
                            own(nc.vector.tensor_scalar(a, a, -TAKEN, HIDE, ALU.is_equal, ALU.mult))
                            own(nc.vector.tensor_scalar(a, a, -HIDE, None, ALU.add))
                    inverse(i)
                if i >= 3 and i % 2 == 0:
                    low(i - 3)
            g2 = gg + 1 + len(HEADS)
            for k in range(4):
                split_low(vec, n + N_STEPS + k + 1)
                vec.wait_ge(w_used, n + N_STEPS + k + 1)
                add_residual(vec, g2 + k, k)

        def dsa_pool(pool, ph, c):
            pool.wait_ge(w_used, unit0[ph])
            pool.dma_start(pos_i[:], t["positions"].broadcast_to((P, S))).then_inc(pos_in, 16)
            pool_root(pool, c, TT)
            for s_ in range(N_STEPS + 2):
                if s_ in NORMED:
                    pool_root(pool, c, 16)
                if 2 <= s_ and STEPS[s_ - 2][4]:
                    k, m = ROTATED.index(s_ - 2), STEPS[s_ - 2][2]
                    pool.wait_ge(d_rot, k + 1)
                    if k == 0:
                        pool.wait_ge(d_sin, 2)
                    for i in range(m):
                        ins = nc.gpsimd.tensor_tensor(made(s_ - 2)[:, i, :], made(s_ - 2)[:, i, :], cos_t[:], ALU.mult)
                    ins.then_inc(d_cos, 1)
            for i, (b, h) in enumerate(HEADS):
                pool.wait_ge(d_inv, i + 1)
                nc.gpsimd.tensor_scalar(pr_d[i % 2][:, 0:(b + 1) * P], pr_d[i % 2][:, 0:(b + 1) * P], soft_d[:, i % 2, 3:4], None,
                                        ALU.mult).then_inc(d_prob, 1)

        def store_pe(pe, ph):
            g = group0[ph]
            for tt in range(TT):
                free_pair(pe, g)
                if tt == 0:
                    for k in range(4):
                        read_out(pe, g - 4 + k)
                for kt in range(KT):
                    mm = nc.tensor.transpose(pair[g % 2][:, kt // 4, (kt % 4) * P:(kt % 4 + 1) * P],
                                             x[:, kt, tt * P:(tt + 1) * P], ident)
                mm.then_inc(own_done, 1)
                g += 1

        def store_vec(vec, ph):
            g, o = group0[ph], own0[ph]
            for tt in range(TT):
                vec.wait_ge(own_done, o + tt + 1)
                nc.vector.tensor_copy(x_tok[:, tt, :].rearrange("p (a b) -> p a b", a=2), pair[g % 2][:]).then_inc(evac[g % 2], 1)
                g += 1

        def store_sync(sp, ph):
            g = group0[ph]
            ov = out.rearrange("a (t p) d -> (a p) t d", p=P)
            for tt in range(TT):
                read_out(sp, g + tt)
                sp.dma_start(ov[:, tt, :], x_tok[:, tt, :]).then_inc(stored, 16)
            sp.wait_ge(stored, 16 * TT)

        A_ADD = {"gmlp": 8, "ffn": 16}

        def a_base(ph):
            return sum(A_ADD.get(kind, 0) for kind, _ in phases[:ph])

        def x_group(ph):
            return group0[ph] - OUT_GROUPS if phases[ph - 1][0] != "load" else group0[ph - 1]

        block = ctx.enter_context(nc.Block())

        @block.sync
        def _(sp):
            load_sync(sp, 0)
            for ph, (kind, l) in enumerate(phases):
                if kind == "ffn":
                    ffn_units(sp, ph, l)
                elif kind == "xattn":
                    xattn_units(sp, ph, l)
                elif kind == "gmlp":
                    gmlp_units(sp, ph, l, l // 3)
                elif kind == "ssd":
                    ssd_units(sp, ph)
                elif kind == "dsa":
                    dsa_units(sp, ph)
            load_unit(sp, n_units, [(stage[n_units % 2][:, 0:16], t["ffn_w_up"][0][0:P, 0:16])])
            store_sync(sp, len(phases) - 1)

        @block.tensor
        def _(pe):
            c = Counts()
            for ph, (kind, l) in enumerate(phases):
                if kind == "load":
                    load_pe(pe, ph, c)
                elif kind == "ffn":
                    ffn_pe(pe, ph, l, c, x_group(ph))
                elif kind == "xattn":
                    xattn_pe(pe, ph, l, c, x_group(ph))
                elif kind == "gmlp":
                    gmlp_pe(pe, ph, l, l // 3, c, x_group(ph))
                elif kind == "ssd":
                    ssd_pe(pe, ph, c, x_group(ph))
                elif kind == "dsa":
                    dsa_pe(pe, ph, c, x_group(ph))
                elif kind == "store":
                    store_pe(pe, ph)

        @block.scalar
        def _(act):
            c = Counts()
            for ph, (kind, l) in enumerate(phases):
                if kind == "load":
                    load_act(act, ph, c)
                    split_high(act, 0)
                elif kind == "ffn":
                    ffn_act(act, ph, l, c, x_group(ph))
                elif kind == "xattn":
                    xattn_act(act, ph, l, c, x_group(ph))
                elif kind == "gmlp":
                    gmlp_act(act, ph, l, l // 3, c, x_group(ph))
                elif kind == "ssd":
                    ssd_act(act, ph, c, x_group(ph))
                elif kind == "dsa":
                    dsa_act(act, ph, c, x_group(ph))

        @block.vector
        def _(vec):
            c = Counts()
            for ph, (kind, l) in enumerate(phases):
                if kind == "load":
                    load_vec(vec, ph, c)
                    split_low(vec, 0)
                elif kind == "ffn":
                    ffn_vec(vec, ph, l, c, x_group(ph))
                elif kind == "xattn":
                    xattn_vec(vec, ph, l, c, x_group(ph))
                elif kind == "gmlp":
                    gmlp_vec(vec, ph, l, l // 3, c, x_group(ph))
                elif kind == "ssd":
                    ssd_vec(vec, ph, c, x_group(ph))
                elif kind == "dsa":
                    dsa_vec(vec, ph, c, x_group(ph))
                elif kind == "store":
                    store_vec(vec, ph)

        @block.gpsimd
        def _(pool):
            c = Counts()
            for ph, (kind, l) in enumerate(phases):
                if kind == "load":
                    load_pool(pool, ph, c)
                elif kind == "ffn":
                    ffn_pool(pool, ph, l, c)
                elif kind == "xattn":
                    xattn_pool(pool, ph, l, c)
                elif kind == "gmlp":
                    gmlp_pool(pool, ph, l, l // 3, c)
                elif kind == "ssd":
                    ssd_pool(pool, ph, c)
                elif kind == "dsa":
                    dsa_pool(pool, ph, c)


N_LOADS = 25
DSA_DMAS = {2: 3, 7: 4, 8: 4}


class Counts:

    def __init__(self):
        self.sq = self.var = self.hn = self.lo = self.mn = self.ml = self.dv = 0


class Tally:
    pass


_INS = ["x", "mem", "positions", "norm_mix", "gm_w_in", "gm_v_norm", "gm_w_s", "gm_b_s", "gm_w_out", "ssd_w_in",
        "ssd_conv_w", "ssd_conv_b", "ssd_dt_bias", "ssd_a_log", "ssd_d", "ssd_out_norm", "ssd_w_out", "dsa_w_in",
        "dsa_q_norm", "dsa_k_norm", "dsa_kidx_norm", "dsa_w_out", "norm_xa", "norm_mem", "xa_w_q", "xa_w_kv",
        "xa_q_norm", "xa_k_norm", "xa_w_out", "norm_ffn", "ffn_w_up", "ffn_w_down"]


def all_phases():
    phases = [("load", 0)]
    for l, kind in enumerate(LAYERS):
        phases += [(kind, l), ("xattn", l), ("ffn", l)]
    return phases + [("store", 0)]


def kernel(**inputs):
    import concourse.bacc as bacc
    from concourse.bass_utils import run_bass_kernel_spmd

    nc = bacc.Bacc("TRN2", target_bir_lowering=False, num_devices=1)
    arrays, t = {}, {}
    for name, a in [(name, np.ascontiguousarray(inputs[name])) for name in _INS] + [("constants", constants())]:
        arrays[f"in_{name}"] = a
        t[name] = nc.dram_tensor(f"in_{name}", a.shape, mybir.dt.from_np(a.dtype), kind="ExternalInput").ap()
    out = nc.dram_tensor("out_0", (1, S, D), F32, kind="ExternalOutput").ap()
    build(nc, t, out, all_phases())
    return run_bass_kernel_spmd(nc, [arrays], core_ids=[0]).results[0]["out_0"]
```

```python
from contextlib import ExitStack

import concourse.bass as bass
import numpy as np
from concourse import mybir

F32 = mybir.dt.float32
F32R = mybir.dt.float32r
I32 = mybir.dt.int32
ALU = mybir.AluOpType
ACT = mybir.ActivationFunctionType
AX = mybir.AxisListType.X
ds = bass.ds

P = 128
D = 1024
KT = D // P
S = 512
TT = S // P
MEM = 256
MT = MEM // P
EPS = 1e-6
DEPTH = 4
GM_HID = 2048
GM_G = 8
XH = 4
XSCALE = 128 ** -0.5
FFN = 4096
HALF = FFN // 2
HT = HALF // P
SSD_IN = 6176
SSD_XBC = 2048
SSD_DT = 6144
NHEAD = 32
UNIT = 2048
CW = 256

TAB_MIX, TAB_XA, TAB_MEM, TAB_FFN = 0, 32, 64, 96
TAB_VN, TAB_ON, TAB_CB, TAB_XQ, TAB_XK = 0, 32, 48, 80, 84
TAB_DQ, TAB_DK, TAB_DI = 88, 89, 90
TAB1_ROWS = 91

LAYERS = ("gmlp", "ssd", "dsa", "gmlp")

UNITS = {"load": 0, "gmlp": 24, "ssd": 33, "dsa": 14, "xattn": 8, "ffn": 32, "store": 0}
GROUPS = {"load": 6, "gmlp": 29, "ssd": 37, "dsa": 79, "xattn": 18, "ffn": 24, "store": 4}
OWN = {"load": 6, "gmlp": 9, "ssd": 8, "dsa": 65, "xattn": 8, "ffn": 0, "store": 4}
PRB = 4
DH = 16
DI_H = 8
DSCALE = 64 ** -0.5
DSA_IN = 2120
DSA_K, DSA_V, DSA_QI, DSA_KI = 1024, 1280, 1536, 2048
HIDE = 1e30
OUT_OF_REACH = 3.3e38
TAKEN = 3.4e38
PI = 3.1415925
ROUND = 12582912.0
TURN1 = 6.28125
TURN2 = 0.0019350051879882812
TURN3 = 2 * np.pi - TURN1 - TURN2
SSD_G = 8
SSD_ACT = 16
SSD_DVE = 23
PAR_STEPS = 7
SSD_AUX = 9
SSD_AUX0 = 3
PAR_CW, PAR_CB, PAR_A, PAR_D, PAR_G = 0, 16, 20, 36, 38
OUT_GROUPS = 4


def constants():
    c = np.zeros((P, 5 * P + 8), np.float32)
    c[:, 0:P] = np.eye(P)
    c[P - 1, P:2 * P] = 1.0
    t = np.arange(P)
    c[:, 2 * P:3 * P] = t[None, :] >= t[:, None]
    rot = np.zeros((P, P), np.float32)
    for h in (0, 64):
        for i in range(8):
            rot[h + 8 + i, h + i] = -1.0
            rot[h + i, h + 8 + i] = 1.0
    c[:, 3 * P:4 * P] = rot
    c[0, 4 * P:4 * P + 64] = 1.0
    c[1, 4 * P + 64:5 * P] = 1.0
    inv = (np.float32(500000.0) ** (-np.arange(8, dtype=np.float32) / np.float32(8))).astype(np.float32)
    for h in (0, 64):
        c[h:h + 8, 5 * P] = inv
        c[h + 8:h + 16, 5 * P] = inv
    c[0:64, 5 * P + 1] = 1.0
    c[64:128, 5 * P + 2] = 1.0
    c[:, 5 * P + 3] = 1.0
    c[:, 5 * P + 4:5 * P + 8] = -0.5
    return c


def build(nc, t, out, phases):
    unit0, group0, own0 = [], [], []
    u = g = o = 0
    mem_ph = 1 if phases[1][0] == "gmlp" else 0
    for ph, (kind, _) in enumerate(phases):
        unit0.append(u), group0.append(g), own0.append(o)
        more = 2 if ph == mem_ph else 0
        u, g, o = u + UNITS[kind], g + GROUPS[kind] + more, o + OWN[kind] + more
    n_units = u
    dma_count = [1] * (n_units + 2)
    for ph, (kind, _) in enumerate(phases):
        if kind == "ssd":
            for j in range(SSD_G):
                dma_count[unit0[ph] + 2 + 3 * j] = 2
        if kind == "dsa":
            for j, n in DSA_DMAS.items():
                dma_count[unit0[ph] + j] = n
    landed = []
    for n, c in enumerate(dma_count):
        landed.append(16 * c + (landed[n - 2] if n >= 2 else 0))

    with ExitStack() as ctx:
        top = [16512]

        def sb(name, shape, dt=F32, at=None):
            size = 4 * int(np.prod(shape[1:]))
            offset = top[0] if at is None else at
            if at is None:
                top[0] += (size + 31) // 32 * 32
            h = nc.alloc_sbuf_tensor_at(name, shape, dt, offset=offset)
            where[name] = offset
            return h

        where = {}

        def sem(name):
            return ctx.enter_context(nc.semaphore(name))

        x = sb("x_res", [P, KT, S])
        hn_hi = sb("hn_hi", [P, KT, S], F32R)
        hn_lo = sb("hn_lo", [P, KT, S], F32R)
        stage = [sb(f"stage{i}", [P, UNIT]) for i in range(2)]
        w_hi = [sb(f"w_hi{i}", [P, UNIT], F32R) for i in range(2)]
        w_lo = [sb(f"w_lo{i}", [P, UNIT], F32R) for i in range(2)]
        mem_hi = sb("mem_hi", [P, KT, MEM], F32R)
        mem_lo = sb("mem_lo", [P, KT, MEM], F32R)
        mem_tok = sb("mem_tok", [P, MT, D], at=where["mem_hi"])
        mem_raw = sb("mem_raw", [P, KT, MEM], at=where["mem_lo"])
        kv_at = top[0]
        k_t = sb("k_t", [P, XH, MEM])
        v_m = sb("v_m", [P, MT, 512])
        root_b = sb("root_b", [P, S], at=where["k_t"])
        late_sq_sum = sb("late_sq_sum", [P, S], at=where["k_t"] + 2048)[:]
        ws_t = sb("ws_t", [P, GM_G, P], at=where["k_t"])
        bs_b = sb("bs_b", [P, GM_G, P], at=where["v_m"])
        tmp = sb("tmp", [P, 2, S])
        sq_sum = tmp[:, 1, :]
        sq = [sb(f"sq{i}", [P, 2, S]) for i in range(2)]
        cst = sb("cst", [P, 5 * P + 8])
        tab = [sb("tab0", [P, P]), sb("tab1", [P, TAB1_ROWS]), sb("tab2", [P, P])]
        var = sb("var", [P, 16])
        rs = sb("rs", [P, 16])
        soft = sb("soft", [P, 2, 3, 4])
        rinv = sb("rinv", [P, 2, 4])
        tok_root = sb("tok_root", [P, 2, TT])
        q_ms = sb("q_ms", [P, 2, TT])
        q_scale = sb("q_scale", [P, XH, TT])
        nh16 = sb("nh16", [P, 16])
        big = top[0]
        top[0] += 65536
        a_log = sb("a_log", [P, 1])
        dt_bias = sb("dt_bias", [P, 1])
        neg_a = sb("neg_a", [P, 1])
        d_pair = sb("d_pair", [2, 16])
        d_col = sb("d_col", [P, 16])
        dta_tok = sb("dta_tok", [P, 2, TT, NHEAD])
        dec_tok = sb("dec_tok", [P, TT, NHEAD])
        cd_b = sb("cd_b", [P, TT, NHEAD])
        par = [sb(f"par{i}", [P, 40]) for i in range(2)]
        wi_tok = sb("wi_tok", [P, TT, DI_H])
        top8 = sb("top8", [P, 8])
        q_scale_d = sb("q_scale_d", [P, TT, DH])
        soft_d = sb("soft_d", [P, PRB, 4])
        scrap, scrap_d = sb("scrap", [P, 1]), sb("scrap_d", [P, 1])
        ident = cst[:, 0:P]
        ones = cst[:, 5 * P + 3:5 * P + 4]

        hid_hi = sb("hid_hi", [P, HT, S], F32R, at=big)
        hid_lo = sb("hid_lo", [P, HT, S], F32R, at=big + 32768)
        v_tok = sb("v_tok", [P, TT, GM_HID], at=big)
        uv_hi = sb("uv_hi", [P, TT, GM_HID], F32R, at=big)
        u_t = sb("u_t", [P, 16, S], at=big + 32768)
        uv_lo = sb("uv_lo", [P, 16, S], F32R, at=big + 32768)
        ws_raw = sb("ws_raw", [P, GM_G, P], at=big + 32768)
        square_a = sb("square_a", [P, GM_HID], at=big + 32768 + 8192)
        square_d = sb("square_d", [P, GM_HID], at=big + 32768 + 16384)
        q_raw = sb("q_raw", [P, XH, S], at=big)
        k_raw = sb("k_raw", [P, XH, MEM], at=big + 8192)
        prob = [sb(f"prob{i}", [P, TT, MEM], at=big + 12288 + 4096 * i) for i in range(2)]
        prob_t = [sb(f"prob_t{i}", [P, MT, S], at=big + 20480 + 4096 * i) for i in range(2)]
        o_hi = sb("o_hi", [P, XH, S], F32R, at=big + 28672)
        o_lo = sb("o_lo", [P, XH, S], F32R, at=big + 36864)
        y_f = sb("y_f", [P, 16, S], at=big)
        y_lo = sb("y_lo", [P, 16, S], F32R, at=big)
        y_hi = sb("y_hi", [P, 16, S], F32R, at=big + 32768)
        work = big + 32768
        xg = sb("xg", [P, 2, S], at=work)
        bc = sb("bc", [P, 2, S], at=work + 4096)
        zg = sb("zg", [P, 2, S], at=work + 8192)
        xdt = sb("xdt", [P, TT, CW], at=work + 12288)
        xdd = sb("xdd", [P, TT, CW], at=work + 16384)
        cs = sb("cs", [P, 4, S], at=work + 20480)
        dtw = sb("dtw", [P, 4, S], at=work)
        dta = sb("dta", [P, 2, S], at=work + 8192)
        b_tok = sb("b_tok", [P, S], at=kv_at)
        cbm = sb("cbm", [P, S], at=kv_at + 2048)
        state = sb("state", [P, 3, CW], at=kv_at + 4096)
        q_d = sb("q_d", [P, 8, S], at=big)
        k_d = sb("k_d", [P, 4, S], at=big + 16384)
        v_d = sb("v_d", [P, TT, CW], at=big + 24576)
        qi = sb("qi", [P, 4, S], at=big + 28672)
        ki_w = sb("ki_w", [P, 2, S], at=big + 36864)
        msk = sb("msk", [P, TT, S], at=big + 40960)
        pr_d = [sb(f"pr_d{i}", [P, S], at=big + (49152 if i < 2 else 53248) + 2048 * i) for i in range(PRB)]
        pt_d = [sb(f"pt_d{i}", [P, S], at=big + 53248 + 2048 * i) for i in range(2)]
        ang = sb("ang", [P, 2, S], at=big + 57344)
        pos_i = sb("pos_i", [P, S], I32, at=big + 61440)
        cos_t = sb("cos_t", [P, S], at=kv_at)
        sin_t = sb("sin_t", [P, S], at=kv_at + 2048)
        x_tok = sb("x_tok", [P, TT, D], at=big)
        tab_raw = [sb(f"tab_raw{i}", [P, P], at=big + 24576 + 512 * i) for i in range(3)]

        pair = [ctx.enter_context(nc.psum_tensor(f"pair{i}", [P, 2, S], F32)) for i in range(2)]
        aux = ctx.enter_context(nc.psum_tensor("aux", [P, 4, S], F32))

        mem_scratch = nc.dram_tensor("mem_scratch", [P, KT * MEM], F32, kind="Internal").ap()

        w_landed = [sem("w_landed0"), sem("w_landed1")]
        w_high = sem("w_high")
        w_low = sem("w_low")
        w_used = sem("w_used")
        own_done = sem("own_done")
        evac = [sem("evac0"), sem("evac1")]
        x_in, tab_in, par_in, mem_tok_in = sem("x_in"), sem("tab_in"), sem("par_in"), sem("mem_tok_in")
        stored = sem("stored")
        sq_done = sem("sq_done")
        sq_used = sem("sq_used")
        sq_added = sem("sq_added")
        var_done = sem("var_done")
        rs_done = sem("rs_done")
        rb_done = sem("rb_done")
        hn_t = sem("hn_t")
        hn_high = sem("hn_high")
        hn_low = sem("hn_low")
        mn_t, mn_high, mn_low = sem("mn_t"), sem("mn_high"), sem("mn_low")
        mem_in = sem("mem_in")
        mem_made = sem("mem_made")
        mem_kept = sem("mem_kept")
        a_sq = sem("a_sq")
        a_high = sem("a_high")
        a_low = sem("a_low")
        dve = sem("dve_chain")
        kn_done = sem("kn_done")
        score_done = sem("score_done")
        nb_done = sem("nb_done")
        exp_done = sem("exp_done")
        prob_done = sem("prob_done")
        o_high, o_low = sem("o_high"), sem("o_low")
        half_out = sem("half_out")
        ws_in = sem("ws_in")
        ws_ready = sem("ws_ready")
        vss_a, vss_d = sem("vss_a"), sem("vss_d")
        consts_set = sem("consts_set")
        ssd_aux = sem("ssd_aux")
        ssd_d, ssd_dt, ssd_e = sem("ssd_d"), sem("ssd_dt"), sem("ssd_e")
        ssd_scan, ssd_tok, ssd_dec = sem("ssd_scan"), sem("ssd_tok"), sem("ssd_dec")
        s_par = sem("s_par")
        s_act = sem("s_act")
        s_xdd, s_cb, s_seg, s_m, s_c = sem("s_xdd"), sem("s_cb"), sem("s_seg"), sem("s_m"), sem("s_c")
        s_state, s_yz, ssd_y = sem("s_state"), sem("s_yz"), sem("ssd_y")
        s_yhigh, s_ylow = sem("s_yhigh"), sem("s_ylow")

        pos_in = sem("pos_in")
        (d_sq, d_sum, d_norm,
         d_rot, d_cos, d_rope,
         d_ang, d_sin,
         d_logit, d_relu, d_acc,
         d_score, d_nb, d_exp, d_inv, d_prob,
         d_out, d_ohigh, d_olow) = [sem(x_) for x_ in (
             "d_sq", "d_sum", "d_norm", "d_rot", "d_cos", "d_rope", "d_ang", "d_sin", "d_logit", "d_relu", "d_acc",
             "d_score", "d_nb", "d_exp", "d_inv", "d_prob", "d_out", "d_ohigh", "d_olow")]

        def over_tiles(a, m):
            return a[:].rearrange("p (o s) -> p o s", o=1).broadcast_to((P, m, S))

        def seg(r):
            return sq[r // 2][:, r % 2, :]

        def spread64(a):
            shape = tuple(a.shape)
            names = " ".join("abcd"[:len(shape) - 1])
            return a.rearrange(f"{names} (e o) -> {names} e o", o=1).broadcast_to(shape + (64,))

        def repeat(eng, count, body, peel=False):
            if peel:
                body(0)
            with eng.Fori(1 if peel else 0, count) as i:
                body(i)

        def split_high(act, n, adv=0, dmas=None):
            act.wait_ge(w_landed[n % 2], landed[n] + (8 * adv if dmas is None else dmas))
            if n >= 2 or not isinstance(adv, int):
                act.wait_ge(w_used, n - 1 + adv)
            nc.scalar.copy(w_hi[n % 2][:], stage[n % 2][:]).then_inc(w_high, 1)

        def split_low(vec, n, adv=0):
            vec.wait_ge(w_high, n + 1 + adv)
            nc.vector.tensor_tensor(w_lo[n % 2][:], stage[n % 2][:], w_hi[n % 2][:].bitcast(F32),
                                    ALU.subtract).then_inc(w_low, 1)

        def load_unit(sp, n, dst_src, adv=0):
            if n >= 2 or not isinstance(adv, int):
                sp.wait_ge(w_low, n - 1 + adv)
            for dst, src in dst_src:
                sp.dma_start(dst, src).then_inc(w_landed[n % 2], 16)

        def cols(w, c0, width=CW, k0=0, kt=KT):
            return w[k0:k0 + kt * P, :].rearrange("(k p) m -> p k m", p=P)[:, :, ds(c0, width)]

        def slot(n, kt=KT, width=CW):
            return stage[n % 2][:, 0:kt * width].rearrange("p (k m) -> p k m", k=kt)

        def free_pair(pe, g, adv=0):
            if g >= 2:
                pe.wait_ge(evac[g % 2], g // 2 + adv)

        def read_out(eng, g, adv=0):
            eng.wait_ge(evac[g % 2], g // 2 + 1 + adv)

        def three(psum, hi_w, lo_w, hi_x, lo_x, first, last):
            nc.tensor.matmul(psum, hi_w, hi_x, start=first, stop=False, skip_group_check=True)
            nc.tensor.matmul(psum, hi_w, lo_x, start=False, stop=False, skip_group_check=True)
            return nc.tensor.matmul(psum, lo_w, hi_x, start=False, stop=last, skip_group_check=True)

        def unit_w(n, kt=KT, width=CW):
            f = "p (k m) -> p k m"
            return (w_hi[n % 2][:, 0:kt * width].rearrange(f, k=kt),
                    w_lo[n % 2][:, 0:kt * width].rearrange(f, k=kt))

        def product(pe, n, g, rhs_hi, rhs_lo, adv=0, first=True, last=True, ready=None, width=CW,
                    tokens=S, done=True):
            pe.wait_ge(w_low, n + 1 + adv)
            hi, lo = unit_w(n)
            for kt in range(KT):
                if ready:
                    ready(kt)
                for m in range(width // P):
                    c = slice(m * P, (m + 1) * P)
                    mm = three(pair[g % 2][:, m, 0:tokens], hi[:, kt, c], lo[:, kt, c], rhs_hi(kt), rhs_lo(kt),
                               first and kt == 0, last and kt == KT - 1)
            if done:
                mm.then_inc(w_used, 1)

        def product_tok(pe, n, g, x_hi, x_lo, tiles, adv=0, ready=None):
            pe.wait_ge(w_low, n + 1 + adv)
            hi, lo = unit_w(n)
            per = tiles // 2
            for kt in range(KT):
                if ready:
                    ready(kt)
                for tt in range(tiles):
                    po = pair[g % 2][:, tt // per, (tt % per) * CW:(tt % per + 1) * CW]
                    c = slice(tt * P, (tt + 1) * P)
                    mm = three(po, x_hi[:, kt, c], x_lo[:, kt, c], hi[:, kt, :], lo[:, kt, :],
                               kt == 0 and tt % per == 0, kt == KT - 1)
            mm.then_inc(w_used, 1)

        def norm_act_squares(act, c, x_group, steps=range(KT // 2)):
            for k in steps:
                read_out(act, x_group + k)
                if c.sq + k >= 2:
                    act.wait_ge(sq_used, c.sq + k - 1)
                nc.scalar.activation(sq[(c.sq + k) % 2][:], x[:, 2 * k:2 * k + 2, :], ACT.Square).then_inc(sq_done, 1)
            if len(steps) == KT // 2:
                c.sq += KT // 2

        def norm_pool_squares(pool, c, sq_sum=sq_sum):
            for k in range(KT // 2 - 1):
                pool.wait_ge(sq_done, c.sq + k + 1)
                s2 = sq[(c.sq + k) % 2]
                for i in range(1 if k == 0 else 0, 2):
                    first = s2[:, 0, :] if k == 0 else sq_sum
                    if k > 0:
                        pool.wait_ge(sq_added, c.ad)
                    ins = nc.gpsimd.tensor_tensor(sq_sum, first, s2[:, i, :], ALU.add)
                    if i == 0:
                        ins.then_inc(sq_added, 1)
                        c.ad += 1
                ins.then_inc(sq_used, 1)
                if k < KT // 2 - 2:
                    pool.wait_ge(sq_used, c.sq + k + 1)
            c.sq += KT // 2

        def norm_pe_sums(pe, c, sq_sum=sq_sum):
            pe.wait_ge(sq_used, c.sq + KT // 2 - 1)
            pe.wait_ge(sq_done, c.sq + KT // 2)
            last = sq[(c.sq + KT // 2 - 1) % 2]
            for i, part in enumerate((sq_sum, last[:, 0, :], last[:, 1, :])):
                for tt in range(TT):
                    mm = nc.tensor.matmul(aux[:, 3, tt:tt + 1], part[:, tt * P:(tt + 1) * P], ones,
                                          start=(i == 0 and tt == 0), stop=i == 2, skip_group_check=True)
            mm.then_inc(sq_used, 1)
            c.sq += KT // 2

        def make_var(vec, c, sums, width, scale, at=0):
            vec.wait_ge(rs_done, c.var)
            nc.vector.tensor_scalar(var[:, at:at + width], sums, scale, EPS, ALU.mult, ALU.add).then_inc(var_done, 1)
            c.var += 1

        def pool_root(pool, c, width, at=0):
            pool.wait_ge(var_done, c.var + 1)
            pool.wait_ge(rb_done, c.var)
            nc.gpsimd.tensor_tensor(rs[:, at:at + width], var[:, at:at + width], nh16[:, 0:width], ALU.pow).then_inc(rs_done, 1)
            c.var += 1

        def spread(pe, c, bank, col=0, step=1, tiles=TT, last=True, wait=True):
            if wait:
                pe.wait_ge(rs_done, c.var + 1)
            for tt in range(tiles):
                mm = nc.tensor.matmul(aux[:, bank, tt * P:(tt + 1) * P],
                                      rs[:, col + step * tt:col + step * tt + 1].broadcast_to((P, P)), ident,
                                      start=True, stop=True)
            if last:
                mm.then_inc(rb_done, 1)
                c.var += 1

        def norm_tiles(vec, c, gain, tiles):
            for kt in tiles:
                if c.hn >= 2:
                    vec.wait_ge(hn_low, c.hn - 1)
                nc.vector.scalar_tensor_tensor(tmp[:, kt % 2, :], x[:, kt, :], tab[0][:, gain + kt:gain + kt + 1],
                                               aux[:, 2, :], ALU.mult, ALU.mult).then_inc(hn_t, 1)
                c.hn += 1
                if kt > 0:
                    norm_low(vec, c, kt - 1)
                if kt == KT - 1:
                    norm_low(vec, c, kt)

        def norm_low(vec, c, kt):
            vec.wait_ge(hn_high, c.lo + 1)
            nc.vector.tensor_tensor(hn_lo[:, kt, :], tmp[:, kt % 2, :], hn_hi[:, kt, :].bitcast(F32),
                                    ALU.subtract).then_inc(hn_low, 1)
            c.lo += 1

        def norm_act_high(act, c, tiles=range(KT)):
            for kt in tiles:
                c.hn += 1
                act.wait_ge(hn_t, c.hn)
                nc.scalar.copy(hn_hi[:, kt, :], tmp[:, kt % 2, :]).then_inc(hn_high, 1)

        def hn_ready(pe, n):
            return lambda kt: pe.wait_ge(hn_low, KT * n + kt + 1)

        def hn(a):
            return lambda kt: a[:, kt, :]

        def add_residual(vec, g, k, adv=0):
            nc.vector.tensor_tensor(x[:, ds(2 * k, 2), :], pair[g % 2][:], x[:, ds(2 * k, 2), :],
                                    ALU.add).then_inc(evac[g % 2], 1)

        def mem_norm_vec(vec, c, l, tiles=range(KT)):
            if tiles[0] == 0 and l > 0:
                vec.wait_ge(mem_in, 16 * l)
            elif tiles[0] == 0:
                vec.wait_ge(mem_kept, 16)
            for k in tiles:
                if c.mn >= 2:
                    vec.wait_ge(mn_low, c.mn - 1)
                nc.vector.tensor_scalar(tmp_m(k), mem_raw[:, k, :], tab[0][:, TAB_MEM + 8 * l + k:TAB_MEM + 8 * l + k + 1],
                                        None, ALU.mult).then_inc(mn_t, 1)
                c.mn += 1
                if k > tiles[0]:
                    mem_low(vec, c, k - 1)
            mem_low(vec, c, tiles[-1])

        def tmp_m(k):
            return mem_tmp[:, k % 2, :]

        mem_tmp = sb("mem_tmp", [P, 2, MEM])

        def mem_low(vec, c, k):
            vec.wait_ge(mn_high, c.ml + 1)
            nc.vector.tensor_tensor(mem_lo[:, k, :], tmp_m(k), mem_hi[:, k, :].bitcast(F32), ALU.subtract).then_inc(mn_low, 1)
            c.ml += 1

        def mem_norm_act(act, c, tiles=range(KT)):
            for k in tiles:
                c.mn += 1
                act.wait_ge(mn_t, c.mn)
                nc.scalar.copy(mem_hi[:, k, :], tmp_m(k)).then_inc(mn_high, 1)

        def mem_norm_pool(pool, l, u_free):
            pool.wait_ge(w_used, u_free)
            pool.dma_start(mem_raw[:], mem_scratch.rearrange("p (k m) -> p k m", k=KT)).then_inc(mem_in, 16)


        def load_sync(sp, ph):
            sp.dma_start(cst[:], t["constants"]).then_inc(x_in, 16)
            xv = t["x"].rearrange("a (t p) d -> (a p) t d", p=P)
            for tt in range(TT):
                sp.dma_start(x_tok[:, tt, :], xv[:, tt, :]).then_inc(x_in, 16)
            for name, row in (("norm_mix", TAB_MIX), ("norm_xa", TAB_XA), ("norm_mem", TAB_MEM), ("norm_ffn", TAB_FFN)):
                sp.dma_start(tab_raw[0][row:row + 32, :], t[name].rearrange("l (k p) -> (l k) p", p=P)).then_inc(tab_in, 16)

        def load_params(act):
            n = 0

            def put(dst, src, **kw):
                nonlocal n
                act.dma_start(dst, src, **kw).then_inc(par_in, 16)
                n += 1
            put(tab_raw[1][TAB_VN:TAB_VN + 32, :], t["gm_v_norm"].rearrange("l (k p) -> (l k) p", p=P))
            put(tab_raw[1][TAB_ON:TAB_ON + 16, :], t["ssd_out_norm"].rearrange("l (k p) -> (l k) p", p=P))
            put(tab_raw[1][TAB_CB:TAB_CB + 32, :], t["ssd_conv_b"].rearrange("l (k p) -> (l k) p", p=P))
            put(tab_raw[1][TAB_XQ:TAB_XQ + 4, :], t["xa_q_norm"])
            put(tab_raw[1][TAB_XK:TAB_XK + 4, :], t["xa_k_norm"])
            for row, name in ((TAB_DQ, "dsa_q_norm"), (TAB_DK, "dsa_k_norm"), (TAB_DI, "dsa_kidx_norm")):
                for h in (0, 64):
                    put(tab_raw[1][row:row + 1, h:h + 64], t[name])
            put(a_log[96:P, :], t["ssd_a_log"].rearrange("a h -> h a"))
            put(dt_bias[96:P, :], t["ssd_dt_bias"].rearrange("a h -> h a"))
            put(d_pair[:], t["ssd_d"].rearrange("a (j h) -> (a h) j", h=2), allow_slow_non_contiguous=True)
            put(tab_raw[2][:], t["ssd_conv_w"].rearrange("l c (k p) -> (l c k) p", p=P))
            assert n == N_PARAMS

        def load_pe(pe, ph, c):
            g = group0[ph]
            pe.wait_ge(x_in, 16 * (1 + TT))
            for k in range(0, KT, 2):
                free_pair(pe, g)
                for i in range(2):
                    for tt in range(TT):
                        mm = nc.tensor.transpose(pair[g % 2][:, i, tt * P:(tt + 1) * P],
                                                 x_tok[:, tt, (k + i) * P:(k + i + 1) * P], ident)
                mm.then_inc(own_done, 1)
                g += 1
            free_pair(pe, g)
            pe.wait_ge(tab_in, 16 * 4)
            nc.tensor.transpose(pair[g % 2][:, 0, 0:P], tab_raw[0][:], ident).then_inc(own_done, 1)
            g += 1
            free_pair(pe, g)
            pe.wait_ge(par_in, 16 * N_PARAMS)
            nc.tensor.transpose(pair[g % 2][:, 0, 0:TAB1_ROWS], tab_raw[1][0:TAB1_ROWS, :],
                                cst[0:TAB1_ROWS, 0:TAB1_ROWS])
            nc.tensor.transpose(pair[g % 2][:, 1, 0:P], tab_raw[2][:], ident).then_inc(own_done, 1)

        def load_vec(vec, ph, c):
            g, o = group0[ph], own0[ph]
            for k in range(0, KT, 2):
                vec.wait_ge(own_done, o + k // 2 + 1)
                nc.vector.tensor_copy(x[:, k:k + 2, :], pair[g % 2][:]).then_inc(evac[g % 2], 1)
                g += 1
            vec.wait_ge(own_done, o + 5)
            nc.vector.tensor_copy(tab[0][:], pair[g % 2][:, 0, 0:P]).then_inc(evac[g % 2], 1)
            g += 1
            vec.wait_ge(own_done, o + 6)
            nc.vector.tensor_copy(tab[1][:], pair[g % 2][:, 0, 0:TAB1_ROWS])
            nc.vector.tensor_copy(tab[2][:], pair[g % 2][:, 1, 0:P]).then_inc(evac[g % 2], 1)
            read_out(vec, g)
            nc.vector.tensor_tensor(tab[1][:, TAB_XK:TAB_XK + DEPTH], tab[1][:, TAB_XK:TAB_XK + DEPTH],
                                    tab[1][:, TAB_XQ:TAB_XQ + DEPTH], ALU.mult).then_inc(dve, 1)
            c.dv += 1
            vec.wait_ge(dve, c.dv)
            vec.wait_ge(consts_set, 2)

        def load_pool(pool, ph, c):
            nc.gpsimd.memset(var[:], 1.0).then_inc(consts_set, 1)
            nc.gpsimd.memset(nh16[:], -0.5).then_inc(consts_set, 1)
            pool.wait_ge(consts_set, 2)
            pool.wait_ge(x_in, 16 * (1 + TT))
            pool.dma_start(mem_tok[:], t["mem"].rearrange("a (t p) d -> (a p) t d", p=P)).then_inc(mem_tok_in, 16)

        def mem_pe_turn(pe, g):
            pe.wait_ge(mem_tok_in, 16)
            for k in range(0, KT, 4):
                free_pair(pe, g)
                for i in range(4):
                    for tt in range(MT):
                        mm = nc.tensor.transpose(pair[g % 2][:, i // 2, (i % 2) * MEM + tt * P:(i % 2) * MEM + (tt + 1) * P],
                                                 mem_tok[:, tt, (k + i) * P:(k + i + 1) * P], ident)
                mm.then_inc(own_done, 1)
                g += 1

        def mem_pe_sums(pe, c):
            for k in range(KT // 2):
                pe.wait_ge(sq_done, c.sq + k + 1)
                for i in range(2):
                    for tt in range(MT):
                        mm = nc.tensor.matmul(aux[:, 3, tt:tt + 1], sq[(c.sq + k) % 2][:, i, tt * P:(tt + 1) * P], ones,
                                              start=(k == 0 and i == 0 and tt == 0), stop=(k == KT // 2 - 1 and i == 1),
                                              skip_group_check=True)
                mm.then_inc(sq_used, 1)
            c.sq += KT // 2

        def mem_act_squares(act, c, g):
            for k in range(KT // 2):
                read_out(act, g + k // 2)
                if c.sq + k >= 2:
                    act.wait_ge(sq_used, c.sq + k - 1)
                nc.scalar.activation(sq[(c.sq + k) % 2][:, :, 0:MEM], mem_raw[:, 2 * k:2 * k + 2, :],
                                     ACT.Square).then_inc(sq_done, 1)
            c.sq += KT // 2

        def mem_vec_copy(vec, g, o):
            for k in range(0, KT, 4):
                vec.wait_ge(own_done, o + k // 4 + 1)
                nc.vector.tensor_copy(mem_raw[:, k:k + 4, :].rearrange("p (a b) m -> p a (b m)", a=2),
                                      pair[g % 2][:]).then_inc(evac[g % 2], 1)
                g += 1

        def mem_vec_var(vec, c):
            vec.wait_ge(sq_used, c.sq + KT // 2)
            c.sq += KT // 2
            make_var(vec, c, aux[:, 3, 0:MT], MT, 1.0 / D)

        def mem_vec_scale(vec, var_count):
            vec.wait_ge(rb_done, var_count)
            for k in range(KT):
                ins = nc.vector.tensor_tensor(mem_raw[:, k, :], mem_raw[:, k, :], aux[:, 2, 0:MEM], ALU.mult)
            ins.then_inc(mem_made, 1)

        def mem_pool(pool, c):
            c.sq += KT // 2
            pool_root(pool, c, MT)
            pool.wait_ge(mem_made, 1)
            pool.dma_start(mem_scratch.rearrange("p (k m) -> p k m", k=KT), mem_raw[:]).then_inc(mem_kept, 16)
            pool.wait_ge(mem_kept, 16)

        def raw_tiles(vec, c, gains, x_group, tiles):
            read_out(vec, x_group + tiles[-1] // 2)
            for kt in tiles:
                if c.hn >= 2:
                    vec.wait_ge(hn_low, c.hn - 1)
                gain = gains + kt
                nc.vector.tensor_scalar(tmp[:, kt % 2, :], x[:, kt, :], tab[0][:, gain:gain + 1], None, ALU.mult).then_inc(hn_t, 1)
                c.hn += 1
                if kt > tiles[0]:
                    norm_low(vec, c, kt - 1)
            norm_low(vec, c, tiles[-1])

        def ffn_units(sp, ph, l):
            up, down = t["ffn_w_up"][l], t["ffn_w_down"][l]
            n0 = unit0[ph]
            for half in range(2):
                def up_units(i):
                    for j in range(2):
                        load_unit(sp, n0 + j, [(slot(j + n0), cols(up, half * HALF + (2 * i + j) * CW))], 2 * i)

                repeat(sp, 4, up_units, n0 == 0)
                n0 += 8
                with sp.Fori(0, 2) as i:
                    for j in range(4):
                        load_unit(sp, n0 + j, [(slot(j + n0), cols(down, (2 * i + j // 2) * CW, k0=half * HALF + (j % 2) * D))],
                                  4 * i)
                n0 += 8

        def ffn_pe(pe, ph, l, c, x_group):
            n, g = unit0[ph], group0[ph]
            free_pair(pe, g)
            product(pe, n, g, hn(hn_hi), hn(hn_lo), ready=hn_ready(pe, ph - 1))
            norm_pe_sums(pe, c, late_sq_sum)
            free_pair(pe, g + 1)
            product(pe, n + 1, g + 1, hn(hn_hi), hn(hn_lo), ready=lambda kt: kt == 2 and spread(pe, c, 2))
            for half in range(2):
                with pe.Fori(1 - half, 4) as i:
                    for j in range(2):
                        free_pair(pe, g + j, i)
                        product(pe, n + j, g + j, hn(hn_hi), hn(hn_lo), 2 * i)
                n, g = n + 8, g + 8
                a0 = a_base(ph) + 8 * half
                with pe.Fori(0, 2) as i:
                    for j in range(4):
                        if j % 2 == 0:
                            free_pair(pe, g + j // 2, i)
                        first = j == 0
                        product(pe, n + j, g + j // 2, lambda kt, j=j: hid_hi[:, 8 * (j % 2) + kt, :],
                                lambda kt, j=j: hid_lo[:, 8 * (j % 2) + kt, :], 4 * i, first=j % 2 == 0, last=j % 2 == 1,
                                ready=(lambda kt, j=j, a0=a0: pe.wait_ge(a_low, a0 + (8 * j + kt) // 2 + 1)) if j < 2 else None)
                n, g = n + 8, g + 4

        def ffn_act(act, ph, l, c, x_group):
            for k in range(KT // 2):
                norm_act_squares(act, c, x_group, [k])
                norm_act_high(act, c, range(2 * k, 2 * k + 2))
            c.sq += KT // 2
            n, g = unit0[ph], group0[ph]
            for half in range(2):
                a0 = a_base(ph) + 8 * half
                def up(i):
                    for j in range(2):
                        split_high(act, n + j + 1, 2 * i)
                        read_out(act, g + j, i)
                        nc.scalar.activation(tmp[:], tmp[:], ACT.Square).then_inc(a_sq, 1)
                        act.wait_ge(a_sq, a0 + j + 1 + 2 * i)
                        nc.scalar.copy(hid_hi[:, ds(4 * i + 2 * j, 2), :], tmp[:]).then_inc(a_high, 1)

                repeat(act, 4, up, n == 0)
                n, g = n + 8, g + 8
                if l + 1 < DEPTH:
                    mem_norm_act(act, c, MEM_PARTS[2 * half])
                with act.Fori(0, 2) as i:
                    for j in range(4):
                        split_high(act, n + j + 1, 4 * i)
                if half == 0 and l + 1 < DEPTH:
                    mem_norm_act(act, c, MEM_PARTS[1])
                n, g = n + 8, g + 4

        def ffn_vec(vec, ph, l, c, x_group):
            n, g = unit0[ph], group0[ph]
            split_low(vec, n + 1)
            vec.wait_ge(sq_used, c.sq + KT // 2)
            c.sq += KT // 2
            make_var(vec, c, aux[:, 3, 0:TT], TT, 1.0 / D)
            vec.wait_ge(rb_done, c.var)
            nc.vector.tensor_copy(root_b[:], aux[:, 2, :]).then_inc(dve, 1)
            c.dv += 1
            vec.wait_ge(dve, c.dv)
            for half in range(2):
                a0 = a_base(ph) + 8 * half

                def up(i):
                    for j in range(2):
                        if not (isinstance(i, int) and j == 0):
                            split_low(vec, n + j + 1, 2 * i)
                        vec.wait_ge(w_used, n + j + 1 + 2 * i)
                        if a0 + j > 0 or not isinstance(i, int):
                            vec.wait_ge(a_low, a0 + j + 2 * i)
                        nc.vector.scalar_tensor_tensor(tmp[:], pair[(g + j) % 2][:], 0.0, over_tiles(root_b, 2), ALU.max,
                                                       ALU.mult).then_inc(evac[(g + j) % 2], 1)
                        vec.wait_ge(a_high, a0 + j + 1 + 2 * i)
                        nc.vector.tensor_tensor(hid_lo[:, ds(4 * i + 2 * j, 2), :], tmp[:],
                                                hid_hi[:, ds(4 * i + 2 * j, 2), :].bitcast(F32),
                                                ALU.subtract).then_inc(a_low, 1)

                if half == 0:
                    up(0)
                with vec.Fori(1 - half, 4) as i:
                    up(i)
                n, g = n + 8, g + 8
                if l + 1 < DEPTH:
                    mem_norm_vec(vec, c, l + 1, MEM_PARTS[2 * half])
                with vec.Fori(0, 2) as i:
                    for j in range(4):
                        split_low(vec, n + j + 1, 4 * i)
                        if j % 2 == 1:
                            vec.wait_ge(w_used, n + j + 1 + 4 * i)
                            if half == 1:
                                read_out(vec, g - 12 + j // 2, i)
                            add_residual(vec, g + j // 2, 2 * i + j // 2)
                if half == 0 and l + 1 < DEPTH:
                    mem_norm_vec(vec, c, l + 1, MEM_PARTS[1])
                n, g = n + 8, g + 4

        def ffn_pool(pool, ph, l, c):
            norm_pool_squares(pool, c, late_sq_sum)
            pool_root(pool, c, TT)
            if l + 1 < DEPTH:
                mem_norm_pool(pool, l + 1, unit0[ph])

        TURNED, VALUED = (0, 1, 3, 5), (2, 4, 6, 7)
        def xattn_units(sp, ph, l):
            n = unit0[ph]
            w_q, w_kv = t["xa_w_q"][l], t["xa_w_kv"][l]
            for j, (w, c0) in enumerate([(w_kv, 0), (w_kv, CW), (w_kv, 512), (w_q, 0), (w_q, CW), (w_kv, 512 + CW)]):
                load_unit(sp, n + j, [(slot(n + j), cols(w, c0))])
            for j in range(2):
                load_unit(sp, n + 6 + j, [(slot(n + j, 4, 512), cols(t["xa_w_out"][l], j * 512, 512, kt=4))])

        def xattn_pe(pe, ph, l, c, x_group):
            n, g = unit0[ph], group0[ph]
            mem_ready = lambda kt: pe.wait_ge(mn_low, KT * l + kt + 1)
            mem_h, mem_l = (lambda kt: mem_hi[:, kt, :]), (lambda kt: mem_lo[:, kt, :])
            free_pair(pe, g)
            product(pe, n, g, mem_h, mem_l, ready=mem_ready, tokens=MEM)
            free_pair(pe, g + 1)
            product(pe, n + 1, g + 1, mem_h, mem_l, tokens=MEM)
            norm_pe_sums(pe, c, late_sq_sum)
            c.var += 1
            free_pair(pe, g + 2)
            product_tok(pe, n + 2, g + 2, mem_hi, mem_lo, MT)
            def query_sums(j):
                pe.wait_ge(sq_done, c.sq + 1)
                for i in range(2):
                    for tt in range(TT):
                        col = TT * (2 * j + i) + tt
                        mm = nc.tensor.matmul(aux[:, 3, col:col + 1], sq[c.sq % 2][:, i, tt * P:(tt + 1) * P], ones,
                                              start=True, stop=True)
                mm.then_inc(sq_used, 1)
                c.sq += 1

            free_pair(pe, g + 3)
            product(pe, n + 3, g + 3, hn(hn_hi), hn(hn_lo), ready=hn_ready(pe, ph - 1))
            for h in range(0, XH, 2):
                pe.wait_ge(sq_done, c.sq + 1)
                for i in range(2):
                    for tt in range(MT):
                        mm = nc.tensor.matmul(aux[:, 0, XH * tt + h + i:XH * tt + h + i + 1],
                                              sq[c.sq % 2][:, i, tt * P:(tt + 1) * P], ones, start=True, stop=True)
                mm.then_inc(sq_used, 1)
                c.sq += 1
            def amid_queries(kt):
                if kt == 2:
                    pe.wait_ge(rs_done, c.var + 1)
                    for h in range(XH):
                        for tt in range(MT):
                            col = XH * tt + h
                            mm = nc.tensor.matmul(aux[:, h // 2, (h % 2) * MEM + tt * P:(h % 2) * MEM + (tt + 1) * P],
                                                  rs[:, col:col + 1].broadcast_to((P, P)), ident, start=True, stop=True)
                    mm.then_inc(rb_done, 1)
                    c.var += 1
                if kt == 5:
                    query_sums(0)

            free_pair(pe, g + 4)
            product(pe, n + 4, g + 4, hn(hn_hi), hn(hn_lo), ready=amid_queries)
            pg = g + 6

            def scores(h):
                if h == 0:
                    pe.wait_ge(kn_done, XH * (l + 1))
                if h % 2 == 0:
                    read_out(pe, g + 3 + h // 2)
                if h == 1:
                    c.var += 2
                    pe.wait_ge(var_done, c.var)
                if h >= 2:
                    pe.wait_ge(exp_done, TT * (XH * l + h - 1))
                for tt in range(TT):
                    mm = nc.tensor.matmul(aux[:, 2 * (h % 2) + tt // 2, (tt % 2) * MEM:(tt % 2 + 1) * MEM],
                                          q_raw[:, h, tt * P:(tt + 1) * P], k_t[:, h, :], start=True, stop=True)
                mm.then_inc(score_done, 1)

            def turn(h):
                gg = pg + TURNED[h]
                pe.wait_ge(prob_done, XH * l + h + 1)
                free_pair(pe, gg)
                for m in range(MT):
                    for tt in range(TT):
                        mm = nc.tensor.transpose(pair[gg % 2][:, m, tt * P:(tt + 1) * P],
                                                 prob[h % 2][:, tt, m * P:(m + 1) * P], ident)
                mm.then_inc(own_done, 1)

            def values(h):
                gg = pg + VALUED[h]
                read_out(pe, pg + TURNED[h])
                free_pair(pe, gg)
                for m in range(MT):
                    mm = nc.tensor.matmul(pair[gg % 2][:, 0, :], v_m[:, m, h * P:(h + 1) * P], prob_t[h % 2][:, m, :],
                                          start=m == 0, stop=m == MT - 1)
                mm.then_inc(own_done, 1)

            scores(0)
            query_sums(1)
            scores(1)
            free_pair(pe, g + 5)
            product_tok(pe, n + 5, g + 5, mem_hi, mem_lo, MT)
            turn(0)
            scores(2)
            turn(1)
            values(0)
            scores(3)
            for h in range(2, XH):
                turn(h)
                values(h - 1)
            values(XH - 1)
            for j in range(2):
                pe.wait_ge(w_low, n + 6 + j + 1)
                hi, lo = unit_w(n + j, 4, 512)
                for half in range(2):
                    gg = g + 14 + 2 * j + half
                    free_pair(pe, gg)
                    for kt in range(XH):
                        pe.wait_ge(o_low, XH * l + kt + 1)
                        for m in range(2):
                            cc = slice((2 * half + m) * P, (2 * half + m + 1) * P)
                            mm = three(pair[gg % 2][:, m, :], hi[:, kt, cc], lo[:, kt, cc], o_hi[:, kt, :], o_lo[:, kt, :],
                                       kt == 0, kt == XH - 1)
                    mm.then_inc(w_used if half else half_out, 1)

        def xattn_act(act, ph, l, c, x_group):
            n, g = unit0[ph], group0[ph]

            def raw_keys(j):
                act.wait_ge(w_used, n + 1 + j)
                nc.scalar.copy(k_raw[:, 2 * j:2 * j + 2, :], pair[(g + j) % 2][:, :, 0:MEM]).then_inc(evac[(g + j) % 2], 1)

            split_high(act, n + 1)
            for k in range(KT // 2):
                norm_act_squares(act, c, x_group, [k])
                if k < 2:
                    norm_act_high(act, c, range(2 * k, 2 * k + 2))
            c.sq += KT // 2
            split_high(act, n + 2)
            raw_keys(0)
            norm_act_high(act, c, range(4, KT))
            split_high(act, n + 3)
            raw_keys(1)
            for j in range(2):
                read_out(act, g + j)
                act.wait_ge(sq_used, c.sq - 1)
                nc.scalar.activation(sq[c.sq % 2][:, :, 0:MEM], k_raw[:, 2 * j:2 * j + 2, :], ACT.Square).then_inc(sq_done, 1)
                c.sq += 1

            def values_out(j, unit):
                act.wait_ge(w_used, n + unit + 1)
                nc.scalar.copy(v_m[:, :, j * CW:(j + 1) * CW], pair[(g + unit) % 2][:, :, 0:CW]).then_inc(evac[(g + unit) % 2], 1)

            def query_squares(j):
                read_out(act, g + 3 + j)
                act.wait_ge(sq_used, c.sq - 1)
                nc.scalar.activation(sq[c.sq % 2][:], q_raw[:, 2 * j:2 * j + 2, :], ACT.Square).then_inc(sq_done, 1)
                c.sq += 1

            values_out(0, 2)
            split_high(act, n + 4)
            query_squares(0)
            split_high(act, n + 5)
            query_squares(1)

            def exps(h):
                act.wait_ge(nb_done, XH * l + h + 1)
                if h >= 2:
                    act.wait_ge(own_done, own0[ph] + TURNED[h - 2] + 1)
                for tt in range(TT):
                    nc.scalar.activation(prob[h % 2][:, tt, :], aux[:, 2 * (h % 2) + tt // 2, (tt % 2) * MEM:(tt % 2 + 1) * MEM],
                                         ACT.Exp, bias=soft[:, h % 2, 1, tt:tt + 1], scale=q_scale[:, h, tt:tt + 1],
                                         accum_out=soft[:, h % 2, 2, tt:tt + 1]).then_inc(exp_done, 1)

            def high(h):
                act.wait_ge(own_done, own0[ph] + VALUED[h] + 1)
                nc.scalar.copy(o_hi[:, h, :], pair[(g + 6 + VALUED[h]) % 2][:, 0, :]).then_inc(o_high, 1)

            exps(0)
            exps(1)
            split_high(act, n + 6)
            values_out(1, 5)
            exps(2)
            high(0)
            exps(3)
            high(1)
            split_high(act, n + 7)
            high(2)
            high(3)
            split_high(act, n + 8)

        def xattn_vec(vec, ph, l, c, x_group):
            n, g = unit0[ph], group0[ph]
            split_low(vec, n + 1)
            raw_tiles(vec, c, TAB_XA + 8 * l, x_group, range(4))
            split_low(vec, n + 2)
            raw_tiles(vec, c, TAB_XA + 8 * l, x_group, range(4, KT))
            split_low(vec, n + 3)

            def own(ins):
                c.dv += 1
                ins.then_inc(dve, 1)
                vec.wait_ge(dve, c.dv)

            vec.wait_ge(sq_used, c.sq + KT // 2)
            c.sq += KT // 2
            make_var(vec, c, aux[:, 3, 0:TT], TT, 1.0 / D)
            vec.wait_ge(rs_done, c.var)
            nc.vector.tensor_copy(tok_root[:, 0, :], rs[:, 0:TT]).then_inc(rb_done, 1)
            vec.wait_ge(rb_done, c.var)
            own(nc.vector.tensor_tensor(tok_root[:, 1, :], tok_root[:, 0, :], tok_root[:, 0, :], ALU.mult))
            split_low(vec, n + 4)

            def raw_queries(j):
                vec.wait_ge(w_used, n + 4 + j)
                nc.vector.tensor_copy(q_raw[:, 2 * j:2 * j + 2, :], pair[(g + 3 + j) % 2][:]).then_inc(evac[(g + 3 + j) % 2], 1)

            def query_scales(j):
                vec.wait_ge(rs_done, c.var)
                nc.vector.scalar_tensor_tensor(q_scale[:, 2 * j:2 * j + 2, :], rs[:, 8 * j:8 * j + 8].rearrange("p (h t) -> p h t", h=2),
                                               XSCALE, tok_root[:, 0:1, :].broadcast_to((P, 2, TT)), ALU.mult, ALU.mult).then_inc(rb_done, 1)

            def query_var(j):
                vec.wait_ge(sq_used, c.sq + 1)
                c.sq += 1
                own(nc.vector.tensor_tensor(q_ms[:], aux[:, 3, 8 * j:8 * j + 8].rearrange("p (h t) -> p h t", h=2),
                                            tok_root[:, 1:2, :].broadcast_to((P, 2, TT)), ALU.mult))
                make_var(vec, c, q_ms[:].rearrange("p h t -> p (h t)"), 8, 1.0 / P, 8 * j)

            raw_queries(0)
            vec.wait_ge(sq_used, c.sq + 2)
            c.sq += 2
            make_var(vec, c, aux[:, 0, 0:XH * MT], XH * MT, 1.0 / P)
            read_out(vec, g)
            read_out(vec, g + 1)
            vec.wait_ge(rb_done, c.var)
            for h in range(XH):
                nc.vector.scalar_tensor_tensor(k_t[:, h, :], k_raw[:, h, :], tab[1][:, TAB_XK + l:TAB_XK + l + 1],
                                               aux[:, h // 2, (h % 2) * MEM:(h % 2 + 1) * MEM], ALU.mult,
                                               ALU.mult).then_inc(kn_done, 1)
            query_var(0)
            query_scales(0)
            split_low(vec, n + 5)
            raw_queries(1)

            def maxima(h):
                vec.wait_ge(score_done, XH * l + h + 1)
                a = 2 * (h % 2)
                nc.vector.reduce_max(soft[:, h % 2, 0, :].rearrange("p (a b) -> p a b", a=2),
                                     aux[:, a:a + 2, :].rearrange("p a (b m) -> p a b m", b=2), AX).then_inc(dve, 1)
                c.dv += 1
                vec.wait_ge(dve, c.dv)
                if h % 2 == 0:
                    vec.wait_ge(rb_done, c.var)
                nc.vector.scalar_tensor_tensor(soft[:, h % 2, 1, :], soft[:, h % 2, 0, :], -1.0, q_scale[:, h, :],
                                               ALU.mult, ALU.mult).then_inc(nb_done, 1)

            def norm(h):
                vec.wait_ge(exp_done, TT * (XH * l + h + 1))
                nc.vector.reciprocal(rinv[:, h % 2, :], soft[:, h % 2, 2, :]).then_inc(dve, 1)
                c.dv += 1
                vec.wait_ge(dve, c.dv)
                for tt in range(TT):
                    ins = nc.vector.tensor_scalar(prob[h % 2][:, tt, :], prob[h % 2][:, tt, :], rinv[:, h % 2, tt:tt + 1],
                                                  None, ALU.mult)
                ins.then_inc(prob_done, 1)

            def copy_turned(h):
                vec.wait_ge(own_done, own0[ph] + TURNED[h] + 1)
                gg = g + 6 + TURNED[h]
                nc.vector.tensor_copy(prob_t[h % 2][:], pair[gg % 2][:]).then_inc(evac[gg % 2], 1)

            def low(h):
                vec.wait_ge(o_high, XH * l + h + 1)
                gg = g + 6 + VALUED[h]
                nc.vector.tensor_tensor(o_lo[:, h, :], pair[gg % 2][:, 0, :], o_hi[:, h, :].bitcast(F32),
                                        ALU.subtract).then_inc(o_low, 1)
                nc.vector.tensor_copy(junk[:, h:h + 1], cst[:, 0:1]).then_inc(evac[gg % 2], 1)

            maxima(0)
            query_var(1)
            maxima(1)
            query_scales(1)
            norm(0)
            norm(1)
            split_low(vec, n + 6)
            copy_turned(0)
            maxima(2)
            copy_turned(1)
            low(0)
            norm(2)
            maxima(3)
            copy_turned(2)
            norm(3)
            low(1)
            split_low(vec, n + 7)
            copy_turned(3)
            low(2)
            low(3)
            for k in range(4):
                if k == 2:
                    split_low(vec, n + 8)
                gg = g + 14 + k
                if k % 2:
                    vec.wait_ge(w_used, n + 7 + k // 2)
                else:
                    vec.wait_ge(half_out, 2 * l + k // 2 + 1)
                add_residual(vec, gg, k)
                if k == 1:
                    raw_tiles(vec, c, TAB_FFN + 8 * l, g + 14, range(4))
                elif k > 1:
                    raw_tiles(vec, c, TAB_FFN + 8 * l, g + 14, range(2 * k, 2 * k + 2))

        junk = sb("junk", [P, 4])

        def xattn_pool(pool, ph, l, c):
            norm_pool_squares(pool, c, late_sq_sum)
            pool_root(pool, c, TT)
            pool_root(pool, c, XH * MT)
            c.sq += XH
            for j in range(2):
                pool_root(pool, c, 2 * TT, 2 * TT * j)

        UM = [("u", 0), ("u", 1)]
        for k in range(6):
            UM += [("m", k), ("u", k + 2)]
        UM += [("m", 6), ("m", 7)]

        def gmlp_units(sp, ph, l, j):
            w, n = t["gm_w_in"][j], unit0[ph]

            def v_units(i):
                for k in range(2):
                    load_unit(sp, n + k, [(slot(n + k), cols(w, GM_HID + (2 * i + k) * CW))], 2 * i)

            repeat(sp, 4, v_units, n == 0)
            n += 8
            with sp.Fori(0, 4) as i:
                for k in range(2):
                    load_unit(sp, n + k, [(slot(n + k), cols(w, (2 * i + k) * CW))], 2 * i)
            n += 8
            with sp.Fori(0, 2) as i:
                for k in range(4):
                    load_unit(sp, n + k, [(slot(n + k), cols(t["gm_w_out"][j], (2 * i + k // 2) * CW, k0=(k % 2) * D))], 4 * i)

        def gmlp_pe(pe, ph, l, j, c, x_group):
            n, g, o = unit0[ph], group0[ph], own0[ph]
            norm_pe_sums(pe, c)
            spread(pe, c, 2)
            with pe.Fori(0, 4) as i:
                for k in range(2):
                    free_pair(pe, g + k, i)
                    product_tok(pe, n + k, g + k, hn_hi, hn_lo, TT, 2 * i, ready=hn_ready(pe, ph - 1) if k == 0 else None)
            n, g = n + 8, g + 8
            if ph == mem_ph:
                mem_pe_turn(pe, g)
                g += 2
                o += 2
            pe.wait_ge(ws_in, 32 * (j + 1))
            free_pair(pe, g)
            for k in range(GM_G):
                mm = nc.tensor.transpose(pair[g % 2][:, k // 4, (k % 4) * P:(k % 4 + 1) * P], ws_raw[:, k, :], ident)
            mm.then_inc(own_done, 1)
            g += 1
            for kind, k in UM:
                free_pair(pe, g)
                if kind == "u":
                    product(pe, n, g, hn(hn_hi), hn(hn_lo))
                    n += 1
                    if ph == mem_ph and k == 0:
                        mem_pe_sums(pe, c)
                    if k == 1:
                        c.var += 1
                        v_scaled = c.var
                        if ph == mem_ph:
                            spread(pe, c, 2, tiles=MT)
                else:
                    if k == 0:
                        pe.wait_ge(rb_done, v_scaled)
                        pe.wait_ge(ws_ready, j + 1)
                    for i in range(2):
                        ct = 2 * k + i
                        for b in range(TT):
                            mm = nc.tensor.matmul(pair[g % 2][:, i, b * P:(b + 1) * P], v_tok[:, b, ct * P:(ct + 1) * P],
                                                  ws_t[:, k, :], start=True, stop=True)
                    mm.then_inc(own_done, 1)
                g += 1
            a0 = a_base(ph)
            with pe.Fori(0, 2) as i:
                for k in range(4):
                    if k % 2 == 0:
                        free_pair(pe, g + k // 2, i)
                    product(pe, n + k, g + k // 2,
                            lambda kt, k=k: uv_hi[:, :, (8 * (k % 2) + kt) * P:(8 * (k % 2) + kt + 1) * P],
                            lambda kt, k=k: uv_lo[:, 8 * (k % 2) + kt, :].rearrange("p (a b) -> p a b", a=TT),
                            4 * i, first=k % 2 == 0, last=k % 2 == 1,
                            ready=(lambda kt, k=k: pe.wait_ge(a_low, a0 + (8 * k + kt) // 2 + 1)) if k < 2 else None)

        def gmlp_act(act, ph, l, j, c, x_group):
            n, g, o = unit0[ph], group0[ph], own0[ph]
            norm_act_squares(act, c, x_group)
            if n == 0:
                split_high(act, 0)
            norm_act_high(act, c)

            def v_step(i):
                for k in range(2):
                    split_high(act, n + k + 1, 2 * i)
                    act.wait_ge(w_used, n + k + 1 + 2 * i)
                    nc.scalar.activation(v_tok[:, :, ds((2 * i + k) * CW, CW)],
                                         pair[(g + k) % 2][:].rearrange("p a (b m) -> p (a b) m", b=2),
                                         ACT.Gelu_apprx_tanh).then_inc(evac[(g + k) % 2], 1)

            repeat(act, 4, v_step, n == 0)
            n, g = n + 8, g + 8
            read_out(act, g - 2)
            read_out(act, g - 1)
            for b in range(2):
                if b:
                    act.wait_ge(vss_a, 2 * j + b)
                nc.scalar.activation(square_a[:], v_tok[:, b, :], ACT.Square, accum_out=vss[:, b:b + 1]).then_inc(vss_a, 1)
            if ph == mem_ph:
                mem_act_squares(act, c, g)
                g += 2
                o += 2
            g += 1
            m = 0
            for q, (kind, k) in enumerate(UM):
                if kind == "u":
                    split_high(act, n + 1)
                    act.wait_ge(w_used, n + 1)
                    if k == 0:
                        act.wait_ge(own_done, o + 1)
                    if k == 2:
                        act.wait_ge(vss_a, 2 * (j + 1))
                    if k == 4:
                        act.wait_ge(vss_d, 2 * (j + 1))
                    nc.scalar.activation(u_t[:, 2 * k:2 * k + 2, :], pair[g % 2][:], ACT.Gelu_apprx_tanh).then_inc(evac[g % 2], 1)
                    n += 1
                else:
                    act.wait_ge(a_sq, a_base(ph) + k + 1)
                    nc.scalar.copy(uv_hi[:, :, 2 * k * P:(2 * k + 2) * P].rearrange("p b (c q) -> p c b q", c=2),
                                   tmp[:].rearrange("p c (b q) -> p c b q", b=TT)).then_inc(a_high, 1)
                    if ph == mem_ph and k == 5:
                        mem_norm_act(act, c)
                g += 1
            with act.Fori(0, 2) as i:
                for k in range(4):
                    split_high(act, n + k + 1, 4 * i)

        vss = sb("vss", [P, TT])

        def gmlp_vec(vec, ph, l, j, c, x_group):
            n, g, o = unit0[ph], group0[ph], own0[ph]
            vec.wait_ge(sq_used, c.sq + KT // 2)
            c.sq += KT // 2
            make_var(vec, c, aux[:, 3, 0:TT], TT, 1.0 / D)
            if n == 0:
                split_low(vec, 0)
            vec.wait_ge(rb_done, c.var)
            norm_tiles(vec, c, TAB_MIX + 8 * l, range(KT))
            with vec.Fori(0, 4) as i:
                for k in range(2):
                    split_low(vec, n + k + 1, 2 * i)
            n, g = n + 8, g + 8
            if ph == mem_ph:
                mem_vec_copy(vec, g, o)
                g += 2
                o += 2
            vec.wait_ge(own_done, o + 1)
            nc.vector.tensor_copy(ws_t[:], pair[g % 2][:].rearrange("p a (b t) -> p (a b) t", b=4)).then_inc(evac[g % 2], 1)
            read_out(vec, g)
            nc.vector.memset(ws_t[64:128, :, 0:64], 0.0).then_inc(ws_ready, 1)
            v_last = g - 1 - (2 if ph == mem_ph else 0)
            read_out(vec, v_last - 1)
            read_out(vec, v_last)
            for b in range(2, TT):
                if b == 3:
                    vec.wait_ge(vss_d, 2 * j + 1)
                nc.vector.tensor_tensor_reduce(square_d[:], v_tok[:, b, :], v_tok[:, b, :], 1.0, 0.0, ALU.mult, ALU.add,
                                               vss[:, b:b + 1]).then_inc(vss_d, 1)
            vec.wait_ge(vss_d, 2 * (j + 1))
            vec.wait_ge(vss_a, 2 * (j + 1))
            make_var(vec, c, vss[:], TT, 1.0 / GM_HID)
            split_low(vec, n + 1)
            vec.wait_ge(rs_done, c.var)
            for b in range(TT):
                ins = nc.vector.tensor_scalar(v_tok[:, b, :], v_tok[:, b, :], rs[:, b:b + 1], None, ALU.mult)
            ins.then_inc(rb_done, 1)
            n += 1
            g += 1
            um_group = {}
            for q, (kind, k) in enumerate(UM):
                um_group[kind, k] = g + q
                if kind == "u":
                    if k > 0:
                        split_low(vec, n + 1)
                        n += 1
                    if ph == mem_ph and k == 1:
                        mem_vec_var(vec, c)
                else:
                    own = [x_ for x_ in UM[:q] if x_[0] == "m"]
                    gg = g + q
                    vec.wait_ge(own_done, o + 2 + len(own))
                    for i in range(2):
                        ct = 2 * k + i
                        if a_base(ph) + k > 0:
                            vec.wait_ge(a_low, a_base(ph) + k)
                        gain = TAB_VN + 16 * j + ct
                        ins = nc.vector.scalar_tensor_tensor(
                            tmp[:, i, :].rearrange("p (b t) -> p b t", b=TT), pair[gg % 2][:, i, :].rearrange("p (b t) -> p b t", b=TT),
                            tab[1][:, gain:gain + 1], bs_b[:, k:k + 1, :].broadcast_to((P, TT, P)), ALU.mult, ALU.add)
                    ins.then_inc(evac[gg % 2], 1)
                    read_out(vec, gg)
                    read_out(vec, um_group["u", k])
                    nc.vector.tensor_tensor(tmp[:], tmp[:], u_t[:, 2 * k:2 * k + 2, :], ALU.mult).then_inc(a_sq, 1)
                    vec.wait_ge(a_high, a_base(ph) + k + 1)
                    nc.vector.tensor_tensor(uv_lo[:, 2 * k:2 * k + 2, :].rearrange("p c (b q) -> p c b q", b=TT),
                                            tmp[:].rearrange("p c (b q) -> p c b q", b=TT),
                                            uv_hi[:, :, 2 * k * P:(2 * k + 2) * P].rearrange("p b (c q) -> p c b q", c=2).bitcast(F32),
                                            ALU.subtract).then_inc(a_low, 1)
                    if ph == mem_ph and k == 0:
                        mem_vec_scale(vec, c.var)
                    if ph == mem_ph and k == 5:
                        mem_norm_vec(vec, c, 0)
            g += len(UM)
            with vec.Fori(0, 2) as i:
                for k in range(4):
                    split_low(vec, n + k + 1, 4 * i)
                    if k % 2 == 1:
                        vec.wait_ge(w_used, n + k + 1 + 4 * i)
                        add_residual(vec, g + k // 2, 2 * i + k // 2)

        def gmlp_pool(pool, ph, l, j, c):
            norm_pool_squares(pool, c)
            pool_root(pool, c, TT)
            pool.wait_ge(w_used, unit0[ph])
            if unit0[ph] == 0:
                pool.wait_ge(own_done, 6)
            pool.dma_start(ws_raw[:], t["gm_w_s"][j].rearrange("g t s -> t g s")).then_inc(ws_in, 16)
            pool.dma_start(bs_b[:], t["gm_b_s"][j:j + 1].broadcast_to((P, GM_G, P))).then_inc(ws_in, 16)
            pool_root(pool, c, TT)
            if ph == mem_ph:
                mem_pool(pool, c)

        def ssd_units(sp, ph):
            w, n = t["ssd_w_in"][0], unit0[ph]
            load_unit(sp, n, [(slot(n, width=P), cols(w, SSD_IN - P, P))])
            wbc = w[:, 2 * SSD_XBC:SSD_DT].rearrange("(k p) (q m) -> p k q m", p=P, q=2)
            with sp.Fori(0, SSD_G // 2) as i:
                for p in range(2):
                    gv, u = 2 * i + p, n + 1 + 3 * p
                    load_unit(sp, u, [(slot(u), cols(w, SSD_XBC + gv * CW))], 6 * i)
                    bc_col = sp.snap(gv * P)
                    load_unit(sp, u + 1, [(slot(u + 1)[:, :, q * P:(q + 1) * P], wbc[:, :, q, ds(bc_col, P)])
                                          for q in range(2)], 6 * i)
                    load_unit(sp, u + 2, [(slot(u + 2), cols(w, 2 * CW * i + p * CW))], 6 * i)
            n += 1 + 3 * SSD_G
            with sp.Fori(0, 2) as i:
                for k in range(4):
                    load_unit(sp, n + k, [(slot(n + k), cols(t["ssd_w_out"][0], (2 * i + k // 2) * CW, k0=(k % 2) * D))], 4 * i)

        def ssd_pe(pe, ph, c, x_group):
            n, g, o = unit0[ph], group0[ph], own0[ph]
            norm_pe_sums(pe, c)
            spread(pe, c, 2)
            nc.tensor.matmul(aux[:, 0, 0:16], cst[0:2, 4 * P:5 * P], d_pair[:], start=True, stop=True).then_inc(ssd_aux, 1)
            free_pair(pe, g)
            pe.wait_ge(w_low, n + 1)
            hi, lo = unit_w(n, width=P)
            for kt in range(KT):
                hn_ready(pe, ph - 1)(kt)
                mm = three(pair[g % 2][:, 0, :], hi[:, kt, :], lo[:, kt, :], hn_hi[:, kt, :], hn_lo[:, kt, :], kt == 0, kt == KT - 1)
            mm.then_inc(w_used, 1)
            def turn_dt(kt):
                if kt == 6:
                    pe.wait_ge(ssd_tok, 1)
                    nc.tensor.matmul(aux[:, 1, 0:P], cst[:, P:2 * P], dta_tok[:, 1, :, :].rearrange("p b h -> p (b h)"),
                                     start=True, stop=True).then_inc(ssd_aux, 1)
                if kt != 5:
                    return
                pe.wait_ge(ssd_scan, TT)
                pe.wait_ge(ssd_d, 1)
                for q in range(2):
                    for b in range(TT):
                        mm = nc.tensor.transpose(aux[:, 0, (q * TT + b) * 32:(q * TT + b + 1) * 32], dta[96:P, q, b * P:(b + 1) * P],
                                                 cst[96:P, 96:P])
                mm.then_inc(ssd_aux, 1)

            for k in range(2):
                free_pair(pe, g + 1 + k)
                product(pe, n + 1 + k, g + 1 + k, hn(hn_hi), hn(hn_lo), ready=turn_dt if k == 1 else None)

            def norm_sums(gv):
                pe.wait_ge(s_act, SSD_ACT * gv + 16)
                pe.wait_ge(s_seg, 4 * gv + 4)
                for ct in range(2):
                    for b in range(TT):
                        mm = nc.tensor.matmul(aux[:, 3, b:b + 1], tmp[:, ct, b * P:(b + 1) * P], ones,
                                              start=(ct == 0 and b == 0), stop=ct == 1, skip_group_check=True)
                mm.then_inc(ssd_aux, 1)

            def norm_spread(gv):
                pe.wait_ge(rs_done, c.var + 1 + gv)
                for b in range(TT):
                    mm = nc.tensor.matmul(aux[:, 2, b * P:(b + 1) * P], rs[:, b:b + 1].broadcast_to((P, P)), ident,
                                          start=True, stop=True)
                mm.then_inc(rb_done, 1)

            def two_groups(i):
                for p in range(2):
                    gv, u, gg, adv, ga = 2 * i + p, n + 1 + 3 * p, g + 1 + 4 * p, 6 * i, 4 * i
                    after_one = p == 1 or not isinstance(i, int)

                    def head_sums(r):
                        for b in range(TT):
                            mm = nc.tensor.matmul(aux[:, 2 + r % 2, b * P:(b + 1) * P],
                                                  par[p][:, PAR_A + 4 * b + r:PAR_A + 4 * b + r + 1].broadcast_to((P, P)), ident,
                                                  start=True, stop=True)
                        mm.then_inc(ssd_aux, 1)

                    def amid_z(kt):
                        if kt == 0:
                            pe.wait_ge(s_par, gv + 1)
                            pe.wait_ge(ssd_y, 2 * gv)
                            head_sums(0)
                            head_sums(1)
                        if kt == 1:
                            pe.wait_ge(s_act, SSD_ACT * gv + 3)
                            pe.wait_ge(s_state, gv)
                            pe.wait_ge(ssd_dec, 1)
                            for ct in range(2):
                                for b in range(TT):
                                    mm = nc.tensor.transpose(aux[:, b // 2, (b % 2) * CW + ct * P:(b % 2) * CW + (ct + 1) * P],
                                                             xg[:, ct, b * P:(b + 1) * P], ident)
                            mm.then_inc(ssd_aux, 1)

                    for k in range(0 if after_one else 2, 3):
                        free_pair(pe, gg + k, ga)
                        product(pe, u + k, gg + k, hn(hn_hi), hn(hn_lo), adv,
                                ready=(lambda kt: kt == 5 and norm_sums(gv - 1)) if k == 0 and after_one
                                else amid_z if k == 2 else None)
                        if k == 0 and after_one:
                            norm_spread(gv - 1)
                    pe.wait_ge(s_act, SSD_ACT * gv + 6)
                    pe.wait_ge(s_xdd, gv + 1)
                    for b in range(TT):
                        mm = nc.tensor.transpose(aux[:, 0, b * P:(b + 1) * P], bc[:, 0, b * P:(b + 1) * P], ident)
                    mm.then_inc(ssd_aux, 1)
                    for b in range(TT):
                        mm = nc.tensor.matmul(aux[:, 1, b * P:(b + 1) * P], bc[:, 0, b * P:(b + 1) * P], bc[:, 1, b * P:(b + 1) * P],
                                              start=True, stop=True)
                    mm.then_inc(ssd_aux, 1)
                    for r in range(2, 4):
                        pe.wait_ge(s_seg, 4 * gv + r - 1)
                        head_sums(r)
                    pe.wait_ge(s_act, SSD_ACT * gv + 9)
                    pe.wait_ge(s_cb, gv + 1)
                    for b in range(TT - 1):
                        mm = nc.tensor.matmul(aux[:, b // 2, (b % 2) * CW:(b % 2 + 1) * CW], b_tok[:, b * P:(b + 1) * P], xdd[:, b, :],
                                              start=True, stop=True)
                    mm.then_inc(ssd_aux, 1)
                    free_pair(pe, gg + 3, ga)
                    pe.wait_ge(s_state, gv + 1)
                    for r in range(4):
                        pe.wait_ge(s_m, 4 * gv + r + 1)
                        pe.wait_ge(s_c, 4 * gv + r + 1)
                        rows = slice(64 * (r % 2), 64 * (r % 2) + 64)
                        for b in range(TT):
                            po = pair[(gg + 3) % 2][rows, r // 2, b * P:(b + 1) * P]
                            mm = nc.tensor.matmul(po, xdt[:, b, 64 * r:64 * r + 64], seg(r)[:, b * P:(b + 1) * P],
                                                  start=True, stop=b == 0)
                            if b > 0:
                                mm = nc.tensor.matmul(po, state[:, b - 1, 64 * r:64 * r + 64], cs[:, r, b * P:(b + 1) * P],
                                                      start=False, stop=True)
                    mm.then_inc(own_done, 1)

            two_groups(0)
            with pe.Fori(1, SSD_G // 2) as i:
                two_groups(i)
            norm_sums(SSD_G - 1)
            norm_spread(SSD_G - 1)
            c.var += SSD_G
            n, g = n + 1 + 3 * SSD_G, g + 1 + 4 * SSD_G
            with pe.Fori(0, 2) as i:
                for k in range(4):
                    if k % 2 == 0:
                        free_pair(pe, g + k // 2, i)
                    product(pe, n + k, g + k // 2, lambda kt, k=k: y_hi[:, 8 * (k % 2) + kt, :],
                            lambda kt, k=k: y_lo[:, 8 * (k % 2) + kt, :], 4 * i, first=k % 2 == 0, last=k % 2 == 1,
                            ready=(lambda kt, k=k: pe.wait_ge(s_ylow, (8 * k + kt) // 2 + 1)) if k < 2 else None)

        def ssd_act(act, ph, c, x_group):
            n, g, o = unit0[ph], group0[ph], own0[ph]
            norm_act_squares(act, c, x_group)
            norm_act_high(act, c)
            split_high(act, n + 1)
            act.wait_ge(ssd_dt, 1)
            nc.scalar.activation(dtw[96:P, 2, :], dtw[96:P, 1, :], ACT.Exp, scale=-1.0).then_inc(ssd_e, 1)
            nc.scalar.activation(neg_a[96:P, :], a_log[96:P, :], ACT.Exp).then_inc(ssd_e, 1)
            split_high(act, n + 2)
            split_high(act, n + 3)
            act.wait_ge(ssd_tok, 2)
            nc.scalar.activation(dec_tok[:], dec_tok[:], ACT.Exp).then_inc(ssd_e, 1)
            nc.scalar.activation(cd_b[:], aux[:, 1, 0:P].rearrange("p (b h) -> p b h", b=TT), ACT.Exp).then_inc(ssd_e, 1)

            def two_groups(i):
                for p in range(2):
                    gv, u, gg, adv, ga = 2 * i + p, n + 1 + 3 * p, g + 1 + 4 * p, 6 * i, 4 * i
                    k = 0

                    def did(ins):
                        nonlocal k
                        k += 1
                        ins.then_inc(s_act, 1)

                    act.wait_ge(w_used, u + 1 + adv)
                    act.wait_ge(s_par, gv + 1)
                    act.wait_ge(ssd_y, 2 * gv)
                    for ct in range(2):
                        did(nc.scalar.activation(xg[:, ct, :], pair[gg % 2][:, ct, :], ACT.Identity,
                                                 bias=par[p][:, PAR_CB + ct:PAR_CB + ct + 1],
                                                 scale=par[p][:, PAR_CW + 12 + ct:PAR_CW + 12 + ct + 1]))
                    if not (isinstance(i, int) and gv == 0):
                        split_high(act, u + 2, adv, 64 * i)
                    read_out(act, gg, ga)
                    did(nc.scalar.activation(xg[:], xg[:], ACT.Silu))
                    act.wait_ge(w_used, u + 2 + adv)
                    act.wait_ge(own_done, o + gv)
                    for ct in range(2):
                        did(nc.scalar.activation(bc[:, ct, :], pair[(gg + 1) % 2][:, ct, :], ACT.Identity,
                                                 bias=par[p][:, PAR_CB + 2 + ct:PAR_CB + 3 + ct],
                                                 scale=par[p][:, PAR_CW + 14 + ct:PAR_CW + 15 + ct]))
                    split_high(act, u + 3, adv, 64 * i)
                    read_out(act, gg + 1, ga)
                    did(nc.scalar.activation(bc[:], bc[:], ACT.Silu))
                    a = SSD_AUX * gv + SSD_AUX0

                    def start_decay(r, step_):
                        act.wait_ge(ssd_aux, a + step_)
                        did(nc.scalar.activation(cs[:, r, :], aux[:, 2 + r % 2, :], ACT.Exp))

                    def pair_decay(r):
                        act.wait_ge(s_seg, 4 * gv + r + 1)
                        did(nc.scalar.activation(seg(r), seg(r), ACT.Exp))

                    start_decay(0, 1)
                    start_decay(1, 2)
                    act.wait_ge(ssd_aux, a + 4)
                    did(nc.scalar.copy(b_tok[:], aux[:, 0, :]))
                    pair_decay(0)
                    pair_decay(1)
                    start_decay(2, 6)
                    pair_decay(2)
                    start_decay(3, 7)
                    pair_decay(3)
                    act.wait_ge(w_used, u + 3 + adv)
                    nc.scalar.activation(zg[:], pair[(gg + 2) % 2][:], ACT.Silu).then_inc(evac[(gg + 2) % 2], 1)
                    act.wait_ge(s_yz, gv + 1)
                    did(nc.scalar.activation(tmp[:], xg[:], ACT.Square))
                    if not (isinstance(i, int) and gv == SSD_G - 1):
                        split_high(act, u + 4, adv, 64 * i)
                    assert k == SSD_ACT

            two_groups(0)
            with act.Fori(1, SSD_G // 2 - 1) as i:
                two_groups(i)
            two_groups(SSD_G // 2 - 1)
            n, g = n + 1 + 3 * SSD_G, g + 1 + 4 * SSD_G
            act.wait_ge(own_done, o + SSD_G)
            act.wait_ge(ssd_y, 2 * SSD_G)
            for k in range(8):
                nc.scalar.copy(y_hi[:, 2 * k:2 * k + 2, :], y_f[:, 2 * k:2 * k + 2, :]).then_inc(s_yhigh, 1)
            with act.Fori(0, 2) as i:
                for k in range(4):
                    split_high(act, n + k + 1, 4 * i)

        def ssd_vec(vec, ph, c, x_group):
            n, g, o = unit0[ph], group0[ph], own0[ph]
            vec.wait_ge(sq_used, c.sq + KT // 2)
            c.sq += KT // 2
            make_var(vec, c, aux[:, 3, 0:TT], TT, 1.0 / D)
            vec.wait_ge(rb_done, c.var)
            norm_tiles(vec, c, TAB_MIX + 8, range(KT))
            split_low(vec, n + 1)
            vec.wait_ge(ssd_aux, 1)
            nc.vector.tensor_copy(d_col[:], aux[:, 0, 0:16]).then_inc(ssd_d, 1)

            def own(ins):
                c.dv += 1
                ins.then_inc(dve, 1)
                vec.wait_ge(dve, c.dv)

            q = slice(96, P)
            vec.wait_ge(w_used, n + 1)
            own(nc.vector.tensor_scalar(dtw[q, 0, :], pair[g % 2][q, 0, :], dt_bias[q, :], None, ALU.add))
            nc.vector.tensor_copy(scrap_d[:], cst[:, 0:1]).then_inc(evac[g % 2], 1)
            nc.vector.scalar_tensor_tensor(dtw[q, 1, :], dtw[q, 0, :], -1.0, dtw[q, 0, :], ALU.mult, ALU.max).then_inc(ssd_dt, 1)
            own(nc.vector.tensor_scalar(dtw[q, 0, :], dtw[q, 0, :], 0.0, None, ALU.max))
            vec.wait_ge(ssd_e, 2)
            own(nc.vector.tensor_scalar(dtw[q, 1, :], dtw[q, 2, :], 2.0, None, ALU.add))
            own(nc.vector.reciprocal(dtw[q, 3, :], dtw[q, 1, :]))
            split_low(vec, n + 2)
            own(nc.vector.tensor_tensor(dtw[q, 1, :], dtw[q, 2, :], dtw[q, 3, :], ALU.mult))
            own(nc.vector.tensor_tensor(dtw[q, 2, :], dtw[q, 1, :], dtw[q, 1, :], ALU.mult))
            own(nc.vector.tensor_scalar(dtw[q, 3, :], dtw[q, 2, :], 1.0 / 17, None, ALU.mult))
            for odd in (15, 13, 11, 9, 7, 5, 3):
                own(nc.vector.scalar_tensor_tensor(dtw[q, 3, :], dtw[q, 3, :], 1.0 / odd, dtw[q, 2, :], ALU.add, ALU.mult))
            own(nc.vector.scalar_tensor_tensor(dtw[q, 3, :], dtw[q, 3, :], 1.0, dtw[q, 1, :], ALU.add, ALU.mult))
            own(nc.vector.scalar_tensor_tensor(dta[q, 0, :], dtw[q, 3, :], 2.0, dtw[q, 0, :], ALU.mult, ALU.add))
            own(nc.vector.tensor_scalar(neg_a[q, :], neg_a[q, :], -1.0, None, ALU.mult))
            own(nc.vector.tensor_scalar(dtw[q, 3, :], dta[q, 0, :], neg_a[q, :], None, ALU.mult))
            own(nc.vector.memset(dtw[q, 2, 0:P], 1.0))
            for b in range(TT):
                nc.vector.tensor_tensor_scan(dta[q, 1, b * P:(b + 1) * P], dtw[q, 2, 0:P], dtw[q, 3, b * P:(b + 1) * P],
                                             0.0, ALU.mult, ALU.add).then_inc(ssd_scan, 1)
            vec.wait_ge(ssd_scan, TT)
            vec.wait_ge(ssd_aux, 2)
            nc.vector.tensor_copy(dta_tok[:].rearrange("p q b h -> p (q b h)"), aux[:, 0, 0:2 * P]).then_inc(ssd_tok, 1)
            vec.wait_ge(ssd_aux, 3)
            vec.wait_ge(ssd_tok, 1)
            nc.vector.tensor_tensor(dec_tok[:], aux[:, 1, 0:P].rearrange("p (b h) -> p b h", b=TT), dta_tok[:, 1, :, :],
                                    ALU.subtract).then_inc(ssd_tok, 1)
            vec.wait_ge(ssd_e, 4)
            nc.vector.tensor_copy(scrap_d[:], cst[:, 0:1]).then_inc(ssd_dec, 1)

            def parameters(gv, pr, step):
                step(nc.vector.tensor_copy(pr[:, PAR_CW:PAR_CW + 16].rearrange("p (t c) -> p t c", t=4)[:, :, 0:2],
                                           tab[2][:].rearrange("p (t c) -> p t c", t=4)[:, :, ds(2 * gv, 2)]), False)
                step(nc.vector.tensor_copy(pr[:, PAR_CW:PAR_CW + 16].rearrange("p (t c) -> p t c", t=4)[:, :, 2:4],
                                           tab[2][:].rearrange("p (t c q) -> p t c q", t=4, c=4)[:, :, 2:4, ds(gv, 1)].rearrange("p t c q -> p t (c q)")), False)
                step(nc.vector.tensor_copy(pr[:, PAR_CB:PAR_CB + 2], tab[1][:, ds(TAB_CB + 2 * gv, 2)]), False)
                step(nc.vector.tensor_copy(pr[:, PAR_CB + 2:PAR_CB + 3], tab[1][:, ds(TAB_CB + 16 + gv, 1)]), False)
                step(nc.vector.tensor_copy(pr[:, PAR_CB + 3:PAR_CB + 4], tab[1][:, ds(TAB_CB + 24 + gv, 1)]), False)
                step(nc.vector.tensor_copy(pr[:, PAR_D:PAR_D + 2], d_col[:, ds(2 * gv, 2)]), False)
                step(nc.vector.tensor_copy(pr[:, PAR_G:PAR_G + 2], tab[1][:, ds(TAB_ON + 2 * gv, 2)]))
                nc.vector.tensor_copy(pr[:, PAR_A:PAR_A + 16].rearrange("p (b r) -> p b r", b=TT),
                                      dta_tok[:, 1, :, ds(4 * gv, 4)]).then_inc(s_par, 1)
                vec.wait_ge(s_par, gv + 1)

            v0 = c.dv + PAR_STEPS

            def first_step(ins, wait=True):
                c.dv += 1
                ins.then_inc(dve, 1)
                if wait:
                    vec.wait_ge(dve, c.dv)

            parameters(0, par[0], first_step)
            split_low(vec, n + 3)

            def two_groups(i):
                for p in range(2):
                    gv, u, gg, adv, ga = 2 * i + p, n + 1 + 3 * p, g + 1 + 4 * p, 6 * i, 4 * i
                    k = 0

                    def step(ins, wait=True):
                        nonlocal k
                        k += 1
                        ins.then_inc(dve, 1)
                        if wait:
                            vec.wait_ge(dve, v0 + SSD_DVE * gv + k)

                    pr = par[p]

                    def conv(dst, src, tap_act, pc, last):
                        vec.wait_ge(s_act, SSD_ACT * gv + tap_act)
                        for back in range(1, 4):
                            for ct in range(2):
                                w = PAR_CW + 4 * (3 - back) + pc + ct
                                ins = nc.vector.scalar_tensor_tensor(dst[:, ct, back:S], src[:, ct, 0:S - back], pr[:, w:w + 1],
                                                                     dst[:, ct, back:S], ALU.mult, ALU.add)
                                if back == 3 and ct == 1:
                                    ins.then_inc(last, 1)
                                else:
                                    step(ins, ct == 1)

                    conv(xg, pair[gg % 2], 2, 0, evac[gg % 2])
                    if not (isinstance(i, int) and gv == 0):
                        split_low(vec, u + 2, adv)
                    conv(bc, pair[(gg + 1) % 2], 5, 2, evac[(gg + 1) % 2])
                    f = "p b (r c) -> p b r c"
                    a = SSD_AUX * gv + SSD_AUX0
                    vec.wait_ge(ssd_aux, a + 3)
                    px = aux[:, 0:2, :].rearrange("p a (b r c) -> p (a b) r c", b=2, r=4)
                    step(nc.vector.tensor_tensor(xdt[:].rearrange(f, r=4), px, spread64(dta_tok[:, 0, :, ds(4 * gv, 4)]), ALU.mult))
                    nc.vector.tensor_tensor(xdd[:].rearrange(f, r=4), xdt[:].rearrange(f, r=4),
                                            spread64(dec_tok[:, :, ds(4 * gv, 4)]), ALU.mult).then_inc(s_xdd, 1)

                    def decays(r):
                        vec.wait_ge(s_act, SSD_ACT * gv + (7, 8, 12, 14)[r])
                        for b in range(TT):
                            ins = nc.vector.tensor_scalar(seg(r)[:, b * P:(b + 1) * P], aux[:, 2 + r % 2, b * P:(b + 1) * P],
                                                          pr[:, PAR_A + 4 * b + r:PAR_A + 4 * b + r + 1], 0.0, ALU.subtract, ALU.min)
                        ins.then_inc(s_seg, 1)

                    def weights(r):
                        if r == 0:
                            vec.wait_ge(s_cb, gv + 1)
                        vec.wait_ge(s_act, SSD_ACT * gv + (10, 11, 13, 15)[r])
                        nc.vector.tensor_tensor(seg(r), seg(r), cbm[:], ALU.mult).then_inc(s_m, 1)

                    decays(0)
                    decays(1)
                    vec.wait_ge(ssd_aux, a + 5)
                    nc.vector.tensor_tensor(cbm[:].rearrange("p (b l) -> p b l", b=TT), aux[:, 1, :].rearrange("p (b l) -> p b l", b=TT),
                                            cst[:, 2 * P:3 * P].rearrange("p (a l) -> p a l", a=1).broadcast_to((P, TT, P)),
                                            ALU.mult).then_inc(s_cb, 1)
                    weights(0)
                    decays(2)
                    weights(1)
                    vec.wait_ge(ssd_aux, a + 8)
                    step(nc.vector.tensor_copy(state[:, 0, :], aux[:, 0, 0:CW]))
                    for b in range(1, TT - 1):
                        sv = lambda m: state[:, m, :].rearrange("p (r c) -> p r c", r=4)
                        step(nc.vector.tensor_tensor(sv(b), sv(b - 1),
                                                     spread64(cd_b[:, b:b + 1, ds(4 * gv, 4)].rearrange("p b r -> p (b r)")), ALU.mult))
                        ins = nc.vector.tensor_tensor(state[:, b, :], aux[:, b // 2, (b % 2) * CW:(b % 2 + 1) * CW], state[:, b, :], ALU.add)
                        if b == TT - 2:
                            ins.then_inc(s_state, 1)
                        else:
                            step(ins)
                    decays(3)
                    weights(2)
                    weights(3)
                    split_low(vec, u + 3, adv)
                    vec.wait_ge(own_done, o + gv + 1)
                    for ct in range(2):
                        ins = nc.vector.scalar_tensor_tensor(xg[:, ct, :], xg[:, ct, :], pr[:, PAR_D + ct:PAR_D + ct + 1],
                                                             pair[(gg + 3) % 2][:, ct, :], ALU.mult, ALU.add)
                        if ct == 0:
                            step(ins, False)
                        else:
                            ins.then_inc(evac[(gg + 3) % 2], 1)
                    read_out(vec, gg + 3, ga)
                    read_out(vec, gg + 2, ga)
                    nc.vector.tensor_tensor(xg[:], xg[:], zg[:], ALU.mult).then_inc(s_yz, 1)
                    vec.wait_ge(ssd_aux, a + 9)
                    vec.wait_ge(rs_done, c.var + gv)
                    nc.vector.tensor_scalar(var[:, 0:TT], aux[:, 3, 0:TT], 1.0 / CW, EPS, ALU.mult, ALU.add).then_inc(var_done, 1)
                    if not (isinstance(i, int) and gv == SSD_G - 1):
                        split_low(vec, u + 4, adv)
                        parameters(gv + 1, par[1 - p], step)
                    vec.wait_ge(rb_done, c.var + 1 + gv)
                    for ct in range(2):
                        nc.vector.scalar_tensor_tensor(y_f[:, ds(2 * gv + ct, 1), :].rearrange("p a s -> p (a s)"), xg[:, ct, :],
                                                       pr[:, PAR_G + ct:PAR_G + ct + 1], aux[:, 2, :], ALU.mult, ALU.mult).then_inc(ssd_y, 1)
                    assert k == SSD_DVE or k == SSD_DVE - PAR_STEPS, k
            two_groups(0)
            with vec.Fori(1, SSD_G // 2 - 1) as i:
                two_groups(i)
            two_groups(SSD_G // 2 - 1)
            c.var += SSD_G
            c.dv = v0 + SSD_DVE * SSD_G - PAR_STEPS
            n, g = n + 1 + 3 * SSD_G, g + 1 + 4 * SSD_G
            for k in range(8):
                vec.wait_ge(s_yhigh, k + 1)
                if k == 0:
                    vec.wait_ge(ssd_y, 2 * SSD_G)
                nc.vector.tensor_tensor(y_lo[:, 2 * k:2 * k + 2, :], y_f[:, 2 * k:2 * k + 2, :],
                                        y_hi[:, 2 * k:2 * k + 2, :].bitcast(F32), ALU.subtract).then_inc(s_ylow, 1)
            with vec.Fori(0, 2) as i:
                for k in range(4):
                    split_low(vec, n + k + 1, 4 * i)
                    if k % 2 == 1:
                        vec.wait_ge(w_used, n + k + 1 + 4 * i)
                        add_residual(vec, g + k // 2, 2 * i + k // 2)

        def ssd_pool(pool, ph, c):
            norm_pool_squares(pool, c)
            pool_root(pool, c, TT)
            with pool.Fori(0, SSD_G // 2) as i:
                for p in range(2):
                    gv = 2 * i + p
                    for r in range(4):
                        pool.wait_ge(s_act, SSD_ACT * gv + (7, 8, 12, 14)[r])
                        nc.gpsimd.tensor_tensor(cs[:, r, :], cs[:, r, :], bc[:, 1, :], ALU.mult).then_inc(s_c, 1)
                    pool.wait_ge(var_done, c.var + 1 + gv)
                    pool.wait_ge(rb_done, c.var + gv)
                    nc.gpsimd.tensor_tensor(rs[:, 0:TT], var[:, 0:TT], nh16[:, 0:TT], ALU.pow).then_inc(rs_done, 1)
            c.var += SSD_G

        STEPS = ([("qi", k, 2, None, True) for k in range(2)] + [("ki", 0, 1, TAB_DI, True)]
                 + [("q", k, 2, TAB_DQ, True) for k in range(4)] + [("k", k, 2, TAB_DK, True) for k in range(2)]
                 + [("v", 0, 0, None, False)])
        N_STEPS = len(STEPS)
        NORMED = [s_ for s_, st in enumerate(STEPS) if st[3] is not None]
        SPREAD = [s_ for s_ in NORMED if STEPS[s_][0] != "q"]
        ROTATED = [s_ for s_, st in enumerate(STEPS) if st[4]]
        HEADS = [(b, h) for b in range(TT) for h in range(DH)]

        INDEX = [(b, h) for b in range(1, TT) for h in range(DI_H)]

        def index_after(i):
            b, h = HEADS[i]
            return DI_H * (b + 1) + h // 2 if h % 2 and b + 2 < TT else None

        def made(s_):
            kind, k = STEPS[s_][0:2]
            return {"qi": qi, "ki": ki_w, "q": q_d, "k": k_d}[kind][:, 2 * k:2 * k + 2, :]

        def head_q(h):
            return slice(64 * (h % 2), 64 * (h % 2) + 64), h // 2

        def dsa_units(sp, ph):
            w, n = t["dsa_w_in"][0], unit0[ph]
            for s_, (kind, k, *_) in enumerate(STEPS):
                s = slot(n + s_)
                if kind == "ki":
                    parts = [(s[:, :, 0:64], cols(w, DSA_KI, 64)), (s[:, :, 64:P], cols(w, DSA_KI, 64)),
                             (s[:, :, P:CW], cols(w, DSA_IN - P, P))]
                elif kind == "k":
                    parts = [(s[:, :, 64 * q:64 * q + 64], cols(w, DSA_K + 64 * (2 * k + q // 2), 64)) for q in range(4)]
                else:
                    parts = [(s, cols(w, {"qi": DSA_QI, "q": 0, "v": DSA_V}[kind] + k * CW))]
                load_unit(sp, n + s_, parts)
            for k in range(4):
                load_unit(sp, n + N_STEPS + k, [(slot(n + N_STEPS + k), cols(t["dsa_w_out"][0], k * CW))])

        def dsa_pe(pe, ph, c, x_group):
            n, g, o = unit0[ph], group0[ph], own0[ph]
            norm_pe_sums(pe, c)
            spread(pe, c, 2)
            v0 = c.var
            for s_ in range(N_STEPS + 2):
                if s_ < N_STEPS:
                    ready = hn_ready(pe, ph - 1) if s_ == 0 else None
                    free_pair(pe, g + s_)
                    if STEPS[s_][0] == "v":
                        product_tok(pe, n + s_, g + s_, hn_hi, hn_lo, TT)
                    else:
                        product(pe, n + s_, g + s_, hn(hn_hi), hn(hn_lo), ready=ready)
                if s_ in NORMED:
                    k = NORMED.index(s_)
                    pe.wait_ge(d_sq, k + 1)
                    done = sum(r <= s_ - 3 for r in ROTATED)
                    if done:
                        pe.wait_ge(d_rope, done)
                    for i in range(STEPS[s_][2]):
                        for b in range(TT):
                            mm = nc.tensor.matmul(aux[:, 0, 4 * b + 2 * i:4 * b + 2 * i + 2], sq[k % 2][:, i, b * P:(b + 1) * P],
                                                  cst[:, 5 * P + 1:5 * P + 3], start=True, stop=True)
                    mm.then_inc(d_sum, 1)
                if STEPS[s_ - 2][4] if 2 <= s_ else False:
                    k = ROTATED.index(s_ - 2)
                    if s_ - 2 in SPREAD:
                        pe.wait_ge(d_norm, SPREAD.index(s_ - 2) + 1)
                    else:
                        read_out(pe, g + s_ - 2)
                    if k:
                        pe.wait_ge(d_rope, k)
                    pe.wait_ge(var_done, v0 + sum(r <= s_ for r in NORMED))
                    for i in range(STEPS[s_ - 2][2]):
                        mm = nc.tensor.matmul(aux[:, i, :], cst[:, 3 * P:4 * P], made(s_ - 2)[:, i, :], start=True, stop=True)
                    mm.then_inc(d_rot, 1)
                if s_ - 1 in SPREAD:
                    k = SPREAD.index(s_ - 1)
                    pe.wait_ge(rs_done, v0 + NORMED.index(s_ - 1) + 1)
                    if k:
                        pe.wait_ge(d_norm, k)
                    else:
                        pe.wait_ge(hn_low, KT * ph)
                    for i in range(STEPS[s_ - 1][2]):
                        for b in range(TT):
                            for half in range(2):
                                col = rs[:, 4 * b + 2 * i + half:4 * b + 2 * i + half + 1].broadcast_to((P, 64))
                                mm = nc.tensor.matmul(aux[64 * half:64 * half + 64, 2 + i, b * P:(b + 1) * P], col, ident,
                                                      start=True, stop=True)
                    mm.then_inc(rb_done, 1)
            c.var += len(NORMED)
            gg = g + N_STEPS
            free_pair(pe, gg)
            for b in range(TT):
                mm = nc.tensor.transpose(pair[gg % 2][:, 0, b * P:(b + 1) * P], ki_w[:, 1, b * P:(b + 1) * P], ident)
            mm.then_inc(own_done, 1)
            pe.wait_ge(d_rope, len(ROTATED))
            read_out(pe, gg - 1)
            read_out(pe, gg)

            def index_logits(k):
                b, h = INDEX[k]
                rows, ht = head_q(h)
                if k >= 2:
                    pe.wait_ge(d_relu, k - 1)
                nc.tensor.matmul(pair[k % 2][:, 1, 0:(b + 1) * P], qi[rows, ht, b * P:(b + 1) * P], ki_w[rows, 0, 0:(b + 1) * P],
                                 start=True, stop=True).then_inc(d_logit, 1)

            for k in range(DI_H):
                index_logits(k)

            def scores(i):
                b, h = HEADS[i]
                rows, ht = head_q(h)
                if i >= 2:
                    pe.wait_ge(d_nb, i - 1)
                nc.tensor.matmul(aux[:, 2 + i % 2, 0:(b + 1) * P], q_d[rows, ht, b * P:(b + 1) * P], k_d[rows, h // 4, 0:(b + 1) * P],
                                 start=True, stop=True).then_inc(d_score, 1)

            def turn(i):
                b, h = HEADS[i]
                q = gg + 1 + i
                pe.wait_ge(d_prob, i + 1)
                free_pair(pe, q)
                for m in range(b + 1):
                    mm = nc.tensor.transpose(pair[q % 2][:, 0, m * P:(m + 1) * P], pr_d[i % PRB][:, m * P:(m + 1) * P], ident)
                mm.then_inc(own_done, 1)

            def values(i):
                b, h = HEADS[i]
                rows, ht = head_q(h)
                read_out(pe, gg + 1 + i)
                if i >= 4 and i % 2 == 0:
                    pe.wait_ge(d_olow, i // 2 - 1)
                for m in range(b + 1):
                    mm = nc.tensor.matmul(aux[rows, (i // 2) % 2, 0:P], v_d[:, m, 64 * (h // 4):64 * (h // 4) + 64],
                                          pt_d[i % 2][:, m * P:(m + 1) * P], start=m == 0, stop=m == b)
                mm.then_inc(d_out, 1)

            for i in range(len(HEADS) + 3):
                if i < len(HEADS):
                    scores(i)
                    if index_after(i) is not None:
                        index_logits(index_after(i))
                if 2 <= i < len(HEADS) + 2:
                    turn(i - 2)
                if i >= 3:
                    values(i - 3)
            g2 = gg + 1 + len(HEADS)
            pe.wait_ge(d_olow, len(HEADS) // 2)
            for k in range(4):
                free_pair(pe, g2 + k)
                product(pe, n + N_STEPS + k, g2 + k, hn(hn_hi), hn(hn_lo))

        def dsa_act(act, ph, c, x_group):
            n, g, o = unit0[ph], group0[ph], own0[ph]
            norm_act_squares(act, c, x_group)
            norm_act_high(act, c)
            split_high(act, n + 1)
            act.wait_ge(d_ang, 1)
            nc.scalar.activation(sin_t[:], ang[:, 0, :], ACT.Sin).then_inc(d_sin, 1)
            nc.scalar.activation(cos_t[:], ang[:, 1, :], ACT.Sin).then_inc(d_sin, 1)
            for s_ in range(N_STEPS):
                if s_ > 0:
                    split_high(act, n + s_ + 1)
                if s_ in NORMED:
                    k = NORMED.index(s_)
                    m = STEPS[s_][2]
                    if s_ in SPREAD:
                        read_out(act, g + s_)
                        raw = made(s_)[:, 0:m, :]
                    else:
                        act.wait_ge(w_used, n + s_ + 1)
                        raw = pair[(g + s_) % 2][:]
                    if k >= 2:
                        act.wait_ge(d_sum, k - 1)
                    nc.scalar.activation(sq[k % 2][:, 0:m, :], raw, ACT.Square).then_inc(d_sq, 1)
                if STEPS[s_][0] == "v":
                    act.wait_ge(w_used, n + s_ + 1)
                    nc.scalar.copy(v_d[:], pair[(g + s_) % 2][:].rearrange("p a (b m) -> p (a b) m", b=2)).then_inc(evac[(g + s_) % 2], 1)
            gg = g + N_STEPS
            act.wait_ge(d_rope, len(ROTATED))

            def clip(k):
                b, h = INDEX[k]
                act.wait_ge(d_logit, k + 1)
                if k >= 2:
                    act.wait_ge(d_acc, k - 1)
                nc.scalar.activation(tmp[:, k % 2, 0:(b + 1) * P], pair[k % 2][:, 1, 0:(b + 1) * P], ACT.Relu).then_inc(d_relu, 1)

            for k in range(DI_H):
                clip(k)

            def exps(i):
                b, h = HEADS[i]
                act.wait_ge(d_nb, i + 1)
                nc.scalar.activation(pr_d[i % PRB][:, 0:(b + 1) * P], pr_d[i % PRB][:, 0:(b + 1) * P], ACT.Exp,
                                     bias=soft_d[:, i % PRB, 1:2], scale=q_scale_d[:, b, h:h + 1], accum_out=soft_d[:, i % PRB, 2:3]).then_inc(d_exp, 1)

            def copy_turned(i):
                b, h = HEADS[i]
                q = gg + 1 + i
                act.wait_ge(own_done, o + 2 + i)
                if i >= 2:
                    act.wait_ge(d_out, i - 1)
                nc.scalar.copy(pt_d[i % 2][:, 0:(b + 1) * P], pair[q % 2][:, 0, 0:(b + 1) * P]).then_inc(evac[q % 2], 1)

            def high(i):
                b, h = HEADS[i]
                act.wait_ge(d_out, i + 1)
                nc.scalar.copy(hn_hi[:, h // 2, b * P:(b + 1) * P], aux[:, (i // 2) % 2, 0:P]).then_inc(d_ohigh, 1)

            for i in range(len(HEADS) + 4):
                if i < len(HEADS):
                    exps(i)
                    if index_after(i) is not None:
                        clip(index_after(i))
                if 2 <= i < len(HEADS) + 2:
                    copy_turned(i - 2)
                if i >= 4 and i % 2 == 1:
                    high(i - 4)
            for k in range(4):
                split_high(act, n + N_STEPS + k + 1)

        def dsa_vec(vec, ph, c, x_group):
            n, g, o = unit0[ph], group0[ph], own0[ph]
            vec.wait_ge(sq_used, c.sq + KT // 2)
            c.sq += KT // 2
            make_var(vec, c, aux[:, 3, 0:TT], TT, 1.0 / D)
            vec.wait_ge(rb_done, c.var)
            norm_tiles(vec, c, TAB_MIX + 16, range(KT))

            def own(ins):
                c.dv += 1
                ins.then_inc(dve, 1)
                vec.wait_ge(dve, c.dv)

            split_low(vec, n + 1)
            vec.wait_ge(pos_in, 16)
            own(nc.vector.tensor_copy(ang[:, 0, :], pos_i[:]))
            own(nc.vector.tensor_scalar(ang[:, 0, :], ang[:, 0, :], cst[:, 5 * P:5 * P + 1], None, ALU.mult))
            own(nc.vector.tensor_scalar(ang[:, 1, :], ang[:, 0, :], 1 / (2 * np.pi), ROUND, ALU.mult, ALU.add))
            own(nc.vector.tensor_scalar(ang[:, 1, :], ang[:, 1, :], ROUND, None, ALU.subtract))
            for part in (TURN1, TURN2, TURN3):
                own(nc.vector.scalar_tensor_tensor(ang[:, 0, :], ang[:, 1, :], -part, ang[:, 0, :], ALU.mult, ALU.add))
            own(nc.vector.tensor_scalar(ang[:, 0, :], ang[:, 0, :], -PI, PI, ALU.max, ALU.min))
            own(nc.vector.scalar_tensor_tensor(ang[:, 1, :], ang[:, 0, :], -1.0, ang[:, 0, :], ALU.mult, ALU.max))
            nc.vector.tensor_scalar(ang[:, 1, :], ang[:, 1, :], -1.0, np.pi / 2, ALU.mult, ALU.add).then_inc(d_ang, 1)

            v0 = c.var
            for s_ in range(N_STEPS + 2):
                if 0 < s_ < N_STEPS:
                    split_low(vec, n + s_ + 1)
                if s_ < N_STEPS and STEPS[s_][0] == "q":
                    vec.wait_ge(d_sq, NORMED.index(s_) + 1)
                    nc.vector.tensor_scalar(made(s_), pair[(g + s_) % 2][:], tab[1][:, TAB_DQ:TAB_DQ + 1], None,
                                            ALU.mult).then_inc(evac[(g + s_) % 2], 1)
                elif s_ < N_STEPS and STEPS[s_][0] != "v":
                    vec.wait_ge(w_used, n + s_ + 1)
                    nc.vector.tensor_copy(made(s_), pair[(g + s_) % 2][:]).then_inc(evac[(g + s_) % 2], 1)
                if s_ - 1 in NORMED and s_ - 1 not in SPREAD:
                    h0 = 4 * STEPS[s_ - 1][1]
                    vec.wait_ge(rs_done, v0 + NORMED.index(s_ - 1) + 1)
                    nc.vector.tensor_scalar(q_scale_d[:, :, h0:h0 + 4], rs[:].rearrange("p (b j) -> p b j", b=TT), DSCALE, None,
                                            ALU.mult).then_inc(rb_done, 1)
                if s_ in NORMED:
                    k = NORMED.index(s_)
                    width = 16
                    vec.wait_ge(d_sum, k + 1)
                    if STEPS[s_][2] == 1:
                        vec.wait_ge(rs_done, c.var)
                        nc.vector.tensor_scalar(var[:, 0:16].rearrange("p (b i) -> p b i", b=TT)[:, :, 0:2],
                                                aux[:, 0, 0:16].rearrange("p (b i) -> p b i", b=TT)[:, :, 0:2],
                                                1.0 / 64, EPS, ALU.mult, ALU.add).then_inc(var_done, 1)
                        c.var += 1
                    else:
                        make_var(vec, c, aux[:, 0, 0:width], width, 1.0 / 64)
                if 2 <= s_ and STEPS[s_ - 2][4]:
                    k, m = ROTATED.index(s_ - 2), STEPS[s_ - 2][2]
                    vec.wait_ge(d_rot, k + 1)
                    if k == 0:
                        vec.wait_ge(d_sin, 2)
                    own(nc.vector.tensor_tensor(tmp[:, 0:m, :], aux[:, 0:m, :], over_tiles(sin_t, m), ALU.mult))
                    vec.wait_ge(d_cos, k + 1)
                    nc.vector.tensor_tensor(made(s_ - 2)[:, 0:m, :], made(s_ - 2)[:, 0:m, :], tmp[:, 0:m, :], ALU.add).then_inc(d_rope, 1)
                    vec.wait_ge(d_rope, k + 1)
                if s_ - 1 in SPREAD:
                    k, m, gain = NORMED.index(s_ - 1), STEPS[s_ - 1][2], STEPS[s_ - 1][3]
                    vec.wait_ge(rb_done, v0 + k + 1)
                    nc.vector.scalar_tensor_tensor(made(s_ - 1)[:, 0:m, :], made(s_ - 1)[:, 0:m, :], tab[1][:, gain:gain + 1],
                                                   aux[:, 2:2 + m, :], ALU.mult, ALU.mult).then_inc(d_norm, 1)
            gg = g + N_STEPS
            vec.wait_ge(own_done, o + 1)
            nc.vector.tensor_scalar(wi_tok[:], pair[gg % 2][:, 0, :].rearrange("p (b m) -> p b m", b=TT)[:, :, P - DI_H:P],
                                    DI_H ** -0.5 * 64 ** -0.5, None, ALU.mult).then_inc(evac[gg % 2], 1)
            read_out(vec, gg)
            own(nc.vector.memset(msk[:, 0, 0:P], 0.0))
            own(nc.vector.memset(msk[0:64, 0, 64:P], -HIDE))

            def add_up(k):
                b, h = INDEX[k]
                a = msk[:, b, 0:(b + 1) * P]
                vec.wait_ge(d_relu, k + 1)
                if h == 0:
                    ins = nc.vector.tensor_scalar(a, tmp[:, k % 2, 0:(b + 1) * P], wi_tok[:, b, h:h + 1], None, ALU.mult)
                else:
                    vec.wait_ge(d_acc, k)
                    ins = nc.vector.scalar_tensor_tensor(a, tmp[:, k % 2, 0:(b + 1) * P], wi_tok[:, b, h:h + 1], a, ALU.mult, ALU.add)
                ins.then_inc(d_acc, 1)
                if h == DI_H - 1:
                    vec.wait_ge(d_acc, k + 1)
                    own(nc.vector.memset(msk[0:64, b, (b + 1) * P - 64:(b + 1) * P], -OUT_OF_REACH))

            for k in range(DI_H):
                add_up(k)

            def top_round(b):
                a = msk[:, b, 0:(b + 1) * P]
                own(nc.vector.max(top8[:], a))
                own(nc.vector.match_replace(a, top8[:], a, -TAKEN))

            def scores(i):
                b, h = HEADS[i]
                w = (b + 1) * P
                vec.wait_ge(d_score, i + 1)
                if i >= PRB:
                    vec.wait_ge(own_done, o + 2 + i - PRB)
                own(nc.vector.tensor_tensor_reduce(pr_d[i % PRB][:, 0:w], aux[:, 2 + i % 2, 0:w], msk[:, b, 0:w], 1.0, -3e38,
                                                   ALU.add, ALU.max, soft_d[:, i % PRB, 0:1]))
                nc.vector.tensor_scalar(soft_d[:, i % PRB, 1:2], soft_d[:, i % PRB, 0:1], q_scale_d[:, b, h:h + 1], -1.0,
                                        ALU.mult, ALU.mult).then_inc(d_nb, 1)

            def inverse(i):
                vec.wait_ge(d_exp, i + 1)
                nc.vector.reciprocal(soft_d[:, i % PRB, 3:4], soft_d[:, i % PRB, 2:3]).then_inc(d_inv, 1)

            def low(i):
                b, h = HEADS[i]
                vec.wait_ge(d_ohigh, i // 2 + 1)
                nc.vector.tensor_tensor(hn_lo[:, h // 2, b * P:(b + 1) * P], aux[:, (i // 2) % 2, 0:P],
                                        hn_hi[:, h // 2, b * P:(b + 1) * P].bitcast(F32), ALU.subtract).then_inc(d_olow, 1)

            for i in range(len(HEADS) + 5):
                if 1 <= i <= len(HEADS):
                    inverse(i - 1)
                if i < len(HEADS):
                    scores(i)
                    b, h = HEADS[i]
                    if b + 1 < TT:
                        top_round(b + 1)
                        if h == DH - 1:
                            a = msk[:, b + 1, 0:(b + 2) * P]
                            own(nc.vector.tensor_scalar(a, a, -TAKEN, HIDE, ALU.is_equal, ALU.mult))
                            own(nc.vector.tensor_scalar(a, a, -HIDE, None, ALU.add))
                    if index_after(i) is not None:
                        add_up(index_after(i))
                if i >= 5 and i % 2 == 0:
                    low(i - 5)
            g2 = gg + 1 + len(HEADS)
            for k in range(4):
                split_low(vec, n + N_STEPS + k + 1)
                vec.wait_ge(w_used, n + N_STEPS + k + 1)
                add_residual(vec, g2 + k, k)

        def dsa_pool(pool, ph, c):
            norm_pool_squares(pool, c)
            pool.wait_ge(w_used, unit0[ph])
            pool.dma_start(pos_i[:], t["positions"].broadcast_to((P, S))).then_inc(pos_in, 16)
            pool_root(pool, c, TT)
            for s_ in range(N_STEPS + 2):
                if s_ in NORMED:
                    pool_root(pool, c, 16)
                if 2 <= s_ and STEPS[s_ - 2][4]:
                    k, m = ROTATED.index(s_ - 2), STEPS[s_ - 2][2]
                    pool.wait_ge(d_rot, k + 1)
                    if k == 0:
                        pool.wait_ge(d_sin, 2)
                    for i in range(m):
                        ins = nc.gpsimd.tensor_tensor(made(s_ - 2)[:, i, :], made(s_ - 2)[:, i, :], cos_t[:], ALU.mult)
                    ins.then_inc(d_cos, 1)
            for i, (b, h) in enumerate(HEADS):
                pool.wait_ge(d_inv, i + 1)
                nc.gpsimd.tensor_scalar(pr_d[i % PRB][:, 0:(b + 1) * P], pr_d[i % PRB][:, 0:(b + 1) * P], soft_d[:, i % PRB, 3:4], None,
                                        ALU.mult).then_inc(d_prob, 1)

        def store_pe(pe, ph):
            g = group0[ph]
            for tt in range(TT):
                free_pair(pe, g)
                if tt == 0:
                    for k in range(4):
                        read_out(pe, g - 4 + k)
                for kt in range(KT):
                    mm = nc.tensor.transpose(pair[g % 2][:, kt // 4, (kt % 4) * P:(kt % 4 + 1) * P],
                                             x[:, kt, tt * P:(tt + 1) * P], ident)
                mm.then_inc(own_done, 1)
                g += 1

        def store_vec(vec, ph):
            g, o = group0[ph], own0[ph]
            for tt in range(TT):
                vec.wait_ge(own_done, o + tt + 1)
                nc.vector.tensor_copy(x_tok[:, tt, :].rearrange("p (a b) -> p a b", a=2), pair[g % 2][:]).then_inc(evac[g % 2], 1)
                g += 1

        def store_sync(sp, ph):
            g = group0[ph]
            ov = out.rearrange("a (t p) d -> (a p) t d", p=P)
            for tt in range(TT):
                read_out(sp, g + tt)
                sp.dma_start(ov[:, tt, :], x_tok[:, tt, :]).then_inc(stored, 16)
            sp.wait_ge(stored, 16 * TT)

        A_ADD = {"gmlp": 8, "ffn": 16}

        def a_base(ph):
            return sum(A_ADD.get(kind, 0) for kind, _ in phases[:ph])

        def x_group(ph):
            return group0[ph] - OUT_GROUPS if phases[ph - 1][0] != "load" else group0[ph - 1]

        block = ctx.enter_context(nc.Block())

        @block.sync
        def _(sp):
            load_sync(sp, 0)
            for ph, (kind, l) in enumerate(phases):
                if kind == "ffn":
                    ffn_units(sp, ph, l)
                elif kind == "xattn":
                    xattn_units(sp, ph, l)
                elif kind == "gmlp":
                    gmlp_units(sp, ph, l, l // 3)
                elif kind == "ssd":
                    ssd_units(sp, ph)
                elif kind == "dsa":
                    dsa_units(sp, ph)
            load_unit(sp, n_units, [(stage[n_units % 2][:, 0:16], t["ffn_w_up"][0][0:P, 0:16])])
            store_sync(sp, len(phases) - 1)

        @block.tensor
        def _(pe):
            c = Counts()
            for ph, (kind, l) in enumerate(phases):
                if kind == "load":
                    load_pe(pe, ph, c)
                    if mem_ph == 0:
                        mem_pe_turn(pe, group0[ph] + 6)
                        mem_pe_sums(pe, c)
                        spread(pe, c, 2, tiles=MT)
                elif kind == "ffn":
                    ffn_pe(pe, ph, l, c, x_group(ph))
                elif kind == "xattn":
                    xattn_pe(pe, ph, l, c, x_group(ph))
                elif kind == "gmlp":
                    gmlp_pe(pe, ph, l, l // 3, c, x_group(ph))
                elif kind == "ssd":
                    ssd_pe(pe, ph, c, x_group(ph))
                elif kind == "dsa":
                    dsa_pe(pe, ph, c, x_group(ph))
                elif kind == "store":
                    store_pe(pe, ph)

        @block.scalar
        def _(act):
            c = Counts()
            for ph, (kind, l) in enumerate(phases):
                if kind == "load":
                    load_params(act)
                    if mem_ph == 0:
                        g = group0[ph] + 6
                        mem_act_squares(act, c, g)
                        mem_norm_act(act, c)
                        split_high(act, 0)
                elif kind == "ffn":
                    ffn_act(act, ph, l, c, x_group(ph))
                elif kind == "xattn":
                    xattn_act(act, ph, l, c, x_group(ph))
                elif kind == "gmlp":
                    gmlp_act(act, ph, l, l // 3, c, x_group(ph))
                elif kind == "ssd":
                    ssd_act(act, ph, c, x_group(ph))
                elif kind == "dsa":
                    dsa_act(act, ph, c, x_group(ph))

        @block.vector
        def _(vec):
            c = Counts()
            for ph, (kind, l) in enumerate(phases):
                if kind == "load":
                    load_vec(vec, ph, c)
                    if mem_ph == 0:
                        mem_vec_copy(vec, group0[ph] + 6, own0[ph] + 6)
                        mem_vec_var(vec, c)
                        mem_vec_scale(vec, c.var)
                        mem_norm_vec(vec, c, 0)
                        split_low(vec, 0)
                elif kind == "ffn":
                    ffn_vec(vec, ph, l, c, x_group(ph))
                elif kind == "xattn":
                    xattn_vec(vec, ph, l, c, x_group(ph))
                elif kind == "gmlp":
                    gmlp_vec(vec, ph, l, l // 3, c, x_group(ph))
                elif kind == "ssd":
                    ssd_vec(vec, ph, c, x_group(ph))
                elif kind == "dsa":
                    dsa_vec(vec, ph, c, x_group(ph))
                elif kind == "store":
                    store_vec(vec, ph)

        @block.gpsimd
        def _(pool):
            c = Counts()
            for ph, (kind, l) in enumerate(phases):
                if kind == "load":
                    load_pool(pool, ph, c)
                    if mem_ph == 0:
                        mem_pool(pool, c)
                elif kind == "ffn":
                    ffn_pool(pool, ph, l, c)
                elif kind == "xattn":
                    xattn_pool(pool, ph, l, c)
                elif kind == "gmlp":
                    gmlp_pool(pool, ph, l, l // 3, c)
                elif kind == "ssd":
                    ssd_pool(pool, ph, c)
                elif kind == "dsa":
                    dsa_pool(pool, ph, c)


N_PARAMS = 15
MEM_PARTS = (range(0, 2), range(2, 6), range(6, 8))
DSA_DMAS = {2: 3, 7: 4, 8: 4}


class Counts:

    def __init__(self):
        self.ad = self.sq = self.var = self.hn = self.lo = self.mn = self.ml = self.dv = 0


_INS = ["x", "mem", "positions", "norm_mix", "gm_w_in", "gm_v_norm", "gm_w_s", "gm_b_s", "gm_w_out", "ssd_w_in",
        "ssd_conv_w", "ssd_conv_b", "ssd_dt_bias", "ssd_a_log", "ssd_d", "ssd_out_norm", "ssd_w_out", "dsa_w_in",
        "dsa_q_norm", "dsa_k_norm", "dsa_kidx_norm", "dsa_w_out", "norm_xa", "norm_mem", "xa_w_q", "xa_w_kv",
        "xa_q_norm", "xa_k_norm", "xa_w_out", "norm_ffn", "ffn_w_up", "ffn_w_down"]


def all_phases():
    phases = [("load", 0)]
    for l, kind in enumerate(LAYERS):
        phases += [(kind, l), ("xattn", l), ("ffn", l)]
    return phases + [("store", 0)]


def kernel(**inputs):
    import concourse.bacc as bacc
    from concourse.bass_utils import run_bass_kernel_spmd

    nc = bacc.Bacc("TRN2", target_bir_lowering=False, num_devices=1)
    arrays, t = {}, {}
    for name, a in [(name, np.ascontiguousarray(inputs[name])) for name in _INS] + [("constants", constants())]:
        arrays[f"in_{name}"] = a
        t[name] = nc.dram_tensor(f"in_{name}", a.shape, mybir.dt.from_np(a.dtype), kind="ExternalInput").ap()
    out = nc.dram_tensor("out_0", (1, S, D), F32, kind="ExternalOutput").ap()
    build(nc, t, out, all_phases())
    return run_bass_kernel_spmd(nc, [arrays], core_ids=[0]).results[0]["out_0"]
```
